# Optimizing a Trainium2 kernel written in Bass

```python
import jax, jax.numpy as jnp
from jax import lax
import numpy as np
import math

D_MODEL = 1024
BATCH = 1
SEQ = 256
DEPTH = 2

D_MIX = D_MODEL
SB_HEAD_DIM = 64
SB_HEADS = (D_MIX // 2) // SB_HEAD_DIM
SB_WIDTH = SB_HEADS * SB_HEAD_DIM
SB_BLOCK = 128
GLA_HEADS = 4
GLA_DV = (D_MIX // 2) // GLA_HEADS
GLA_DK = GLA_DV // 2
GLA_K_WIDTH = GLA_HEADS * GLA_DK
GLA_V_WIDTH = GLA_HEADS * GLA_DV
GLA_RANK = 16
GLA_GATE_NORM = 16.0
GLA_CHUNK = 64
D_IN_PROJ = 3 * SB_WIDTH + 2 * GLA_K_WIDTH + 2 * GLA_V_WIDTH + GLA_RANK
N_GROUPS = 4
EXPERTS_PER_GROUP = 8
TOP_K_IN_GROUP = 2
D_EXPERT = 256
N_MOD = 6
EPS = 1e-6


def rms_norm(x, gain):
    xf = x.astype(jnp.float32)
    y = xf * lax.rsqrt(jnp.mean(xf * xf, axis=-1, keepdims=True) + EPS)
    return (y * gain.astype(jnp.float32)).astype(x.dtype)

def split_heads(t, n_heads):
    b, s, w = t.shape
    return t.reshape(b, s, n_heads, w // n_heads).transpose(0, 2, 1, 3)

def merge_heads(t):
    b, h, s, d = t.shape
    return t.transpose(0, 2, 1, 3).reshape(b, s, h * d)

def stick_breaking_attention(q, k, v):
    B, H, S, d = q.shape
    nb = S // SB_BLOCK
    scale = d ** -0.5
    q_blocks = jnp.moveaxis(q.reshape(B, H, nb, SB_BLOCK, d), 2, 0)
    key_pos = jnp.arange(S)

    def one_block(args):
        q_blk, blk = args
        z = jnp.einsum('bhqd,bhkd->bhqk', q_blk, k).astype(jnp.float32) * scale
        query_pos = blk * SB_BLOCK + jnp.arange(SB_BLOCK)
        before = key_pos[None, :] < query_pos[:, None]
        log_fail = jnp.where(before, -jax.nn.softplus(z), 0.0)
        suffix = lax.cumsum(log_fail, axis=3, reverse=True) - log_fail
        w = jnp.where(before, jnp.exp(jax.nn.log_sigmoid(z) + suffix), 0.0)
        return jnp.einsum('bhqk,bhkd->bhqd', w.astype(v.dtype), v)

    out = lax.map(one_block, (q_blocks, jnp.arange(nb)))
    return jnp.moveaxis(out, 0, 2).reshape(B, H, S, d)

def gla_chunked(q, k, v, log_g):
    B, H, S, dk = q.shape
    dv = v.shape[-1]
    C = GLA_CHUNK
    nc = S // C
    f32 = jnp.float32
    qc = q.astype(f32).reshape(B, H, nc, C, dk) * (dk ** -0.5)
    kc = k.astype(f32).reshape(B, H, nc, C, dk)
    vc = v.astype(f32).reshape(B, H, nc, C, dv)
    b = jnp.cumsum(log_g.astype(f32).reshape(B, H, nc, C, dk), axis=3)
    b_last = b[:, :, :, -1:, :]
    q_dec = qc * jnp.exp(b)
    k_inv = kc * jnp.exp(-b)
    causal = jnp.tril(jnp.ones((C, C), dtype=bool))
    scores = jnp.where(causal, jnp.einsum('bhnqd,bhnkd->bhnqk', q_dec, k_inv), 0.0)
    intra = jnp.einsum('bhnqk,bhnkv->bhnqv', scores, vc)
    chunk_kv = jnp.einsum('bhnkd,bhnkv->bhndv', kc * jnp.exp(b_last - b), vc)
    chunk_decay = jnp.exp(b_last[:, :, :, 0, :])

    def step(state, inp):
        dec, kv_c = inp
        return dec[..., None] * state + kv_c, state

    _, prev = lax.scan(step, jnp.zeros((B, H, dk, dv), f32),
                       (jnp.moveaxis(chunk_decay, 2, 0), jnp.moveaxis(chunk_kv, 2, 0)))
    prev = jnp.moveaxis(prev, 0, 2)
    inter = jnp.einsum('bhnqd,bhndv->bhnqv', q_dec, prev)
    return (intra + inter).reshape(B, H, S, dv).astype(v.dtype)

def hybrid_mixer(h, w_in, w_gk2, b_gk, q_gain, k_gain, gla_gain, w_out):
    proj = h @ w_in
    widths = (SB_WIDTH, SB_WIDTH, SB_WIDTH, GLA_K_WIDTH, GLA_K_WIDTH,
              GLA_V_WIDTH, GLA_V_WIDTH, GLA_RANK)
    cuts = np.cumsum(widths)[:-1].tolist()
    sb_q, sb_k, sb_v, g_q, g_k, g_v, g_r, g_lr = jnp.split(proj, cuts, axis=-1)
    qa = rms_norm(split_heads(sb_q, SB_HEADS), q_gain)
    ka = rms_norm(split_heads(sb_k, SB_HEADS), k_gain)
    out_a = merge_heads(stick_breaking_attention(qa, ka, split_heads(sb_v, SB_HEADS)))
    log_g = jax.nn.log_sigmoid((g_lr @ w_gk2 + b_gk).astype(jnp.float32)) / GLA_GATE_NORM
    o_b = gla_chunked(split_heads(g_q, GLA_HEADS), split_heads(g_k, GLA_HEADS),
                      split_heads(g_v, GLA_HEADS), split_heads(log_g, GLA_HEADS))
    out_b = merge_heads(rms_norm(o_b, gla_gain)) * jax.nn.silu(g_r)
    return jnp.concatenate([out_a, out_b], axis=-1) @ w_out

def hierarchical_moe(h, w_router_grp, b_router_grp, w_router_exp, b_router_exp,
                     w_gate, w_up, w_down):
    B, S, D = h.shape
    hf = h.reshape(B * S, D)
    f32 = jnp.float32
    grp_prob = jax.nn.softmax((hf @ w_router_grp + b_router_grp).astype(f32), axis=-1)
    grp_w, grp_idx = lax.top_k(grp_prob, 1)
    exp_logits = (hf @ w_router_exp + b_router_exp).astype(f32).reshape(-1, N_GROUPS, EXPERTS_PER_GROUP)
    sel_logits = jnp.take_along_axis(exp_logits, grp_idx[:, :, None], axis=1)[:, 0]
    top_logit, top_idx = lax.top_k(sel_logits, TOP_K_IN_GROUP)
    top_w = jax.nn.softmax(top_logit, axis=-1) * grp_w
    exp_w = jnp.sum(jax.nn.one_hot(top_idx, EXPERTS_PER_GROUP, dtype=f32) * top_w[..., None], axis=1)
    comb = (jax.nn.one_hot(grp_idx[:, 0], N_GROUPS, dtype=f32)[:, :, None]
            * exp_w[:, None, :]).astype(h.dtype)
    y = jnp.zeros_like(hf)
    for g in range(N_GROUPS):
        a = jnp.einsum('nd,edf->nef', hf, w_gate[g])
        u = jnp.einsum('nd,edf->nef', hf, w_up[g])
        y = y + jnp.einsum('nef,efd->nd', jax.nn.silu(a) * u * comb[:, g, :, None], w_down[g])
    return y.reshape(B, S, D)

def first_inputs(seed: int = 0) -> dict:
    key = jax.random.key(seed)
    ks = jax.random.split(key, 20)
    f32 = jnp.float32
    nrm = lambda k, shape, s: jax.random.normal(k, shape, f32) * s
    L, D = DEPTH, D_MODEL
    return {
        "x": nrm(ks[0], (BATCH, SEQ, D), 1.0),
        "c": nrm(ks[1], (BATCH, D), 1.0),
        "w_ada": nrm(ks[2], (L, D, N_MOD * D), 0.5 * D ** -0.5),
        "b_ada": nrm(ks[3], (L, N_MOD * D), 0.02),
        "norm_mix": 1.0 + nrm(ks[4], (L, D), 0.02),
        "norm_ffn": 1.0 + nrm(ks[5], (L, D), 0.02),
        "w_in": nrm(ks[6], (L, D, D_IN_PROJ), D ** -0.5),
        "w_gk2": nrm(ks[7], (L, GLA_RANK, GLA_K_WIDTH), GLA_RANK ** -0.5),
        "b_gk": 2.0 + nrm(ks[8], (L, GLA_K_WIDTH), 0.1),
        "q_gain": 1.0 + nrm(ks[9], (L, SB_HEAD_DIM), 0.02),
        "k_gain": 1.0 + nrm(ks[10], (L, SB_HEAD_DIM), 0.02),
        "gla_gain": 1.0 + nrm(ks[11], (L, GLA_DV), 0.02),
        "w_out": nrm(ks[12], (L, D_MIX, D), D_MIX ** -0.5),
        "w_router_grp": nrm(ks[13], (L, D, N_GROUPS), D ** -0.5),
        "b_router_grp": nrm(ks[14], (L, N_GROUPS), 0.01),
        "w_router_exp": nrm(ks[15], (L, D, N_GROUPS * EXPERTS_PER_GROUP), D ** -0.5),
        "b_router_exp": nrm(ks[16], (L, N_GROUPS * EXPERTS_PER_GROUP), 0.01),
        "w_gate": nrm(ks[17], (L, N_GROUPS, EXPERTS_PER_GROUP, D, D_EXPERT), D ** -0.5),
        "w_up": nrm(ks[18], (L, N_GROUPS, EXPERTS_PER_GROUP, D, D_EXPERT), D ** -0.5),
        "w_down": nrm(ks[19], (L, N_GROUPS, EXPERTS_PER_GROUP, D_EXPERT, D), D_EXPERT ** -0.5),
    }

def first_block(x, c, w_ada, b_ada, norm_mix, norm_ffn, w_in, w_gk2, b_gk, q_gain, k_gain,
              gla_gain, w_out, w_router_grp, b_router_grp, w_router_exp, b_router_exp,
              w_gate, w_up, w_down):
    c_act = jax.nn.silu(c)
    for l in range(DEPTH):
        mod = (c_act @ w_ada[l] + b_ada[l])[:, None, :]
        shift_m, scale_m, gate_m, shift_f, scale_f, gate_f = jnp.split(mod, N_MOD, axis=-1)
        h = rms_norm(x, norm_mix[l]) * (1.0 + scale_m) + shift_m
        x = x + gate_m * hybrid_mixer(h, w_in[l], w_gk2[l], b_gk[l], q_gain[l], k_gain[l],
                                      gla_gain[l], w_out[l])
        h = rms_norm(x, norm_ffn[l]) * (1.0 + scale_f) + shift_f
        x = x + gate_f * hierarchical_moe(h, w_router_grp[l], b_router_grp[l], w_router_exp[l],
                                          b_router_exp[l], w_gate[l], w_up[l], w_down[l])
    return x


GRID_W = 64
ROPE_THETA = 10000.0
NEG_INF = -1e30
Q_BLOCK = 128

MLA_HEADS = 4
MLA_Q_RANK = 192
MLA_KV_RANK = 128
MLA_NOPE_DIM = 64
MLA_ROPE_DIM = 32
MLA_V_DIM = 64
DIFF_HEADS = 4
DIFF_QK_DIM = 32
DIFF_V_DIM = 64
SWA_Q_HEADS = 4
SWA_KV_HEADS = 2
SWA_GROUP = SWA_Q_HEADS // SWA_KV_HEADS
SWA_HEAD_DIM = 64
WINDOW = 128
SWA_BLOCK = 128
NA_HEADS = 4
NA_HEAD_DIM = 64
NA_ROWS_MAX = 8
NA_COLS = 16
D_FF = 4 * D_MODEL

A_OUT = MLA_HEADS * MLA_V_DIM
B_OUT = DIFF_HEADS * DIFF_V_DIM
C_OUT = SWA_Q_HEADS * SWA_HEAD_DIM
D_OUT = NA_HEADS * NA_HEAD_DIM
MIX_WIDTH = A_OUT + B_OUT + C_OUT + D_OUT

IN_SPLIT_WIDTHS = (
    MLA_Q_RANK, MLA_KV_RANK, MLA_ROPE_DIM,
    DIFF_HEADS * 2 * DIFF_QK_DIM, DIFF_HEADS * 2 * DIFF_QK_DIM, B_OUT,
    SWA_Q_HEADS * SWA_HEAD_DIM, SWA_KV_HEADS * SWA_HEAD_DIM, SWA_KV_HEADS * SWA_HEAD_DIM,
    NA_HEADS * NA_HEAD_DIM, NA_HEADS * NA_HEAD_DIM, NA_HEADS * NA_HEAD_DIM,
)
IN_COLS = sum(IN_SPLIT_WIDTHS)


def _split_points():
    pts, acc = [], 0
    for w in IN_SPLIT_WIDTHS[:-1]:
        acc += w
        pts.append(acc)
    return pts

def rms_norm_2(x, g):
    xf = x.astype(jnp.float32)
    y = xf * lax.rsqrt(jnp.mean(xf * xf, axis=-1, keepdims=True) + EPS)
    return (y * g.astype(jnp.float32)).astype(x.dtype)

def rope_table(seq_len, dim):
    inv = 1.0 / (ROPE_THETA ** (jnp.arange(0, dim, 2, dtype=jnp.float32) / dim))
    ang = jnp.arange(seq_len, dtype=jnp.float32)[:, None] * inv[None, :]
    return jnp.cos(ang), jnp.sin(ang)

def apply_rope(x, cos, sin):
    shp = (1, x.shape[1]) + (1,) * (x.ndim - 3) + (cos.shape[-1],)
    c, s = cos.reshape(shp), sin.reshape(shp)
    xf = x.astype(jnp.float32)
    half = x.shape[-1] // 2
    x1, x2 = xf[..., :half], xf[..., half:]
    return jnp.concatenate([x1 * c - x2 * s, x2 * c + x1 * s], axis=-1).astype(x.dtype)

def dense_block_attention(q, k, v, scale):
    B, S, H, dq = q.shape
    nb = S // Q_BLOCK
    qb = jnp.moveaxis(q.reshape(B, nb, Q_BLOCK, H, dq), 1, 0)

    def one_block(qi):
        s = jnp.einsum('bqhd,bkhd->bhqk', qi, k, preferred_element_type=jnp.float32) * scale
        p = jax.nn.softmax(s, axis=-1)
        return jnp.einsum('bhqk,bkhd->bqhd', p.astype(v.dtype), v)

    o = lax.map(one_block, qb)
    return jnp.moveaxis(o, 0, 1).reshape(B, S, H, v.shape[-1])

def mla_mixer(cq, ckv, kr, q_norm_g, w_uq, kv_norm_g, w_uk, w_uv, cos, sin):
    B, S, _ = cq.shape
    q = (rms_norm_2(cq, q_norm_g) @ w_uq).reshape(B, S, MLA_HEADS, MLA_NOPE_DIM + MLA_ROPE_DIM)
    q = jnp.concatenate([q[..., :MLA_NOPE_DIM], apply_rope(q[..., MLA_NOPE_DIM:], cos, sin)], axis=-1)
    c = rms_norm_2(ckv, kv_norm_g)
    k_nope = (c @ w_uk).reshape(B, S, MLA_HEADS, MLA_NOPE_DIM)
    v = (c @ w_uv).reshape(B, S, MLA_HEADS, MLA_V_DIM)
    k_pe = apply_rope(kr[:, :, None, :], cos, sin)
    k = jnp.concatenate([k_nope, jnp.broadcast_to(k_pe, (B, S, MLA_HEADS, MLA_ROPE_DIM))], axis=-1)
    o = dense_block_attention(q, k, v, (MLA_NOPE_DIM + MLA_ROPE_DIM) ** -0.5)
    return o.reshape(B, S, A_OUT)

def diff_mixer(q, k, v, lq1, lk1, lq2, lk2, subln_g, lambda_init, cos, sin):
    B, S, _ = q.shape
    q = apply_rope(q.reshape(B, S, DIFF_HEADS, 2, DIFF_QK_DIM), cos, sin)
    k = apply_rope(k.reshape(B, S, DIFF_HEADS, 2, DIFF_QK_DIM), cos, sin)
    v = v.reshape(B, S, DIFF_HEADS, DIFF_V_DIM)
    f32 = jnp.float32
    lam = (jnp.exp(jnp.sum(lq1.astype(f32) * lk1.astype(f32)))
           - jnp.exp(jnp.sum(lq2.astype(f32) * lk2.astype(f32))) + lambda_init)
    scale = DIFF_QK_DIM ** -0.5
    nb = S // Q_BLOCK
    qb = jnp.moveaxis(q.reshape(B, nb, Q_BLOCK, DIFF_HEADS, 2, DIFF_QK_DIM), 1, 0)

    def one_block(qi):
        s = jnp.einsum('bqhcd,bkhcd->bhcqk', qi, k, preferred_element_type=f32) * scale
        p = jax.nn.softmax(s, axis=-1)
        w = p[:, :, 0] - lam * p[:, :, 1]
        return jnp.einsum('bhqk,bkhd->bqhd', w.astype(v.dtype), v)

    o = jnp.moveaxis(lax.map(one_block, qb), 0, 1).reshape(B, S, DIFF_HEADS, DIFF_V_DIM)
    o = rms_norm_2(o, subln_g) * (1.0 - lambda_init)
    return o.reshape(B, S, B_OUT)

def swa_mixer(q, k, v, sinks, cos, sin):
    B, S, _ = q.shape
    q = apply_rope(q.reshape(B, S, SWA_KV_HEADS, SWA_GROUP, SWA_HEAD_DIM), cos, sin)
    k = apply_rope(k.reshape(B, S, SWA_KV_HEADS, SWA_HEAD_DIM), cos, sin)
    v = v.reshape(B, S, SWA_KV_HEADS, SWA_HEAD_DIM)
    nb = S // SWA_BLOCK
    qb = q.reshape(B, nb, SWA_BLOCK, SWA_KV_HEADS, SWA_GROUP, SWA_HEAD_DIM)

    def band(t):
        tp = jnp.pad(t, ((0, 0), (SWA_BLOCK, SWA_BLOCK), (0, 0), (0, 0)))
        tp = tp.reshape(B, nb + 2, SWA_BLOCK, SWA_KV_HEADS, SWA_HEAD_DIM)
        return jnp.concatenate([tp[:, :-2], tp[:, 1:-1], tp[:, 2:]], axis=2)

    kb, vb = band(k), band(v)
    s = jnp.einsum('bnqkgd,bnjkd->bnkgqj', qb, kb,
                   preferred_element_type=jnp.float32) * (SWA_HEAD_DIM ** -0.5)
    qi = jnp.arange(SWA_BLOCK)[:, None]
    kj = jnp.arange(3 * SWA_BLOCK)[None, :]
    rel = kj - SWA_BLOCK - qi
    kabs = jnp.arange(nb)[:, None] * SWA_BLOCK - SWA_BLOCK + jnp.arange(3 * SWA_BLOCK)[None, :]
    valid = (jnp.abs(rel) <= WINDOW)[None] & ((kabs >= 0) & (kabs < S))[:, None, :]
    s = jnp.where(valid[None, :, None, None], s, NEG_INF)
    sink = jnp.broadcast_to(sinks.astype(jnp.float32).reshape(1, 1, SWA_KV_HEADS, SWA_GROUP, 1, 1),
                            s.shape[:-1] + (1,))
    p = jax.nn.softmax(jnp.concatenate([s, sink], axis=-1), axis=-1)[..., :-1]
    o = jnp.einsum('bnkgqj,bnjkd->bnqkgd', p.astype(v.dtype), vb)
    return o.reshape(B, S, C_OUT)

def na_mixer(q, k, v, rpb):
    B, S, _ = q.shape
    rows = S // GRID_W
    kh = min(NA_ROWS_MAX, rows)
    shp = (B, rows, GRID_W, NA_HEADS, NA_HEAD_DIM)
    q, k, v = q.reshape(shp), k.reshape(shp), v.reshape(shp)
    row_start = jnp.clip(jnp.arange(rows) - kh // 2, 0, rows - kh)
    col = np.arange(GRID_W)
    col_start = np.clip(col - NA_COLS // 2, 0, GRID_W - NA_COLS)
    col_idx = col_start[:, None] + np.arange(NA_COLS)[None, :]
    col_off = col_idx - col[:, None]
    rpb_cols = rpb[:, :, col_off + NA_COLS - 1]
    scale = NA_HEAD_DIM ** -0.5

    def one_row(args):
        q_r, start, r = args
        k_r = lax.dynamic_slice_in_dim(k, start, kh, axis=1)[:, :, col_idx]
        v_r = lax.dynamic_slice_in_dim(v, start, kh, axis=1)[:, :, col_idx]
        bias = jnp.take(rpb_cols, start + jnp.arange(kh) - r + NA_ROWS_MAX - 1, axis=1)
        s = jnp.einsum('bwhd,bawchd->bhwac', q_r, k_r, preferred_element_type=jnp.float32) * scale
        s = s + jnp.transpose(bias, (0, 2, 1, 3)).astype(jnp.float32)[None]
        p = jax.nn.softmax(s.reshape(B, NA_HEADS, GRID_W, kh * NA_COLS), axis=-1).reshape(s.shape)
        return jnp.einsum('bhwac,bawchd->bwhd', p.astype(v.dtype), v_r)

    o = lax.map(one_row, (jnp.moveaxis(q, 1, 0), row_start, jnp.arange(rows)))
    return jnp.moveaxis(o, 0, 1).reshape(B, S, D_OUT)

def second_inputs(seed: int = 0) -> dict:
    key = jax.random.key(seed)
    ks = jax.random.split(key, 24)
    f32 = jnp.float32
    L = DEPTH

    def nrm(k, shape, scale):
        return jax.random.normal(k, shape, f32) * scale

    def gain(k, shape):
        return 1.0 + 0.05 * jax.random.normal(k, shape, f32)

    return {
        'x': nrm(ks[0], (BATCH, SEQ, D_MODEL), 1.0),
        'norm1_g': gain(ks[1], (L, D_MODEL)),
        'w_in': nrm(ks[2], (L, D_MODEL, IN_COLS), D_MODEL ** -0.5),
        'mla_q_norm_g': gain(ks[3], (L, MLA_Q_RANK)),
        'mla_w_uq': nrm(ks[4], (L, MLA_Q_RANK, MLA_HEADS * (MLA_NOPE_DIM + MLA_ROPE_DIM)), MLA_Q_RANK ** -0.5),
        'mla_kv_norm_g': gain(ks[5], (L, MLA_KV_RANK)),
        'mla_w_uk': nrm(ks[6], (L, MLA_KV_RANK, MLA_HEADS * MLA_NOPE_DIM), MLA_KV_RANK ** -0.5),
        'mla_w_uv': nrm(ks[7], (L, MLA_KV_RANK, MLA_HEADS * MLA_V_DIM), MLA_KV_RANK ** -0.5),
        'diff_lambda_q1': nrm(ks[8], (L, DIFF_QK_DIM), 0.1),
        'diff_lambda_k1': nrm(ks[9], (L, DIFF_QK_DIM), 0.1),
        'diff_lambda_q2': nrm(ks[10], (L, DIFF_QK_DIM), 0.1),
        'diff_lambda_k2': nrm(ks[11], (L, DIFF_QK_DIM), 0.1),
        'diff_subln_g': gain(ks[12], (L, DIFF_V_DIM)),
        'swa_sinks': nrm(ks[13], (L, SWA_Q_HEADS), 0.5),
        'na_rpb': nrm(ks[14], (L, NA_HEADS, 2 * NA_ROWS_MAX - 1, 2 * NA_COLS - 1), 0.1),
        'out_g_mla': gain(ks[15], (L, A_OUT)),
        'out_g_swa': gain(ks[16], (L, C_OUT)),
        'out_g_na': gain(ks[17], (L, D_OUT)),
        'w_out': nrm(ks[18], (L, MIX_WIDTH, D_MODEL), MIX_WIDTH ** -0.5),
        'norm2_g': gain(ks[19], (L, D_MODEL)),
        'w_up': nrm(ks[20], (L, D_MODEL, D_FF), D_MODEL ** -0.5),
        'w_down': nrm(ks[21], (L, D_FF, D_MODEL), D_FF ** -0.5),
        'final_norm_g': gain(ks[22], (D_MODEL,)),
    }

def second_block(x, norm1_g, w_in, mla_q_norm_g, mla_w_uq, mla_kv_norm_g, mla_w_uk, mla_w_uv,
              diff_lambda_q1, diff_lambda_k1, diff_lambda_q2, diff_lambda_k2, diff_subln_g,
              swa_sinks, na_rpb, out_g_mla, out_g_swa, out_g_na, w_out, norm2_g, w_up, w_down,
              final_norm_g):
    S = x.shape[1]
    cos32, sin32 = rope_table(S, MLA_ROPE_DIM)
    cos64, sin64 = rope_table(S, SWA_HEAD_DIM)
    splits = _split_points()
    for l in range(DEPTH):
        h = rms_norm_2(x, norm1_g[l])
        proj = h @ w_in[l]
        (a_cq, a_ckv, a_kr, b_q, b_k, b_v, c_q, c_k, c_v, d_q, d_k, d_v) = jnp.split(proj, splits, axis=-1)
        y_a = mla_mixer(a_cq, a_ckv, a_kr, mla_q_norm_g[l], mla_w_uq[l], mla_kv_norm_g[l],
                        mla_w_uk[l], mla_w_uv[l], cos32, sin32)
        lambda_init = 0.8 - 0.6 * math.exp(-0.3 * l)
        y_b = diff_mixer(b_q, b_k, b_v, diff_lambda_q1[l], diff_lambda_k1[l], diff_lambda_q2[l],
                         diff_lambda_k2[l], diff_subln_g[l], lambda_init, cos32, sin32)
        y_c = swa_mixer(c_q, c_k, c_v, swa_sinks[l], cos64, sin64)
        y_d = na_mixer(d_q, d_k, d_v, na_rpb[l])
        mix = jnp.concatenate([rms_norm_2(y_a, out_g_mla[l]), y_b,
                               rms_norm_2(y_c, out_g_swa[l]), rms_norm_2(y_d, out_g_na[l])], axis=-1)
        x = x + mix @ w_out[l]
        h = rms_norm_2(x, norm2_g[l])
        x = x + jnp.square(jax.nn.relu(h @ w_up[l])) @ w_down[l]
    return rms_norm_2(x, final_norm_g)


def setup_inputs(seed=0):
    out = dict(first_inputs(seed))
    for name, value in second_inputs(seed + 1).items():
        if name != "x":
            out[name + "_2"] = value
    return out


def reference(
    x, c, w_ada, b_ada, norm_mix, norm_ffn, w_in, w_gk2, b_gk, q_gain, k_gain, gla_gain, w_out,
    w_router_grp, b_router_grp, w_router_exp, b_router_exp, w_gate, w_up, w_down, norm1_g_2,
    w_in_2, mla_q_norm_g_2, mla_w_uq_2, mla_kv_norm_g_2, mla_w_uk_2, mla_w_uv_2,
    diff_lambda_q1_2, diff_lambda_k1_2, diff_lambda_q2_2, diff_lambda_k2_2, diff_subln_g_2,
    swa_sinks_2, na_rpb_2, out_g_mla_2, out_g_swa_2, out_g_na_2, w_out_2, norm2_g_2, w_up_2,
    w_down_2, final_norm_g_2,
):
    x = first_block(
        x, c, w_ada, b_ada, norm_mix, norm_ffn, w_in, w_gk2, b_gk, q_gain, k_gain, gla_gain,
        w_out, w_router_grp, b_router_grp, w_router_exp, b_router_exp, w_gate, w_up, w_down,
    )
    return second_block(
        x, norm1_g_2, w_in_2, mla_q_norm_g_2, mla_w_uq_2, mla_kv_norm_g_2, mla_w_uk_2,
        mla_w_uv_2, diff_lambda_q1_2, diff_lambda_k1_2, diff_lambda_q2_2, diff_lambda_k2_2,
        diff_subln_g_2, swa_sinks_2, na_rpb_2, out_g_mla_2, out_g_swa_2, out_g_na_2, w_out_2,
        norm2_g_2, w_up_2, w_down_2, final_norm_g_2,
    )


_drawn_inputs = setup_inputs


def setup_inputs(seed=0):
    import zlib

    import numpy as np

    out = dict(_drawn_inputs(seed))
    spreads = {}
    factors = {'norm_mix': 2.989,
     'b_gk': 2.969,
     'q_gain': 8.0,
     'k_gain': 5.098,
     'gla_gain': 5.491,
     'b_router_grp': 24.198,
     'b_router_exp': 17.467,
     'mla_q_norm_g_2': 13.916,
     'diff_lambda_k1_2': 2.923,
     'diff_lambda_q2_2': 4.029,
     'diff_lambda_k2_2': 8.0,
     'diff_subln_g_2': 8.728,
     'swa_sinks_2': 8.0,
     'norm_ffn': 5.751,
     'mla_kv_norm_g_2': 3.412,
     'na_rpb_2': 4.207,
     'out_g_mla_2': 6.679,
     'out_g_swa_2': 5.666,
     'out_g_na_2': 6.193,
     'norm2_g_2': 3.384}
    for name, (base, spread) in spreads.items():
        noise = np.random.default_rng([zlib.crc32(name.encode()), seed]).standard_normal(out[name].shape)
        drawn = base * np.exp(spread * noise) if base else spread * noise
        out[name] = __import__('jax').numpy.asarray(drawn.astype(out[name].dtype))
    for name, factor in factors.items():
        out[name] = (out[name] * factor).astype(out[name].dtype)
    return out
```

```python
import math
from contextlib import ExitStack

import numpy as np
import concourse.bass as bass
from concourse import mybir

F32 = mybir.dt.float32
U32 = mybir.dt.uint32
ALU = mybir.AluOpType
ACT = mybir.ActivationFunctionType
AX = mybir.AxisListType
EPS = 1e-6
NEG = -1e30
RING = 7
CH = 2048


def layout(parts):
    at, n = {}, 0
    for name, w in parts:
        at[name] = (n, w)
        n += w
    return at, n


CONSTS = [("ident", 128), ("tri", 128), ("neg1", 128), ("mneg", 128), ("keep", 128), ("glam", 128),
          ("swa", 512), ("nam", 64), ("cos32", 32), ("sin32", 32), ("cos64", 64), ("sin64", 64),
          ("reset", 256), ("iota8", 8), ("ones", 128)]
PARAMS = [("c", 8)]
for _l in range(2):
    PARAMS += [(f"nm{_l}", 8), (f"nf{_l}", 8), (f"bgk{_l}", 2), (f"qg{_l}", 1), (f"kg{_l}", 1), (f"mg{_l}", 8),
               (f"rb{_l}", 36), (f"rw{_l}", 288), (f"gk2{_l}", 256)]
for _l in range(2):
    PARAMS += [(f"n1{_l}", 8), (f"n2{_l}", 8), (f"mq{_l}", 2), (f"mkv{_l}", 1), (f"m2g{_l}", 8), (f"sink{_l}", 4),
               (f"lam{_l}", 128)]
PARAMS += [("fin", 1024)]
C_AT, C_N = layout(CONSTS)
P_AT, P_N = layout(PARAMS)


class Eng:

    def __init__(self, sem):
        self.sem, self.n, self.items = sem, 0, []

    def op(self, fn, *waits, inc=True, chain=True):
        w = [t for t in waits if t is not None]
        if chain and self.n:
            w.append((self.sem, self.n))
        if inc:
            self.n += 1
        self.items.append((w, fn, self.sem if inc else None, 1))
        return (self.sem, self.n)

    def dma(self, fn, sem, value, *waits):
        self.items.append(([t for t in waits if t is not None], fn, sem, 16))
        return (sem, value)

    def now(self):
        return (self.sem, self.n) if self.n else None

    def replay(self, eng):
        seen = {}
        for waits, fn, sem, by in self.items:
            for t in waits:
                s, v = t() if callable(t) else t
                if seen.get(s, 0) < v:
                    eng.wait_ge(s, v)
                    seen[s] = v
            if fn is None:
                continue
            ins = fn(eng)
            if sem is not None:
                ins.then_inc(sem, by)


def program(nc, a, out, plan):
    ctx = ExitStack()
    with ctx:
        def sb(name, shape, dt=F32):
            return ctx.enter_context(nc.sbuf_tensor(name, shape, dt))

        def sem(name):
            return ctx.enter_context(nc.semaphore(name))

        ring = sb("ring", [128, RING, CH])
        x = sb("x", [128, 2, 1024])
        xn = sb("xn", [128, 2, 1024])
        hT = sb("hT", [128, 8, 256])
        cst = sb("cst", [128, C_N])
        prm = sb("prm", [128, P_N])
        gate = sb("gate", [128, 2, 1024])
        modc = sb("modc", [128, 6, 8])
        bcol = sb("bcol", [128, 48])
        aff = sb("aff", [128, 4, 8])
        st = sb("st", [128, 256])
        cact = sb("cact", [128, 24])
        ar = sb("ar", [128, 22800])
        ps = ctx.enter_context(nc.psum_tensor("ps", [128, 8, 512], F32))

        PE, DV, AC, PO, SP = (Eng(sem(f"e_{n}")) for n in ("pe", "dve", "act", "pool", "sp"))
        ENG = (PE, DV, AC, PO)

        def C(name):
            o, w = C_AT[name]
            return cst[:, o:o + w]

        def PR(name, rows=128):
            o, w = P_AT[name]
            return prm[0:rows, o:o + w]

        ident = C("ident")

        def carve(off, *dims):
            n = int(np.prod(dims))
            v = ar[:, off:off + n]
            if len(dims) == 2:
                return v.rearrange("p (a b) -> p a b", b=dims[1])
            if len(dims) == 3:
                return v.rearrange("p (a b c) -> p a b c", b=dims[1], c=dims[2])
            if len(dims) == 4:
                return v.rearrange("p (a b c d) -> p a b c d", b=dims[1], c=dims[2], d=dims[3])
            return v

        def bc(ap, axis, n):
            v = ap.unsqueeze(axis)
            shape = list(v.shape)
            shape[axis] = n
            return v.to_broadcast(shape)

        def V(name, *args, w=(), **kw):
            return DV.op(lambda e: getter(e, name)(*args, **kw), *w)

        table = {}

        def getter(e, name):
            return table[name](e)

        table.update({
            "copy": lambda e: e.tensor_copy, "tt": lambda e: e.tensor_tensor, "ts": lambda e: e.tensor_scalar,
            "stt": lambda e: e.scalar_tensor_tensor, "red": lambda e: e.tensor_reduce,
            "scan": lambda e: e.tensor_tensor_scan, "recip": lambda e: e.reciprocal, "memset": lambda e: e.memset,
            "cpred": lambda e: e.copy_predicated, "max": lambda e: e.max, "maxidx": lambda e: e.max_index,
        })

        def G(name, *args, w=(), **kw):
            return PO.op(lambda e: getter(e, name)(*args, **kw), *w)

        def A(out_, in_, func, w=(), **kw):
            return AC.op(lambda e: e.activation(out_, in_, func, **kw), *w)

        def acopy(out_, in_, w=()):
            return AC.op(lambda e: e.activation(out_, in_, ACT.Copy), *w)

        def mm(out_, pairs, w=()):
            t, n = None, len(pairs)
            for i, (l, r) in enumerate(pairs):
                t = PE.op(lambda e, l=l, r=r, i=i: e.matmul(out_, l, r, start=(i == 0), stop=(i == n - 1)),
                          *(w if i == 0 else ()), inc=(i == n - 1), chain=False)
            return t

        def mm1(out_, l, r, start, stop, w=(), inc=False):
            return PE.op(lambda e: e.matmul(out_, l, r, start=start, stop=stop, skip_group_check=True), *w,
                         inc=inc, chain=False)

        def tr(out_, in_, w=(), inc=True):
            k = in_.shape[0]
            return PE.op(lambda e: e.transpose(out_, in_, ident[0:k, 0:k]), *w, inc=inc, chain=False)

        class Banks:
            def __init__(self):
                self.at, self.freed = 0, [[] for _ in range(8)]

            def get(self, n=1, lo=0, hi=8):
                if self.at < lo or self.at + n > hi:
                    self.at = lo
                b = self.at
                self.at += n
                w = [t for i in range(b, b + n) for t in self.freed[i]]
                for i in range(b, b + n):
                    self.freed[i] = None
                return b, w

            def put(self, b, n, *tokens):
                for i in range(b, b + n):
                    self.freed[i] = [t for t in tokens if t is not None]

        pb = Banks()

        class Stream:
            def __init__(self):
                self.sems = [sem(f"w{i}") for i in range(RING)]
                self.done, self.n = [], 0

            def next(self, src, *dims, parts=128):
                n = self.n
                self.n += 1
                slot = n % RING
                size = int(np.prod(dims))
                tile = ring[0:parts, slot, 0:size]
                if len(dims) == 2:
                    tile = tile.rearrange("p (a b) -> p a b", b=dims[1])
                self.done.append(None)
                waits = [lambda: self.done[n - RING]] if n >= RING else []
                tok = SP.dma(lambda e: e.dma_start(tile, src), self.sems[slot], 16 * (n // RING + 1), *waits)
                return tile, tok, n

            def free(self, n, tok):
                self.done[n] = tok

        W = Stream()

        def barrier():
            toks = [e.now() for e in ENG]
            for e in ENG:
                e.items.append(([t for t in toks if t is not None], None, None, 0))
            pb.freed = [[] for _ in range(8)]
            pb.at = 0

        s_ld = sem("s_ld")
        n_ld = 0

        def load(dst, src):
            nonlocal n_ld
            n_ld += 16
            SP.dma(lambda e: e.dma_start(dst, src), s_ld, n_ld)

        load(cst[:, :], a["cst"])
        load(prm[:, :], a["prm"])
        load(x[:, :, :], a["x"].rearrange("b (i p) d -> p (b i) d", p=128))
        LD = (s_ld, n_ld)
        for e in ENG:
            e.items.append(([LD], None, None, 0))
        mh = st[:, 128:160]
        G("memset", mh, -0.5)

        def rstd(dst, ss, dim, w=()):
            n = dst.shape[-1]
            G("ts", dst, ss, 1.0 / dim, EPS, ALU.mult, ALU.add, w=w)
            return G("tt", dst, dst, mh[:, 0:n], ALU.pow)

        def norm_T(gain, shift=None, w=()):
            t = None
            for i in range(2):
                t = A(xn[:, i, :], x[:, i, :], ACT.Square, accum_out=st[:, i:i + 1], w=w)
            t = rstd(st[:, 2:4], st[:, 0:2], 1024, w=[t])
            for i in range(2):
                t = V("ts", xn[:, i, :], x[:, i, :], st[:, 2 + i:3 + i], None, ALU.mult, w=[t])
            return to_T(xn, hT, gain, shift, [t])

        def to_T(src, dst, gain, shift, w):
            toks = []
            for k2 in range(4):
                b, bw = pb.get()
                for kk in range(2):
                    for i in range(2):
                        t = tr(ps[:, b, kk * 256 + i * 128:kk * 256 + i * 128 + 128],
                               src[:, i, 2 * k2 + kk::8], w=[*w, *bw])
                used = []
                for kk in range(2):
                    k = 2 * k2 + kk
                    o, s = dst[:, k, :], ps[:, b, kk * 256:kk * 256 + 256]
                    if k2 % 2 == 0:
                        if shift is None:
                            used.append(V("ts", o, s, gain[:, k:k + 1], None, ALU.mult, w=[t]))
                        else:
                            used.append(V("ts", o, s, gain[:, k:k + 1], shift[:, k:k + 1], ALU.mult, ALU.add, w=[t]))
                    else:
                        used.append(A(o, s, ACT.Identity, scale=gain[:, k:k + 1],
                                      **({} if shift is None else {"bias": shift[:, k:k + 1]}), w=[t]))
                pb.put(b, 1, *used)
                toks += used
            return [toks[-1], toks[-3]]

        def rows(wap, c0, cn, k0, kn):
            return wap[:, c0:c0 + cn].rearrange("(p k) n -> p k n", k=8)[:, k0:k0 + kn, :]

        def cols(c0, wap, cn, w, sink, lhs=None):
            lhs = lhs or hT
            b, bw = pb.get(2)
            t = None
            for half in range(2):
                tile, tok, n = W.next(rows(wap, c0, cn, 4 * half, 4), 4, cn)
                for i in range(2):
                    for k in range(4):
                        t = mm1(ps[:, b + i, 0:cn], lhs[:, 4 * half + k, i * 128:(i + 1) * 128], tile[:, k, :],
                                half == 0 and k == 0, half == 1 and k == 3, w=[tok, *w, *bw], inc=(k == 3))
                W.free(n, t)
            used = [sink(i, ps[:, b + i, 0:cn], t) for i in range(2)]
            pb.put(b, 2, *used)
            return used

        def colsT(c0, wap, cn, w, lhs=None):
            lhs = lhs or hT
            nb = cn // 256
            b, bw = pb.get(nb)
            t = None
            parts = [W.next(rows(wap, c0, cn, 4 * half, 4), 4, cn) for half in range(2)]
            for m in range(cn // 128):
                for half in range(2):
                    tile, tok, n = parts[half]
                    for k in range(4):
                        t = mm1(ps[:, b + m // 2, (m % 2) * 256:(m % 2) * 256 + 256], tile[:, k, m * 128:(m + 1) * 128],
                                lhs[:, 4 * half + k, :], half == 0 and k == 0, half == 1 and k == 3,
                                w=[tok, *w, *bw], inc=(k == 3))
            for _, _, n in parts:
                W.free(n, t)
            return b, t

        cc = PR("c")
        t = A(cact[:, 0:8], cc, ACT.Exp, scale=-1.0)
        V("ts", cact[:, 8:16], cact[:, 0:8], 1.0, None, ALU.add, w=[t])
        V("recip", cact[:, 8:16], cact[:, 8:16])
        CACT = V("tt", cact[:, 16:24], cact[:, 8:16], cc, ALU.mult)
        s_mod = sem("s_mod")
        n_mod = [0]

        def ada(l):
            barrier()
            mrow = ar[0:1, 0:6144]
            brow = ar[0:1, 6144:12288]
            n_mod[0] += 16
            tb = AC.dma(lambda e: e.dma_start(brow, a["b_ada"][l:l + 1, :]), s_mod, n_mod[0])
            wv = a["w_ada"][l].rearrange("(p k) n -> p k n", k=8)
            t = None
            for j in range(3):
                b, bw = pb.get(4)
                for k in range(8):
                    tile, tok, n = W.next(wv[:, k, j * 2048:(j + 1) * 2048], 2048)
                    for q in range(4):
                        t = mm1(ps[0:1, b + q, :], cact[:, 16 + k:17 + k], tile[:, q * 512:(q + 1) * 512],
                                k == 0, k == 7, w=[tok, CACT, *bw], inc=(q == 3))
                    W.free(n, t)
                t = V("tt", mrow[:, j * 2048:(j + 1) * 2048], ps[0:1, b:b + 4, :].rearrange("p a b -> p (a b)"),
                      brow[:, j * 2048:(j + 1) * 2048], ALU.add, w=[t, tb])
                pb.put(b, 4, t)
            for s in range(6):
                n_mod[0] += 16
                td = AC.dma(lambda e, s=s: e.dma_start(
                    modc[:, s, :], mrow[:, s * 1024:(s + 1) * 1024].rearrange("o (p k) -> o p k", k=8)),
                    s_mod, n_mod[0], t)
            for g, s in ((0, 2), (1, 5)):
                for h in range(2):
                    b, bw = pb.get()
                    tm = mm(ps[:, b, :], [(C("ones")[0:1, :], mrow[:, s * 1024 + h * 512:s * 1024 + h * 512 + 512])],
                            w=[t, *bw])
                    pb.put(b, 1, acopy(gate[:, g, h * 512:(h + 1) * 512], ps[:, b, :], w=[tm]))
            V("stt", aff[:, 0, :], modc[:, 1, :], 1.0, PR(f"nm{l}"), ALU.add, ALU.mult, w=[td])
            V("copy", aff[:, 1, :], modc[:, 0, :])
            V("stt", aff[:, 2, :], modc[:, 4, :], 1.0, PR(f"nf{l}"), ALU.add, ALU.mult)
            V("copy", aff[:, 3, :], modc[:, 3, :])
            barrier()

        def residual(c, i, p, t, g=None):
            xs = x[:, i, c * 512:(c + 1) * 512]
            if g is None:
                return V("tt", xs, xs, p, ALU.add, w=[t])
            tmp = xn[:, i, c * 512:(c + 1) * 512]
            t1 = V("tt", tmp, p, gate[:, g, c * 512:(c + 1) * 512], ALU.mult, w=[t])
            V("tt", xs, xs, tmp, ALU.add)
            return t1

        def out_proj(wap, mix, gain, w, g=None):
            tt = to_T(mix, hT, gain, None, w)
            for c in range(2):
                cols(c * 512, wap, 512, tt, lambda i, p, t, c=c: residual(c, i, p, t, g))

        def mix1(l):
            barrier()
            th = norm_T(aff[:, 0, :], aff[:, 1, :])
            proj = carve(0, 2, 2560)
            gqT = carve(5120, 2, 256)
            gkT = carve(5632, 2, 256)
            mix = carve(6144, 2, 1024)
            qkT = carve(8192, 8, 256)
            win = a["w_in"][l]

            def sink(c):
                return lambda i, p, t: (acopy if i else lambda o, s, w: V("copy", o, s, w=w))(
                    proj[:, i, c * 512:(c + 1) * 512], p, w=[t])

            P = []
            for c in range(3):
                P += cols(c * 512, win, 512, th, sink(c))
            b, tm = colsT(1536, win, 512, th)
            t1 = acopy(gqT, ps[:, b, :].rearrange("p (a b) -> p a b", b=256), w=[tm])
            t2 = V("copy", gkT, ps[:, b + 1, :].rearrange("p (a b) -> p a b", b=256), w=[tm])
            pb.put(b, 2, t1, t2)
            for c in range(3, 5):
                P += cols(512 + c * 512, win, 512, th, sink(c))
            tile, tok, n = W.next(rows(win, 3072, 16, 0, 8), 8, 16)
            b, bw = pb.get()
            tm = mm(ps[0:16, b, 0:256], [(tile[:, k, :], hT[:, k, :]) for k in range(8)], w=[tok, *th, *bw])
            W.free(n, tm)
            lrT = carve(10240, 256)[0:16, :]
            t_lr = acopy(lrT, ps[0:16, b, 0:256], w=[tm])
            pb.put(b, 1, t_lr)
            sq = carve(10496, 2, 1024)
            t = V("tt", sq, proj[:, :, 0:1024], proj[:, :, 0:1024], ALU.mult, w=P)
            t = V("red", st[:, 0:32], sq.rearrange("p i (h d) -> p (i h) d", d=64), AX.X, ALU.add)
            t = rstd(st[:, 32:64], st[:, 0:32], 64, w=[t])
            for i in range(2):
                t = V("tt", xn[:, i, :].rearrange("p (h d) -> p h d", d=64),
                      proj[:, i, 0:1024].rearrange("p (h d) -> p h d", d=64),
                      bc(st[:, 32 + 16 * i:48 + 16 * i], 2, 64), ALU.mult, w=[t])
            tq = []
            for c in range(4):
                b, bw = pb.get()
                for m in range(2):
                    for i in range(2):
                        tm = tr(ps[:, b, m * 256 + i * 128:m * 256 + i * 128 + 128],
                                xn[:, i, (2 * c + m) * 128:(2 * c + m + 1) * 128], w=[t, *bw])
                o = qkT[:, 2 * c:2 * c + 2, :]
                s = ps[:, b, :].rearrange("p (a b) -> p a b", b=256)
                if c < 2:
                    tv = V("ts", o, s, PR(f"qg{l}"), 0.125, ALU.mult, ALU.mult, w=[tm])
                else:
                    tv = V("ts", o, s, PR(f"kg{l}"), None, ALU.mult, w=[tm])
                pb.put(b, 1, tv)
                tq.append(tv)
            S = 12544
            ab, ex, sp, wt = (carve(S + 1536 * q, 4, 384) for q in range(4))
            for g in range(2):
                def qh(h):
                    return slice((h % 2) * 64, (h % 2) * 64 + 64), h // 2

                def scores(b, j, h, w):
                    pr, ct = qh(h)
                    kk, qq = qkT[pr, 4 + ct, :], qkT[pr, ct, :]
                    return ((ps[:, b + j, 0:256], kk[:, 0:128], qq), (ps[:, b + j, 256:384], kk[:, 128:256], qq[:, 128:256]))

                b, bw = pb.get(4)
                for j in range(4):
                    for o, ll, rr in scores(b, j, 4 * g + j, None):
                        tm = mm(o, [(ll, rr)], w=[*tq, *bw])
                z = ps[:, b:b + 4, 0:384]
                t = A(ab, z, ACT.Abs, w=[tm])
                t = A(ex, ab, ACT.Exp, scale=-1.0, w=[t])
                t = A(ab, ex, ACT.Ln, bias=1.0)
                for j in range(4):
                    t = V("stt", sp[:, j, :], z[:, j, :], 0.0, ab[:, j, :], ALU.max, ALU.add, w=[t])
                pb.put(b, 4, t)
                for o in (0, 256):
                    t = V("tt", sp[:, :, o:o + 128], sp[:, :, o:o + 128], bc(C("keep"), 1, 4), ALU.mult)
                b, bw = pb.get(4)
                for j in range(4):
                    (o0, l0, r0), (o1, l1, r1) = scores(b, j, 4 * g + j, None)
                    mm1(o0, l0, r0, True, False, w=[t, *bw])
                    mm1(o0, C("tri"), sp[:, j, 0:256], False, False)
                    mm1(o0[:, 128:256], C("neg1"), sp[:, j, 256:384], False, False)
                    mm1(o0[:, 0:128], ident, C("mneg"), False, True)
                    mm1(o1, l1, r1, True, False)
                    mm1(o1, C("tri"), sp[:, j, 256:384], False, False)
                    tm = mm1(o1, ident, C("mneg"), False, True, inc=True)
                t = A(wt, ps[:, b:b + 4, 0:384], ACT.Exp, w=[tm])
                pb.put(b, 4, t)
                b, bw = pb.get()
                for j in range(4):
                    vc = slice(1024 + (4 * g + j) * 64, 1024 + (4 * g + j) * 64 + 64)
                    mm(ps[:, b, j * 64:j * 64 + 64], [(wt[:, j, 0:128], proj[:, 0, vc])], w=[t, *P, *bw])
                    tm = mm(ps[:, b, 256 + j * 64:256 + j * 64 + 64],
                            [(wt[:, j, 128:256], proj[:, 0, vc]), (wt[:, j, 256:384], proj[:, 1, vc])])
                t = V("copy", mix[:, :, g * 256:(g + 1) * 256], ps[:, b, :].rearrange("p (a b) -> p a b", b=256), w=[tm])
                pb.put(b, 1, t)
            barrier()
            u, lg, bb, eb, enb, ekd, qd, ki, kd = (carve(8192 + 512 * q, 512) for q in range(9))
            qde, qdo, kdt = (carve(8192 + 512 * (9 + q), 2, 256) for q in range(3))
            state = carve(14336, 2, 4, 128)
            sm = carve(15360, 8, 128)
            V("memset", qde, 0.0)
            V("memset", qdo, 0.0)
            V("memset", sm, 0.0)
            b, bw = pb.get()
            for f in range(2):
                tm = mm(ps[:, b, f * 256:f * 256 + 256], [(PR(f"gk2{l}", 16)[:, f * 128:(f + 1) * 128], lrT)], w=[t_lr, *bw])
            for f in range(2):
                t = V("ts", u[:, f * 256:f * 256 + 256], ps[:, b, f * 256:f * 256 + 256], PR(f"bgk{l}")[:, f:f + 1], None,
                      ALU.add, w=[tm])
            pb.put(b, 1, t)
            t = A(bb, u, ACT.Abs, w=[t])
            t = A(eb, bb, ACT.Exp, scale=-1.0, w=[t])
            t = A(enb, eb, ACT.Ln, bias=1.0)
            t = V("stt", lg, u, 0.0, enb, ALU.min, ALU.subtract, w=[t])
            for f in range(2):
                t = V("scan", bb[:, f * 256:f * 256 + 256], C("reset"), lg[:, f * 256:f * 256 + 256], 0.0, ALU.mult, ALU.add)
            A(eb, bb, ACT.Exp, scale=1 / 16, w=[t])
            t1 = A(enb, bb, ACT.Exp, scale=-1 / 16)
            b4 = bb.rearrange("p (c s) -> p c s", s=64)
            t = V("tt", u.rearrange("p (c s) -> p c s", s=64), b4[:, :, 63:64].to_broadcast([128, 8, 64]), b4, ALU.subtract)
            t2 = A(ekd, u, ACT.Exp, scale=1 / 16, w=[t])
            gq = gqT.rearrange("p a b -> p (a b)")
            gk = gkT.rearrange("p a b -> p (a b)")
            V("stt", qd, gq, 0.125, eb, ALU.mult, ALU.mult, w=[t1])
            V("tt", ki, gk, enb, ALU.mult)
            t = V("tt", kd, gk, ekd, ALU.mult, w=[t2])
            qd4 = qd.rearrange("p (f c e s) -> p f c e s", f=2, c=2, e=2)
            for e, dst in ((0, qde), (1, qdo)):
                tqd = V("copy", dst.rearrange("p f (c e s) -> p f c e s", c=2, e=2)[:, :, :, e, :], qd4[:, :, :, e, :])
            b, bw = pb.get()
            for i in range(2):
                for f in range(2):
                    tm = tr(ps[:, b, i * 256 + f * 128:i * 256 + f * 128 + 128],
                            kd[:, f * 256 + i * 128:f * 256 + i * 128 + 128], w=[t, *bw])
            tk = acopy(kdt, ps[:, b, :].rearrange("p (a b) -> p a b", b=256), w=[tm])
            pb.put(b, 1, tk)
            b, bw = pb.get(3)
            for c in range(3):
                pr = slice((c % 2) * 64, (c % 2) * 64 + 64)
                for f in range(2):
                    tm = mm(ps[:, b + c, f * 256:f * 256 + 256],
                            [(kdt[pr, c // 2, f * 128:(f + 1) * 128], proj[pr, c // 2, 1536 + f * 256:1536 + f * 256 + 256])],
                            w=[tk, *bw])
            for c in range(3):
                for f in range(2):
                    for hh in range(2):
                        pr = slice(hh * 64, hh * 64 + 64)
                        o = state[pr, f, c + 1, :]
                        kv = ps[pr, b + c, f * 256 + hh * 128:f * 256 + hh * 128 + 128]
                        if c == 0:
                            ts = V("copy", o, kv, w=[tm])
                        else:
                            ts = V("stt", o, state[pr, f, c, :], eb[pr, f * 256 + c * 64 + 63:f * 256 + c * 64 + 64], kv,
                                   ALU.mult, ALU.add, w=[tm])
            pb.put(b, 3, ts)
            b, bw = pb.get(2)
            for i in range(2):
                for h in range(4):
                    pr, f = slice((h % 2) * 64, (h % 2) * 64 + 64), h // 2
                    cs = slice(f * 256 + i * 128, f * 256 + i * 128 + 128)
                    tm = mm(ps[:, b + h % 2, i * 256 + f * 128:i * 256 + f * 128 + 128], [(ki[pr, cs], qd[pr, cs])], w=[tqd, *bw])
            gm = bc(C("glam"), 1, 4).bitcast(U32)
            for i in range(2):
                t = V("cpred", sm[:, 4 * i:4 * i + 4, :], gm, ps[:, b + i, :].rearrange("p (a b) -> p a b", b=128), w=[tm])
            pb.put(b, 2, t)
            b, bw = pb.get(4)
            for i in range(2):
                for h in range(4):
                    pr, f = slice((h % 2) * 64, (h % 2) * 64 + 64), h // 2
                    cs = slice(i * 128, i * 128 + 128)
                    pairs = [(sm[:, 4 * (h % 2) + 2 * i + f, :], proj[:, i, 1536 + h * 128:1536 + h * 128 + 128])]
                    if i:
                        pairs.append((qde[pr, f, cs], state[pr, f, 2, :]))
                    pairs.append((qdo[pr, f, cs], state[pr, f, 2 * i + 1, :]))
                    tm = mm(ps[:, b + 2 * i + h % 2, f * 128:f * 128 + 128], pairs, w=[t, ts, *bw])
            o = carve(16384, 2, 512)
            sg = carve(17408, 2, 512)
            s2 = carve(18432, 2, 512)
            for i in range(2):
                t = V("copy", o[:, i, :].rearrange("p (f e d) -> p e f d", f=2, e=2),
                      ps[:, b + 2 * i:b + 2 * i + 2, 0:256].rearrange("p e (f d) -> p e f d", d=128), w=[tm])
            pb.put(b, 4, t)
            V("tt", s2, o, o, ALU.mult)
            t = V("red", st[:, 0:8], s2.rearrange("p i (h d) -> p (i h) d", d=128), AX.X, ALU.add)
            t1 = rstd(st[:, 8:16], st[:, 0:8], 128, w=[t])
            t = A(sg, proj[:, :, 2048:2560], ACT.Exp, scale=-1.0)
            V("ts", sg, sg, 1.0, None, ALU.add, w=[t])
            V("recip", sg, sg)
            V("tt", sg, sg, proj[:, :, 2048:2560], ALU.mult)
            V("tt", o.rearrange("p i (h d) -> p (i h) d", d=128), o.rearrange("p i (h d) -> p (i h) d", d=128),
              bc(st[:, 8:16], 2, 128), ALU.mult, w=[t1])
            t = V("tt", mix[:, :, 512:1024], o, sg, ALU.mult)
            out_proj(a["w_out"][l], mix, PR(f"mg{l}"), [t], 0)
            barrier()

        def moe(l):
            barrier()
            th = norm_T(aff[:, 2, :], aff[:, 3, :])
            lgt = carve(0, 2, 36)
            rw = PR(f"rw{l}").rearrange("p (k n) -> p k n", k=8)
            b, bw = pb.get(2)
            for i in range(2):
                tm = mm(ps[:, b + i, 0:36], [(hT[:, k, i * 128:(i + 1) * 128], rw[:, k, :]) for k in range(8)], w=[*th, *bw])
            t = V("tt", lgt, ps[:, b:b + 2, 0:36], bc(PR(f"rb{l}"), 1, 2), ALU.add, w=[tm])
            pb.put(b, 2, t)
            comb = carve(100, 2, 32)
            oh = carve(200, 3, 8)
            g8, m8, sel, tmp, sc = (carve(300 + 40 * q, 32) for q in range(5))
            ix = sb(f"ix{l}", [128, 8], U32)
            for i in range(2):
                V("memset", g8[:, 0:8], -3e38)
                V("copy", g8[:, 0:4], lgt[:, i, 0:4])
                V("max", m8[:, 0:8], g8[:, 0:8])
                V("maxidx", ix[:, :], m8[:, 0:8], g8[:, 0:8])
                V("copy", m8[:, 8:16], ix[:, :])
                V("ts", oh[:, 0, 0:4], C("iota8")[:, 0:4], m8[:, 8:9], None, ALU.is_equal)
                t = V("ts", tmp[:, 0:4], g8[:, 0:4], m8[:, 0:1], None, ALU.subtract)
                t = A(tmp[:, 4:8], tmp[:, 0:4], ACT.Exp, accum_out=sc[:, 0:1], w=[t])
                V("recip", sc[:, 1:2], sc[:, 0:1], w=[t])
                V("tt", tmp.rearrange("p (g e) -> p g e", e=8), lgt[:, i, 4:36].rearrange("p (g e) -> p g e", e=8),
                  bc(oh[:, 0, 0:4], 2, 8), ALU.mult)
                V("red", sel[:, 0:8], tmp.rearrange("p (g e) -> p e g", e=8), AX.X, ALU.add)
                V("max", m8[:, 0:8], sel[:, 0:8])
                V("maxidx", ix[:, :], m8[:, 0:8], sel[:, 0:8])
                V("copy", m8[:, 8:16], ix[:, :])
                V("ts", oh[:, 1, :], C("iota8"), m8[:, 8:9], None, ALU.is_equal)
                V("ts", oh[:, 2, :], C("iota8"), m8[:, 9:10], None, ALU.is_equal)
                t = V("tt", sc[:, 2:3], m8[:, 1:2], m8[:, 0:1], ALU.subtract)
                t = A(sc[:, 3:4], sc[:, 2:3], ACT.Exp, w=[t])
                V("ts", sc[:, 4:5], sc[:, 3:4], 1.0, None, ALU.add, w=[t])
                V("recip", sc[:, 5:6], sc[:, 4:5])
                V("tt", sc[:, 6:7], sc[:, 5:6], sc[:, 1:2], ALU.mult)
                V("tt", sc[:, 7:8], sc[:, 6:7], sc[:, 3:4], ALU.mult)
                V("ts", sel[:, 8:16], oh[:, 1, :], sc[:, 6:7], None, ALU.mult)
                V("stt", sel[:, 16:24], oh[:, 2, :], sc[:, 7:8], sel[:, 8:16], ALU.mult, ALU.add)
                tcomb = V("tt", comb[:, i, :].rearrange("p (g e) -> p g e", e=8), bc(oh[:, 0, 0:4], 2, 8),
                          bc(sel[:, 16:24], 1, 4), ALU.mult)
            barrier()
            ex, s1, hh = (carve(600 + 1024 * q, 2, 2, 256) for q in range(3))
            aT = carve(4096, 2, 2, 2, 128)
            wg, wu, wd = (a[k][l].rearrange("g e a b -> (g e) a b") for k in ("w_gate", "w_up", "w_down"))
            gu_free = [None, None]
            tr_free = [None, None]
            h_done = [None, None]
            aT_free = [None, None]
            for e in range(32):
                tg, kg, ng = W.next(wg[e].rearrange("(p k) f -> p k f", k=8), 8, 256)
                tu, ku, nu = W.next(wu[e].rearrange("(p k) f -> p k f", k=8), 8, 256)
                td, kd, nd = W.next(wd[e].rearrange("(p k) d -> p k d", k=2), 2, 1024)
                for i in range(2):
                    for tile, tok, o in ((tg, kg, 0), (tu, ku, 256)):
                        tm = mm(ps[:, 4 + i, o:o + 256], [(hT[:, k, i * 128:(i + 1) * 128], tile[:, k, :]) for k in range(8)],
                                w=[tok, gu_free[i]])
                    av, uv = ps[:, 4 + i, 0:256], ps[:, 4 + i, 256:512]
                    e_, s_, h_ = ex[:, i, 0, :], s1[:, i, 0, :], hh[:, i, 0, :]
                    t = A(e_, av, ACT.Exp, scale=-1.0, w=[tm])
                    V("ts", e_, e_, 1.0, None, ALU.add, w=[t])
                    V("recip", e_, e_)
                    V("tt", s_, av, e_, ALU.mult)
                    h_done[i] = V("stt", h_, uv, comb[:, i, e:e + 1], s_, ALU.mult, ALU.mult, w=[tr_free[i]])
                    gu_free[i] = h_done[i]
                W.free(ng, tm)
                W.free(nu, tm)
                for i in range(2):
                    for f in range(2):
                        tt_ = tr(ps[:, 6 + i, f * 128:f * 128 + 128], hh[:, i, 0, f::2], w=[h_done[i], aT_free[i]])
                    tr_free[i] = tt_
                    ta = acopy(aT[:, i, 0, :, :], ps[:, 6 + i, 0:256].rearrange("p (a b) -> p a b", b=128), w=[tt_])
                    for c in range(2):
                        for f in range(2):
                            tm = mm1(ps[:, 2 * i + c, :], aT[:, i, 0, f, :], td[:, f, c * 512:(c + 1) * 512],
                                     e == 0 and f == 0, e == 31 and f == 1, w=[kd, ta], inc=(f == 1))
                    aT_free[i] = tm
                W.free(nd, tm)
            for i in range(2):
                for c in range(2):
                    residual(c, i, ps[:, 2 * i + c, :], tm, 1)
            barrier()

        s_na = sem("s_na")
        n_na = [0]

        def mix2(l):
            barrier()
            proj = carve(0, 2, 2400)
            q3 = carve(4800, 2, 1152)
            naT = carve(7104, 4, 6, 64)
            bias = carve(8640, 2, 4, 256)
            mix = carve(10688, 2, 1024)
            qT = carve(12736, 4, 256)
            kT = carve(13760, 4, 256)
            sc_ = carve(14784, 4, 256)
            pt = carve(15808, 4, 256)
            ptT = carve(16832, 4, 2, 128)
            cT = carve(17856, 2, 256)
            ckT = carve(18368, 256)
            rt = carve(18624, 2, 512)
            rt2 = carve(19648, 2, 512)
            sm = st
            rp = a["na_rpb"][l]
            toks = None
            for s in range(2):
                for h in range(4):
                    src = bass.AP(rp.tensor, rp.offset + 76 + 31 * s + 465 * h, [[1, 64], [31, 6], [1, 64]])
                    n_na[0] += 16
                    toks = AC.dma(lambda e, s=s, h=h, src=src: e.dma_start(naT[64 * s:64 * s + 64, h, :, :], src),
                                  s_na, n_na[0])
            th = norm_T(PR(f"n1{l}"))
            P = []
            for c in range(5):
                def sink(i, p, t, c=c):
                    o = proj[:, i, c * 480:(c + 1) * 480]
                    return acopy(o, p, w=[t]) if i else V("copy", o, p, w=[t])
                P += cols(c * 480, a["w_in_2"][l], 480, th, sink)
            for i in range(2):
                for h in range(4):
                    V("tt", bias[:, i, h, :].rearrange("p (r c) -> p r c", c=64), naT[:, 3 - h, :, :].rearrange("p r c -> p (r c)")[
                        :, 128 * i:128 * i + 256][:, ::-1].rearrange("p (r c) -> p r c", c=64),
                      bc(C("nam"), 1, 4), ALU.add, w=[toks])

            def rope(dst, src, heads, dim, w=()):
                hf = dim // 2
                t = None
                for i in range(2):
                    cs = bc(C(f"cos{dim}")[:, i * hf:(i + 1) * hf], 1, heads)
                    sn = bc(C(f"sin{dim}")[:, i * hf:(i + 1) * hf], 1, heads)
                    x1, x2 = src[:, i, :, 0:hf], src[:, i, :, hf:dim]
                    r1 = rt[:, 0, 0:heads * hf].rearrange("p (h d) -> p h d", d=hf)
                    r2 = rt2[:, 0, 0:heads * hf].rearrange("p (h d) -> p h d", d=hf)
                    r3 = rt[:, 1, 0:heads * hf].rearrange("p (h d) -> p h d", d=hf)
                    r4 = rt2[:, 1, 0:heads * hf].rearrange("p (h d) -> p h d", d=hf)
                    V("tt", r1, x1, cs, ALU.mult, w=w)
                    V("tt", r2, x2, sn, ALU.mult)
                    V("tt", r3, x2, cs, ALU.mult)
                    V("tt", r4, x1, sn, ALU.mult)
                    V("tt", dst[:, i, :, 0:hf], r1, r2, ALU.subtract)
                    t = V("tt", dst[:, i, :, hf:dim], r3, r4, ALU.add)
                return t

            def hd(ap, d):
                return ap.rearrange("p i (h d) -> p i h d", d=d)

            def transp(dst, srcs, w):
                t = None
                for m0 in range(0, len(srcs), 2):
                    b, bw = pb.get()
                    n = srcs[m0](0).shape[-1]
                    grp = srcs[m0:m0 + 2]
                    for m, s in enumerate(grp):
                        for i in range(2):
                            tm = tr(ps[0:n, b, m * 256 + i * 128:m * 256 + i * 128 + 128], s(i), w=[*w, *bw])
                    t = acopy(dst[0:n, m0:m0 + len(grp), :],
                              ps[0:n, b, 0:256 * len(grp)].rearrange("p (a b) -> p a b", b=256), w=[tm])
                    pb.put(b, 1, t)
                return t

            def attend(i, q, k, v, scale, w, bias_=None, sink_=None, apart=False):
                nb = 4 if apart else 2
                b, bw = pb.get(nb)
                for h in range(4):
                    o = ps[:, b + h, 0:256] if apart else ps[:, b + h // 2, (h % 2) * 256:(h % 2) * 256 + 256]
                    tm = mm(o, [(q(h), k(h))], w=[*w, *bw])
                s = ps[:, b:b + 4, 0:256] if apart else ps[:, b:b + 2, :].rearrange("p a (h n) -> p (a h) n", n=256)
                if bias_ is not None:
                    for hh in range(2):
                        V("stt", sc_[:, 2 * hh:2 * hh + 2, :], s[:, 2 * hh:2 * hh + 2, :], scale, bias_(hh), ALU.mult, ALU.add,
                          w=[tm])
                    s, f = sc_, 1.0
                else:
                    f = scale
                V("red", sm[:, 0:4], s, AX.X, ALU.max, w=[tm])
                if sink_ is not None:
                    V("tt", sm[:, 0:4], sm[:, 0:4], sink_, ALU.max)
                t = V("ts", sm[:, 0:4], sm[:, 0:4], -f, None, ALU.mult)
                for h in range(4):
                    t = A(pt[:, h, :], s[:, h, :], ACT.Exp, bias=sm[:, h:h + 1], scale=f, accum_out=sm[:, 4 + h:5 + h], w=[t])
                pb.put(b, nb, t)
                if sink_ is not None:
                    t = V("tt", sm[:, 8:12], sink_, sm[:, 0:4], ALU.add, w=[t])
                    t = A(sm[:, 12:16], sm[:, 8:12], ACT.Exp, w=[t])
                    t = V("tt", sm[:, 4:8], sm[:, 4:8], sm[:, 12:16], ALU.add, w=[t])
                t = V("recip", sm[:, 16:20], sm[:, 4:8], w=[t])
                return t

            def weigh(p4, n, v, w):
                t = None
                for h0 in range(0, n, 2):
                    b, bw = pb.get()
                    for h in range(h0, h0 + 2):
                        for kt in range(2):
                            tm = tr(ps[:, b, (h - h0) * 256 + kt * 128:(h - h0) * 256 + kt * 128 + 128],
                                    p4(h)[:, kt * 128:(kt + 1) * 128], w=[*w, *bw])
                    t = acopy(ptT[:, h0:h0 + 2, :, :].rearrange("p a b c -> p (a b c)"), ps[:, b, :], w=[tm])
                    pb.put(b, 1, t)
                b, bw = pb.get()
                for h in range(n):
                    tm = mm(ps[:, b, h * 64:h * 64 + 64], [(ptT[:, h, kt, :], v(kt, h)) for kt in range(2)], w=[t, *bw])
                return b, tm

            def heads_out(i, c0, b, tm):
                t = V("tt", mix[:, i, c0:c0 + 256].rearrange("p (h d) -> p h d", d=64),
                      ps[:, b, 0:256].rearrange("p (h d) -> p h d", d=64), bc(sm[:, 16:20], 2, 64), ALU.mult, w=[tm])
                pb.put(b, 1, t)
                return t

            def group_norm(c0, w):
                V("tt", rt[:, :, 0:256], mix[:, :, c0:c0 + 256], mix[:, :, c0:c0 + 256], ALU.mult, w=w)
                t = V("red", sm[:, 20:22], rt[:, :, 0:256], AX.X, ALU.add)
                t = rstd(sm[:, 22:24], sm[:, 20:22], 256, w=[t])
                return V("tt", mix[:, :, c0:c0 + 256], mix[:, :, c0:c0 + 256], bc(sm[:, 22:24], 2, 256), ALU.mult, w=[t])

            V("tt", rt[:, :, 0:320], proj[:, :, 0:320], proj[:, :, 0:320], ALU.mult, w=P)
            V("red", sm[:, 24:26], rt[:, :, 0:192], AX.X, ALU.add)
            t = V("red", sm[:, 26:28], rt[:, :, 192:320], AX.X, ALU.add)
            rstd(sm[:, 28:30], sm[:, 24:26], 192, w=[t])
            t = rstd(sm[:, 30:32], sm[:, 26:28], 128)
            V("tt", xn[:, :, 0:192], proj[:, :, 0:192], bc(sm[:, 28:30], 2, 192), ALU.mult, w=[t])
            t = V("tt", xn[:, :, 192:320], proj[:, :, 192:320], bc(sm[:, 30:32], 2, 128), ALU.mult)
            b, bw = pb.get(2)
            for i in range(2):
                for m, (o, wd_) in enumerate(((0, 128), (128, 64), (192, 128))):
                    tm = tr(ps[0:wd_, b + m // 2, (m % 2) * 256 + i * 128:(m % 2) * 256 + i * 128 + 128],
                            xn[:, i, o:o + wd_], w=[t, *bw])
            V("ts", cT[:, 0, :], ps[:, b, 0:256], PR(f"mq{l}")[:, 0:1], None, ALU.mult, w=[tm])
            V("ts", cT[0:64, 1, :], ps[0:64, b, 256:512], PR(f"mq{l}", 64)[:, 1:2], None, ALU.mult)
            t = V("ts", ckT, ps[:, b + 1, 0:256], PR(f"mkv{l}"), None, ALU.mult)
            pb.put(b, 2, t)
            w0, k0, n0 = W.next(a["mla_w_uq_2"][l][0:128, :], 384)
            w1, k1, n1 = W.next(a["mla_w_uq_2"][l][128:192, :], 384, parts=64)
            w2, k2, n2 = W.next(a["mla_w_uk_2"][l], 256)
            w3, k3, n3 = W.next(a["mla_w_uv_2"][l], 256)
            for i in range(2):
                ts_ = slice(i * 128, i * 128 + 128)
                b, bw = pb.get(2)
                mm(ps[:, b, 0:384], [(cT[:, 0, ts_], w0), (cT[0:64, 1, ts_], w1)], w=[t, k0, k1, *bw])
                mm(ps[:, b + 1, 0:256], [(ckT[:, ts_], w2)], w=[k2])
                tm = mm(ps[:, b + 1, 256:512], [(ckT[:, ts_], w3)], w=[k3])
                V("copy", q3[:, i, 0:384], ps[:, b, 0:384], w=[tm])
                tv = acopy(q3[:, i, 384:640], ps[:, b + 1, 256:512], w=[tm])
                t1 = V("copy", q3[:, i, 640:1024].rearrange("p (h d) -> p h d", d=96)[:, :, 0:64],
                       ps[:, b + 1, 0:256].rearrange("p (h d) -> p h d", d=64), w=[tv])
                pb.put(b, 2, tv, t1)
            for n in (n0, n1, n2, n3):
                W.free(n, tm)
            qv = q3[:, :, 0:384].rearrange("p i (h d) -> p i h d", d=96)
            kv = q3[:, :, 640:1024].rearrange("p i (h d) -> p i h d", d=96)
            rope(qv[:, :, :, 64:96], qv[:, :, :, 64:96], 4, 32)
            rope(hd(xn[:, :, 320:352], 32), hd(proj[:, :, 320:352], 32), 1, 32)
            for h in range(4):
                t = V("copy", kv[:, :, h, 64:96], xn[:, :, 320:352])
            t1 = transp(qT, [lambda i, h=h: q3[:, i, h * 96:h * 96 + 96] for h in range(4)], [t])
            t2 = transp(kT, [lambda i, h=h: q3[:, i, 640 + h * 96:736 + h * 96] for h in range(4)], [t])
            for i in range(2):
                ts_ = slice(i * 128, i * 128 + 128)
                t = attend(i, lambda h: qT[0:96, h, ts_], lambda h: kT[0:96, h, :], None, 96 ** -0.5, [t1, t2])
                b, tm = weigh(lambda h: pt[:, h, :], 4, lambda kt, h: q3[:, kt, 384 + h * 64:448 + h * 64], [t, tv])
                t = heads_out(i, 0, b, tm)
            group_norm(0, [t])
            lv = PR(f"lam{l}")
            V("tt", rt[:, 0, 0:32], lv[:, 0:32], lv[:, 32:64], ALU.mult)
            V("tt", rt[:, 0, 32:64], lv[:, 64:96], lv[:, 96:128], ALU.mult)
            t = V("red", sm[:, 32:34], rt[:, 0, 0:64].rearrange("p (a b) -> p a b", b=32), AX.X, ALU.add)
            t = A(sm[:, 34:36], sm[:, 32:34], ACT.Exp, w=[t])
            li = 0.8 - 0.6 * math.exp(-0.3 * l)
            V("tt", sm[:, 36:37], sm[:, 35:36], sm[:, 34:35], ALU.subtract, w=[t])
            V("ts", sm[:, 37:38], sm[:, 36:37], -li, None, ALU.add)
            t = rope(hd(xn[:, :, 0:512], 32), hd(proj[:, :, 352:864], 32), 16, 32)
            t1 = transp(qT, [lambda i, m=m: xn[:, i, m * 128:(m + 1) * 128] for m in range(2)], [t])
            t2 = transp(kT, [lambda i, m=m: xn[:, i, 256 + m * 128:256 + (m + 1) * 128] for m in range(2)], [t])
            for i in range(2):
                ts_ = slice(i * 128, i * 128 + 128)
                for m in range(2):
                    def qs(h):
                        return slice(32 * h, 32 * h + 32)
                    t = attend(i, lambda h: qT[qs(h), m, ts_], lambda h: kT[qs(h), m, :], None, 32 ** -0.5, [t1, t2], apart=True)
                    s4 = sm[:, 16:20].rearrange("p (h c) -> p h c", c=2)
                    t = V("ts", s4[:, :, 1], s4[:, :, 1], sm[:, 37:38], None, ALU.mult)
                    for h in range(2):
                        V("ts", sc_[:, h, :], pt[:, 2 * h + 1, :], sm[:, 17 + 2 * h:18 + 2 * h], None, ALU.mult)
                        t = V("stt", sc_[:, 2 + h, :], pt[:, 2 * h, :], sm[:, 16 + 2 * h:17 + 2 * h], sc_[:, h, :],
                              ALU.mult, ALU.add)
                    b, tm = weigh(lambda h: sc_[:, 2 + h, :], 2,
                                  lambda kt, h: proj[:, kt, 864 + (2 * m + h) * 64:928 + (2 * m + h) * 64], [t])
                    t = V("copy", mix[:, i, 256 + m * 128:384 + m * 128], ps[:, b, 0:128], w=[tm])
                    pb.put(b, 1, t)
            V("tt", rt[:, :, 0:256], mix[:, :, 256:512], mix[:, :, 256:512], ALU.mult)
            t = V("red", sm[:, 40:48], rt[:, :, 0:256].rearrange("p i (h d) -> p i h d", d=64), AX.X, ALU.add)
            t = rstd(sm[:, 48:56], sm[:, 40:48], 64, w=[t])
            V("ts", sm[:, 48:56], sm[:, 48:56], 1.0 - li, None, ALU.mult, w=[t])
            for i in range(2):
                mv = mix[:, i, 256:512].rearrange("p (h d) -> p h d", d=64)
                t = V("tt", mv, mv, bc(sm[:, 48 + 4 * i:52 + 4 * i], 2, 64), ALU.mult)
            t = rope(hd(xn[:, :, 0:384], 64), hd(proj[:, :, 1120:1504], 64), 6, 64)
            t1 = transp(qT, [lambda i, m=m: xn[:, i, m * 64:(m + 1) * 64] for m in range(4)], [t])
            t2 = transp(kT, [lambda i, m=m: xn[:, i, 256 + m * 64:256 + (m + 1) * 64] for m in range(2)], [t])
            swm = C("swa").rearrange("p (i n) -> p i n", i=2)
            for i in range(2):
                ts_ = slice(i * 128, i * 128 + 128)
                t = attend(i, lambda h: qT[0:64, h, ts_], lambda h: kT[0:64, h // 2, :], None, 0.125, [t1, t2],
                           bias_=lambda hh: bc(swm[:, i, :], 1, 2), sink_=PR(f"sink{l}"))
                b, tm = weigh(lambda h: pt[:, h, :], 4, lambda kt, h: proj[:, kt, 1504 + (h // 2) * 64:1568 + (h // 2) * 64], [t])
                t = heads_out(i, 512, b, tm)
            group_norm(512, [t])
            t1 = transp(qT, [lambda i, m=m: proj[:, i, 1632 + m * 64:1696 + m * 64] for m in range(4)], P)
            t2 = transp(kT, [lambda i, m=m: proj[:, i, 1888 + m * 64:1952 + m * 64] for m in range(4)], P)
            for i in range(2):
                ts_ = slice(i * 128, i * 128 + 128)
                t = attend(i, lambda h: qT[0:64, h, ts_], lambda h: kT[0:64, h, :], None, 0.125, [t1, t2],
                           bias_=lambda hh: bias[:, i, 2 * hh:2 * hh + 2, :])
                b, tm = weigh(lambda h: pt[:, h, :], 4, lambda kt, h: proj[:, kt, 2144 + h * 64:2208 + h * 64], [t])
                t = heads_out(i, 768, b, tm)
            t = group_norm(768, [t])
            out_proj(a["w_out_2"][l], mix, PR(f"m2g{l}"), [t])
            barrier()

        def mlp(l):
            barrier()
            th = norm_T(PR(f"n2{l}"))
            uT = carve(0, 32, 256)
            for c in range(8):
                b, tm = colsT(c * 512, a["w_up_2"][l], 512, th)
                for m in range(2):
                    o = uT[:, c * 4 + 2 * m:c * 4 + 2 * m + 2, :]
                    s = ps[:, b + m, :].rearrange("p (a b) -> p a b", b=256)
                    A(o, s, ACT.Relu, w=[tm])
                    t = A(o, o, ACT.Square)
                pb.put(b, 2, t)
            b, bw = pb.get(4)
            wd = a["w_down_2"][l].rearrange("(f p) d -> p f d", p=128)
            for f2 in range(16):
                tile, tok, n = W.next(wd[:, 2 * f2:2 * f2 + 2, :], 2, 1024)
                for i in range(2):
                    for c in range(2):
                        for f in range(2):
                            tm = mm1(ps[:, b + 2 * i + c, :], uT[:, 2 * f2 + f, i * 128:(i + 1) * 128],
                                     tile[:, f, c * 512:(c + 1) * 512], f2 == 0 and f == 0, f2 == 15 and f == 1,
                                     w=[tok, t, *bw], inc=(f == 1))
                W.free(n, tm)
            for i in range(2):
                for c in range(2):
                    t = residual(c, i, ps[:, b + 2 * i + c, :], tm)
            pb.put(b, 4, t)
            barrier()

        s_out = sem("s_out")

        def final(normed):
            barrier()
            t = DV.now()
            if normed:
                for i in range(2):
                    t = A(xn[:, i, :], x[:, i, :], ACT.Square, accum_out=st[:, i:i + 1], w=[t])
                t = rstd(st[:, 2:4], st[:, 0:2], 1024, w=[t])
                for i in range(2):
                    t = V("stt", xn[:, i, :], x[:, i, :], st[:, 2 + i:3 + i], PR("fin"), ALU.mult, ALU.mult, w=[t])
            src = xn if normed else x
            tok = SP.dma(lambda e: e.dma_start(out.rearrange("b (i p) d -> p (b i) d", p=128), src[:, :, :]), s_out, 16, t)
            SP.items.append(([tok], None, None, 0))

        for what, l in plan:
            if what == "mix1":
                ada(l)
                mix1(l)
            elif what == "moe":
                moe(l)
            elif what == "mix2":
                mix2(l)
            elif what == "mlp":
                mlp(l)
        final(plan[-1][0] == "final")

        block = ctx.enter_context(nc.Block())

        @block.sync
        def _(eng):
            SP.replay(eng)

        @block.tensor
        def _(eng):
            PE.replay(eng)

        @block.vector
        def _(eng):
            DV.replay(eng)

        @block.scalar
        def _(eng):
            AC.replay(eng)

        @block.gpsimd
        def _(eng):
            PO.replay(eng)


def constants():
    c = {}
    p = np.arange(128)
    f = np.arange(128)
    c["ident"] = np.eye(128)
    c["tri"] = -(p[:, None] >= f[None, :]).astype(np.float32)
    c["neg1"] = -np.ones((128, 128))
    c["mneg"] = np.where(p[:, None] >= f[None, :], NEG, 0.0)
    c["keep"] = (p[:, None] < f[None, :])
    c["glam"] = (p[:, None] <= f[None, :]) & (p[:, None] // 64 == f[None, :] // 64)
    t = np.arange(256)
    c["swa"] = np.concatenate([np.where(np.abs(t[None, :] - (i * 128 + p[:, None])) <= 128, 0.0, NEG) for i in range(2)], 1)
    qc, kc = (p % 64)[:, None], np.arange(64)[None, :]
    lo = np.clip(qc - 8, 0, 48)
    c["nam"] = np.where((kc >= lo) & (kc < lo + 16), 0.0, NEG)
    for dim in (32, 64):
        inv = (1.0 / (np.float32(10000.0) ** (np.arange(0, dim, 2, dtype=np.float32) / np.float32(dim)))).astype(np.float32)
        ang = (t.astype(np.float32)[:, None] * inv[None, :]).astype(np.float32)
        for n, fn in (("cos", np.cos), ("sin", np.sin)):
            v = fn(ang).astype(np.float32)
            c[f"{n}{dim}"] = np.concatenate([v[0:128], v[128:256]], 1)
    c["reset"] = np.broadcast_to((t % 64 != 0), (128, 256))
    c["iota8"] = np.broadcast_to(np.arange(8), (128, 8))
    c["ones"] = np.ones((128, 128))
    return np.concatenate([np.asarray(c[n], np.float32) for n, _ in CONSTS], 1)


def params(a):
    z = {}

    def pk(v):
        return v.reshape(128, 8)

    def row(v, n=128):
        return np.broadcast_to(v.reshape(1, -1), (n, v.size))

    z["c"] = pk(a["c"][0])
    one = np.ones(512, np.float32)
    pad = np.zeros(64, np.float32)
    for l in range(2):
        z[f"nm{l}"], z[f"nf{l}"] = pk(a["norm_mix"][l]), pk(a["norm_ffn"][l])
        z[f"bgk{l}"] = a["b_gk"][l].reshape(2, 128).T
        z[f"qg{l}"] = np.tile(a["q_gain"][l], 2).reshape(128, 1)
        z[f"kg{l}"] = np.tile(a["k_gain"][l], 2).reshape(128, 1)
        z[f"mg{l}"] = pk(np.concatenate([one, np.tile(a["gla_gain"][l], 4)]))
        z[f"rb{l}"] = row(np.concatenate([a["b_router_grp"][l], a["b_router_exp"][l]]))
        z[f"rw{l}"] = np.concatenate([a["w_router_grp"][l], a["w_router_exp"][l]], 1).reshape(128, 288)
        z[f"gk2{l}"] = np.concatenate([a["w_gk2"][l], np.zeros((112, 256), np.float32)], 0)
        z[f"n1{l}"], z[f"n2{l}"] = pk(a["norm1_g_2"][l]), pk(a["norm2_g_2"][l])
        z[f"mq{l}"] = np.concatenate([a["mla_q_norm_g_2"][l], pad]).reshape(2, 128).T
        z[f"mkv{l}"] = a["mla_kv_norm_g_2"][l].reshape(128, 1)
        z[f"m2g{l}"] = pk(np.concatenate([a["out_g_mla_2"][l], np.tile(a["diff_subln_g_2"][l], 4), a["out_g_swa_2"][l],
                                          a["out_g_na_2"][l]]))
        z[f"sink{l}"] = row(a["swa_sinks_2"][l])
        z[f"lam{l}"] = row(np.concatenate([a[f"diff_lambda_{n}_2"][l] for n in ("q1", "k1", "q2", "k2")]))
    z["fin"] = row(a["final_norm_g_2"])
    return np.ascontiguousarray(np.concatenate([z[n] for n, _ in PARAMS], 1))


PLAN = [("mix1", 0), ("moe", 0), ("mix1", 1), ("moe", 1), ("mix2", 0), ("mlp", 0), ("mix2", 1), ("mlp", 1), ("final", 0)]
_INS = ["x", "b_ada", "w_ada", "w_in", "w_out", "w_gate", "w_up", "w_down", "w_in_2", "mla_w_uq_2", "mla_w_uk_2",
        "mla_w_uv_2", "na_rpb_2", "w_out_2", "w_up_2", "w_down_2"]


def kernel(**inputs):
    import numpy as _np
    import concourse.bacc as _bacc
    from concourse import mybir as _mybir
    from concourse.bass_utils import run_bass_kernel_spmd as _run

    nc = _bacc.Bacc("TRN2", target_bir_lowering=False, num_devices=1)
    host = {n: _np.ascontiguousarray(inputs[n]) for n in _INS}
    host["na_rpb_2"] = _np.ascontiguousarray(host["na_rpb_2"][:, ::-1, ::-1, ::-1])
    host["cst"] = constants()
    host["prm"] = params({n: _np.asarray(v) for n, v in inputs.items()})
    arrays, aps = {}, {}
    for name, v in host.items():
        arrays[f"in_{name}"] = v
        aps[name] = nc.dram_tensor(f"in_{name}", v.shape, _mybir.dt.from_np(v.dtype), kind="ExternalInput").ap()
    aps["na_rpb"] = aps["na_rpb_2"]
    out = nc.dram_tensor("out_0", (1, 256, 1024), F32, kind="ExternalOutput").ap()
    program(nc, aps, out, PLAN)
    r = _run(nc, [arrays], core_ids=[0])
    return r.results[0]["out_0"]
```

```python
import math
from contextlib import ExitStack

import numpy as np
import concourse.bass as bass
from concourse import mybir

F32 = mybir.dt.float32
F32R = mybir.dt.float32r
U32 = mybir.dt.uint32
ALU = mybir.AluOpType
ACT = mybir.ActivationFunctionType
AX = mybir.AxisListType
EPS = 1e-6
NEG = -1e30
RING = 4
SPLIT = 3
CH = 2048


def layout(parts):
    at, n = {}, 0
    for name, w in parts:
        at[name] = (n, w)
        n += w
    return at, n


CONSTS = [("ident", 128), ("tri", 128), ("neg1", 128), ("mneg", 128), ("keep", 128), ("glam", 128),
          ("swa", 512), ("nam", 64), ("cos32", 32), ("sin32", 32), ("cos64", 64), ("sin64", 64),
          ("reset", 256), ("iota8", 8), ("ones", 128), ("stri", 128), ("slot", 128)]
PARAMS = [("c", 8)]
for _l in range(2):
    PARAMS += [(f"nm{_l}", 8), (f"nf{_l}", 8), (f"bgk{_l}", 2), (f"qg{_l}", 1), (f"kg{_l}", 1), (f"mg{_l}", 8),
               (f"rb{_l}", 36), (f"rw{_l}", 288), (f"gk2{_l}", 256)]
for _l in range(2):
    PARAMS += [(f"n1{_l}", 8), (f"n2{_l}", 8), (f"mq{_l}", 2), (f"mkv{_l}", 1), (f"m2g{_l}", 8), (f"sink{_l}", 4),
               (f"lam{_l}", 128)]
C_AT, C_N = layout(CONSTS)
P_AT, P_N = layout(PARAMS)


class Eng:

    def __init__(self, sem):
        self.sem, self.n, self.items = sem, 0, []

    def op(self, fn, *waits, inc=True, chain=True):
        w = [t for t in waits if t is not None]
        if chain and self.n:
            w.append((self.sem, self.n))
        if inc:
            self.n += 1
        self.items.append((w, fn, self.sem if inc else None, 1))
        return (self.sem, self.n)

    def dma(self, fn, sem, value, *waits):
        self.items.append(([t for t in waits if t is not None], fn, sem, 16))
        return (sem, value)

    def begin(self, sem):
        self.outer = (self.items, self.n, self.sem)
        self.items, self.n, self.sem = [], 0, sem

    def end(self, flag, wait, at=None):
        body = self.items
        self.items, self.n, self.sem = self.outer
        item = ("if", flag, wait, body)
        if at is None:
            self.items.append(item)
        else:
            self.items[at] = item

    def now(self):
        return (self.sem, self.n) if self.n else None

    def replay(self, eng, items=None):
        seen = {}
        for waits, fn, sem, by in self.items if items is None else items:
            if waits == "if":
                flag, wait, body = fn, sem, by
                eng.wait_ge(*wait)
                seen[wait[0]] = max(seen.get(wait[0], 0), wait[1])
                with eng.If(eng.value_load(flag, min_val=0, max_val=1) > 0):
                    self.replay(eng, body)
                continue
            for t in waits:
                s, v = t() if callable(t) else t
                if seen.get(s, 0) < v:
                    eng.wait_ge(s, v)
                    seen[s] = v
            if fn is None:
                continue
            ins = fn(eng)
            if sem is not None:
                ins.then_inc(sem, by)


def program(nc, a, out, plan):
    ctx = ExitStack()
    with ctx:
        base = (nc.sbuf_base + 63) // 64 * 64
        top = [base]
        ctx.enter_context(nc.sbuf_tensor("fence", [128, (nc.sbuf_usable_end - base) // 4 - 32], F32))

        def sb(name, shape, dt=F32, at=None):
            if at is None:
                at = top[0]
                top[0] += (int(np.prod(shape[1:])) * 4 + 31) // 32 * 32
                assert top[0] <= nc.sbuf_usable_end
            return nc.alloc_sbuf_tensor_at(name, shape, dt, offset=at)

        def sem(name):
            return ctx.enter_context(nc.semaphore(name))

        ring = sb("ring", [128, RING, CH])
        x = sb("x", [128, 2, 1024])
        xn = sb("xn", [128, 2, 1024])
        hh = sb("hh", [128, 2, 2048], F32R)
        spl = sb("spl", [128, SPLIT, 2, CH], F32R)
        cst = sb("cst", [128, C_N])
        prm = sb("prm", [128, P_N])
        gate = sb("gate", [128, 2, 1024])
        modc = sb("modc", [128, 6, 8])
        bcol = sb("bcol", [128, 48])
        aff = sb("aff", [128, 4, 8])
        st = sb("st", [128, 256])
        cact = sb("cact", [128, 24])
        ixt = sb("ixt", [128, 2, 8], U32)
        flags = sb("flags", [128, 2, 2], mybir.dt.int32)
        U_N = 9216
        A_N = (nc.sbuf_usable_end - top[0]) // 128 * 32
        ur = sb("ur", [128, U_N], F32R, at=top[0])
        ar = sb("ar", [128, A_N], F32, at=top[0])
        hT = tuple(hh[:, q, :].rearrange("p (k n) -> p k n", k=8) for q in range(2))
        ps = ctx.enter_context(nc.psum_tensor("ps", [128, 8, 512], F32))

        PE, DV, AC, PO, SP = (Eng(sem(f"e_{n}")) for n in ("pe", "dve", "act", "pool", "sp"))
        ENG = (PE, DV, AC, PO)

        def C(name):
            o, w = C_AT[name]
            return cst[:, o:o + w]

        def PR(name, rows=128):
            o, w = P_AT[name]
            return prm[0:rows, o:o + w]

        ident = C("ident")

        def carve(off, *dims):
            n = int(np.prod(dims))
            assert off + n <= A_N, (off, n, A_N)
            v = ar[:, off:off + n]
            if len(dims) == 2:
                return v.rearrange("p (a b) -> p a b", b=dims[1])
            if len(dims) == 3:
                return v.rearrange("p (a b c) -> p a b c", b=dims[1], c=dims[2])
            if len(dims) == 4:
                return v.rearrange("p (a b c d) -> p a b c d", b=dims[1], c=dims[2], d=dims[3])
            return v

        def bc(ap, axis, n):
            v = ap.unsqueeze(axis)
            shape = list(v.shape)
            shape[axis] = n
            return v.to_broadcast(shape)

        def V(name, *args, w=(), **kw):
            return DV.op(lambda e: getter(e, name)(*args, **kw), *w)

        table = {}

        def getter(e, name):
            return table[name](e)

        table.update({
            "copy": lambda e: e.tensor_copy, "tt": lambda e: e.tensor_tensor, "ts": lambda e: e.tensor_scalar,
            "stt": lambda e: e.scalar_tensor_tensor, "red": lambda e: e.tensor_reduce,
            "scan": lambda e: e.tensor_tensor_scan, "recip": lambda e: e.reciprocal, "memset": lambda e: e.memset,
            "cpred": lambda e: e.copy_predicated, "max": lambda e: e.max, "maxidx": lambda e: e.max_index,
        })

        def G(name, *args, w=(), **kw):
            return PO.op(lambda e: getter(e, name)(*args, **kw), *w)

        def A(out_, in_, func, w=(), **kw):
            return AC.op(lambda e: e.activation(out_, in_, func, **kw), *w)

        def acopy(out_, in_, w=()):
            return AC.op(lambda e: e.activation(out_, in_, ACT.Copy), *w)

        def mm(out_, pairs, w=()):
            t, n = None, len(pairs)
            for i, (l, r) in enumerate(pairs):
                t = PE.op(lambda e, l=l, r=r, i=i: e.matmul(out_, l, r, start=(i == 0), stop=(i == n - 1)),
                          *(w if i == 0 else ()), inc=(i == n - 1), chain=False)
            return t

        def mm1(out_, l, r, start, stop, w=(), inc=False):
            return PE.op(lambda e: e.matmul(out_, l, r, start=start, stop=stop, skip_group_check=True), *w,
                         inc=inc, chain=False)

        def parts3(l, r):
            return [(l[0], r[0]), (l[0], r[1]), (l[1], r[0])]

        def tr(out_, in_, w=(), inc=True):
            k = in_.shape[0]
            return PE.op(lambda e: e.transpose(out_, in_, ident[0:k, 0:k]), *w, inc=inc, chain=False)

        class Banks:
            def __init__(self):
                self.at, self.freed = 0, [[] for _ in range(8)]

            def get(self, n=1, lo=0, hi=8):
                if self.at < lo or self.at + n > hi:
                    self.at = lo
                b = self.at
                self.at += n
                w = [t for i in range(b, b + n) for t in self.freed[i]]
                for i in range(b, b + n):
                    self.freed[i] = None
                return b, w

            def put(self, b, n, *tokens):
                for i in range(b, b + n):
                    self.freed[i] = [t for t in tokens if t is not None]

        pb = Banks()

        class Stream:
            def __init__(self):
                self.sems = [sem(f"w{i}") for i in range(RING)]
                self.plan, self.raw_free, self.toks, self.tiles = [], [], [], []
                self.at = self.ready = 0
                self.spl_free, self.n_spl, self.spl_of = [()] * SPLIT, 0, {}

            def add(self, src, *dims, parts=128, split=True):
                n, slot = len(self.plan), len(self.plan) % RING
                size = int(np.prod(dims))
                tile = ring[0:parts, slot, 0:size]
                self.plan.append((tile, dims, split, parts, size))
                self.raw_free.append(None)
                v = tile.rearrange("p (a b) -> p a b", b=dims[1]) if len(dims) == 2 else tile
                waits = [lambda: self.raw_free[n - RING]] if n >= RING else []
                self.toks.append(SP.dma(lambda e: e.dma_start(v, src), self.sems[slot], 16 * (n // RING + 1), *waits))

            def prepare(self):
                while self.ready < len(self.plan) and self.ready < self.at + SPLIT:
                    n = self.ready
                    tile, dims, split, parts, size = self.plan[n]

                    def shaped(v):
                        return v.rearrange("p (a b) -> p a b", b=dims[1]) if len(dims) == 2 else v

                    if split:
                        s = self.n_spl % SPLIT
                        if self.spl_free[s] is None:
                            return
                        self.n_spl += 1
                        self.spl_of[n] = s
                        hi, lo = spl[0:parts, s, 0, 0:size], spl[0:parts, s, 1, 0:size]
                        t = AC.op(lambda e, hi=hi, tile=tile: e.activation(hi, tile, ACT.Copy), self.toks[n], *self.spl_free[s], chain=False)
                        t = DV.op(lambda e, hi=hi, lo=lo, tile=tile: e.tensor_tensor(lo, tile, hi, ALU.subtract), t, chain=False)
                        self.spl_free[s] = None
                        self.raw_free[n] = t
                        self.tiles.append(((shaped(hi), shaped(lo)), t))
                    else:
                        self.tiles.append((shaped(tile), self.toks[n]))
                    self.ready += 1

            def next(self):
                n = self.at
                self.at += 1
                self.prepare()
                return (*self.tiles[n], n)

            def free(self, n, tok):
                if n in self.spl_of:
                    self.spl_free[self.spl_of[n]] = (tok,)
                else:
                    self.raw_free[n] = tok
                self.prepare()

        W = Stream()

        def barrier():
            toks = [e.now() for e in ENG]
            for e in ENG:
                e.items.append(([t for t in toks if t is not None], None, None, 0))
            pb.freed = [[] for _ in range(8)]
            pb.at = 0

        s_ld = sem("s_ld")
        n_ld = 0

        def load(dst, src, *waits):
            nonlocal n_ld
            n_ld += 16
            SP.dma(lambda e: e.dma_start(dst, src), s_ld, n_ld, *waits)

        load(cst[:, :], a["cst"])
        load(prm[:, :], a["prm"])
        load(x[:, :, :], a["x"].rearrange("b (i p) d -> p (b i) d", p=128))
        LD = (s_ld, n_ld)
        for e in ENG:
            e.items.append(([LD], None, None, 0))
        mh = st[:, 128:160]
        G("memset", mh, -0.5)

        def rstd(dst, ss, dim, w=()):
            n = dst.shape[-1]
            G("ts", dst, ss, 1.0 / dim, EPS, ALU.mult, ALU.add, w=w)
            return G("tt", dst, dst, mh[:, 0:n], ALU.pow)

        def norm(w=()):
            t = None
            for i in range(2):
                t = A(xn[:, i, :], x[:, i, :], ACT.Square, accum_out=st[:, i:i + 1], w=w)
            t = rstd(st[:, 2:4], st[:, 0:2], 1024, w=[t])
            for i in range(2):
                t = V("ts", xn[:, i, :], x[:, i, :], st[:, 2 + i:3 + i], None, ALU.mult, w=[t])
            return t

        def norm_T(stage, gain, shift=None):
            return to_T(xn, stage, gain, shift, [norm()])

        def split2(hi, lo, src, w):
            t = acopy(hi, src, w=w)
            return V("tt", lo, src, hi, ALU.subtract, w=[t])

        def to_T(src, stage, gain, shift, w, split=True):
            toks = []
            for k2 in range(4):
                b, bw = pb.get()
                for kk in range(2):
                    for i in range(2):
                        t = tr(ps[:, b, kk * 256 + i * 128:kk * 256 + i * 128 + 128],
                               src[:, i, 2 * k2 + kk::8], w=[*w, *bw])
                for kk in range(2):
                    k = 2 * k2 + kk
                    u = A(stage[:, k, :], ps[:, b, kk * 256:kk * 256 + 256], ACT.Identity, scale=gain[:, k:k + 1],
                          **({} if shift is None else {"bias": shift[:, k:k + 1]}), w=[t])
                pb.put(b, 1, u)
                if split:
                    ks = slice(2 * k2, 2 * k2 + 2)
                    u = V("copy", hT[0][:, ks, :], stage[:, ks, :], w=[u])
                    u = V("tt", hT[1][:, ks, :], stage[:, ks, :], hT[0][:, ks, :], ALU.subtract)
                toks.append(u)
            return toks[-1:]

        def rows(wap, c0, cn, k0, kn):
            return wap[:, c0:c0 + cn].rearrange("(p k) n -> p k n", k=8)[:, k0:k0 + kn, :]

        def cols(cn, w, sink):
            b, bw = pb.get(2)
            t = None
            for half in range(2):
                tile, tok, n = W.next()
                for i in range(2):
                    for k in range(4):
                        kk = 4 * half + k
                        pr = parts3([v[:, kk, i * 128:(i + 1) * 128] for v in hT], [v[:, k, :] for v in tile])
                        for q, (l, r) in enumerate(pr):
                            t = mm1(ps[:, b + i, 0:cn], l, r, kk == 0 and q == 0, kk == 7 and q == 2,
                                    w=[tok, *w, *bw], inc=(k == 3 and q == 2))
                W.free(n, t)
            used = [sink(i, ps[:, b + i, 0:cn], t) for i in range(2)]
            pb.put(b, 2, *used)
            return used

        def colsT(cn, w, bank=None):
            nb = cn // 256
            b, bw = pb.get(nb) if bank is None else bank
            t = None
            for half in range(2):
                tile, tok, n = W.next()
                for m in range(cn // 128):
                    for k in range(4):
                        kk = 4 * half + k
                        pr = parts3([v[:, k, m * 128:(m + 1) * 128] for v in tile], [v[:, kk, :] for v in hT])
                        for q, (l, r) in enumerate(pr):
                            t = mm1(ps[:, b + m // 2, (m % 2) * 256:(m % 2) * 256 + 256], l, r,
                                    kk == 0 and q == 0 and m % 2 == 0, kk == 7 and q == 2,
                                    w=[tok, *w, *bw], inc=(k == 3 and q == 2))
                W.free(n, t)
            return b, t

        cc = PR("c")
        t = A(cact[:, 0:8], cc, ACT.Exp, scale=-1.0)
        V("ts", cact[:, 8:16], cact[:, 0:8], 1.0, None, ALU.add, w=[t])
        V("recip", cact[:, 8:16], cact[:, 8:16])
        CACT = V("tt", cact[:, 16:24], cact[:, 8:16], cc, ALU.mult)
        s_mod = sem("s_mod")
        n_mod = [0]

        def ada_plan(l):
            for c in range(12):
                for half in range(2):
                    W.add(rows(a["w_ada"][l], c * 512, 512, 4 * half, 4), 4, 512, split=False)

        def ada(l):
            barrier()
            mrow = ar[0:1, 0:6144]
            brow = ar[0:1, 6144:12288]
            n_mod[0] += 16
            tb = AC.dma(lambda e: e.dma_start(brow, a["b_ada"][l:l + 1, :]), s_mod, n_mod[0])
            for c in range(12):
                b, bw = pb.get()
                for half in range(2):
                    tile, tok, n = W.next()
                    for k in range(4):
                        kk = 4 * half + k
                        t = mm1(ps[0:1, b, :], cact[:, 16 + kk:17 + kk], tile[:, k, :], kk == 0, kk == 7,
                                w=[tok, CACT, *bw], inc=(k == 3))
                    W.free(n, t)
                cs = slice(c * 512, c * 512 + 512)
                t = V("tt", mrow[:, cs], ps[0:1, b, :], brow[:, cs], ALU.add, w=[t, tb])
                pb.put(b, 1, t)
            for s in range(6):
                n_mod[0] += 16
                td = AC.dma(lambda e, s=s: e.dma_start(
                    modc[:, s, :], mrow[:, s * 1024:(s + 1) * 1024].rearrange("o (p k) -> o p k", k=8)),
                    s_mod, n_mod[0], t)
            for g, s in ((0, 2), (1, 5)):
                for h in range(2):
                    b, bw = pb.get()
                    tm = mm(ps[:, b, :], [(C("ones")[0:1, :], mrow[:, s * 1024 + h * 512:s * 1024 + h * 512 + 512])],
                            w=[t, *bw])
                    pb.put(b, 1, acopy(gate[:, g, h * 512:(h + 1) * 512], ps[:, b, :], w=[tm]))
            V("stt", aff[:, 0, :], modc[:, 1, :], 1.0, PR(f"nm{l}"), ALU.add, ALU.mult, w=[td])
            V("copy", aff[:, 1, :], modc[:, 0, :])
            V("stt", aff[:, 2, :], modc[:, 4, :], 1.0, PR(f"nf{l}"), ALU.add, ALU.mult)
            V("copy", aff[:, 3, :], modc[:, 3, :])
            barrier()

        def residual(c, i, p, t, g=None):
            xs = x[:, i, c * 512:(c + 1) * 512]
            if g is None:
                return V("tt", xs, xs, p, ALU.add, w=[t])
            tmp = xn[:, i, c * 512:(c + 1) * 512]
            t1 = V("tt", tmp, p, gate[:, g, c * 512:(c + 1) * 512], ALU.mult, w=[t])
            V("tt", xs, xs, tmp, ALU.add)
            return t1

        def cols_plan(wap, c0, cn):
            for half in range(2):
                W.add(rows(wap, c0, cn, 4 * half, 4), 4, cn)

        def out_proj(mix, stage, gain, w, g=None):
            tt = to_T(mix, stage, gain, None, w)
            for c in range(2):
                cols(512, tt, lambda i, p, t, c=c: residual(c, i, p, t, g))

        def mix1_plan(l):
            win = a["w_in"][l]
            for c in (0, 512, 1024, 1536, 2048, 2560):
                cols_plan(win, c, 512)
            W.add(rows(win, 3072, 16, 0, 8), 8, 16, split=False)
            for c in range(2):
                cols_plan(a["w_out"][l], c * 512, 512)

        def mix1(l):
            barrier()
            proj = carve(0, 2, 2560)
            gqT = carve(5120, 2, 256)
            gkT = carve(5632, 2, 256)
            mix = xn
            qkT = carve(6400, 8, 256)
            stage = carve(8448, 8, 256)
            th = norm_T(stage, aff[:, 0, :], aff[:, 1, :])

            def sink(c):
                return lambda i, p, t: (acopy if i else lambda o, s, w: V("copy", o, s, w=w))(
                    proj[:, i, c * 512:(c + 1) * 512], p, w=[t])

            P = []
            for c in range(3):
                P += cols(512, th, sink(c))
            b, tm = colsT(512, th)
            t1 = acopy(gqT, ps[:, b, :].rearrange("p (a b) -> p a b", b=256), w=[tm])
            t2 = V("copy", gkT, ps[:, b + 1, :].rearrange("p (a b) -> p a b", b=256), w=[tm])
            pb.put(b, 2, t1, t2)
            for c in range(3, 5):
                P += cols(512, th, sink(c))
            tile, tok, n = W.next()
            b, bw = pb.get()
            tm = mm(ps[0:16, b, 0:256], [(tile[:, k, :], stage[:, k, :]) for k in range(8)], w=[tok, *th, *bw])
            W.free(n, tm)
            lrT = carve(6144, 256)[0:16, :]
            t_lr = acopy(lrT, ps[0:16, b, 0:256], w=[tm])
            pb.put(b, 1, t_lr)
            sq = carve(10496, 2, 1024)
            t = V("tt", sq, proj[:, :, 0:1024], proj[:, :, 0:1024], ALU.mult, w=P)
            t = V("red", st[:, 0:32], sq.rearrange("p i (h d) -> p (i h) d", d=64), AX.X, ALU.add)
            t = rstd(st[:, 32:64], st[:, 0:32], 64, w=[t])
            for i in range(2):
                t = V("tt", xn[:, i, :].rearrange("p (h d) -> p h d", d=64),
                      proj[:, i, 0:1024].rearrange("p (h d) -> p h d", d=64),
                      bc(st[:, 32 + 16 * i:48 + 16 * i], 2, 64), ALU.mult, w=[t])
            tq = []
            for c in range(4):
                b, bw = pb.get()
                for m in range(2):
                    for i in range(2):
                        tm = tr(ps[:, b, m * 256 + i * 128:m * 256 + i * 128 + 128],
                                xn[:, i, (2 * c + m) * 128:(2 * c + m + 1) * 128], w=[t, *bw])
                o = qkT[:, 2 * c:2 * c + 2, :]
                s = ps[:, b, :].rearrange("p (a b) -> p a b", b=256)
                if c < 2:
                    tv = V("ts", o, s, PR(f"qg{l}"), 0.125, ALU.mult, ALU.mult, w=[tm])
                else:
                    tv = V("ts", o, s, PR(f"kg{l}"), None, ALU.mult, w=[tm])
                pb.put(b, 1, tv)
                tq.append(tv)
            S = 8448
            ab, ex, sp, wt = (carve(S + 1536 * q, 4, 384) for q in range(4))
            for g in range(2):
                def qh(h):
                    return slice((h % 2) * 64, (h % 2) * 64 + 64), h // 2

                def scores(b, j, h, w):
                    pr, ct = qh(h)
                    kk, qq = qkT[pr, 4 + ct, :], qkT[pr, ct, :]
                    return ((ps[:, b + j, 0:256], kk[:, 0:128], qq), (ps[:, b + j, 256:384], kk[:, 128:256], qq[:, 128:256]))

                b, bw = pb.get(4)
                for j in range(4):
                    for o, ll, rr in scores(b, j, 4 * g + j, None):
                        tm = mm(o, [(ll, rr)], w=[*tq, *bw])
                z = ps[:, b:b + 4, 0:384]
                t = A(ab, z, ACT.Abs, w=[tm])
                t = A(ex, ab, ACT.Exp, scale=-1.0, w=[t])
                t = A(ab, ex, ACT.Ln, bias=1.0)
                for j in range(4):
                    t = V("stt", sp[:, j, :], z[:, j, :], 0.0, ab[:, j, :], ALU.max, ALU.add, w=[t])
                pb.put(b, 4, t)
                for o in (0, 256):
                    t = V("tt", sp[:, :, o:o + 128], sp[:, :, o:o + 128], bc(C("keep"), 1, 4), ALU.mult)
                b, bw = pb.get(4)
                for j in range(4):
                    (o0, l0, r0), (o1, l1, r1) = scores(b, j, 4 * g + j, None)
                    mm1(o0, l0, r0, True, False, w=[t, *bw])
                    mm1(o0, C("tri"), sp[:, j, 0:256], False, False)
                    mm1(o0[:, 128:256], C("neg1"), sp[:, j, 256:384], False, False)
                    mm1(o0[:, 0:128], ident, C("mneg"), False, True)
                    mm1(o1, l1, r1, True, False)
                    mm1(o1, C("tri"), sp[:, j, 256:384], False, False)
                    tm = mm1(o1, ident, C("mneg"), False, True, inc=True)
                t = A(wt, ps[:, b:b + 4, 0:384], ACT.Exp, w=[tm])
                pb.put(b, 4, t)
                b, bw = pb.get()
                for j in range(4):
                    vc = slice(1024 + (4 * g + j) * 64, 1024 + (4 * g + j) * 64 + 64)
                    mm(ps[:, b, j * 64:j * 64 + 64], [(wt[:, j, 0:128], proj[:, 0, vc])], w=[t, *P, *bw])
                    tm = mm(ps[:, b, 256 + j * 64:256 + j * 64 + 64],
                            [(wt[:, j, 128:256], proj[:, 0, vc]), (wt[:, j, 256:384], proj[:, 1, vc])])
                t = V("copy", mix[:, :, g * 256:(g + 1) * 256], ps[:, b, :].rearrange("p (a b) -> p a b", b=256), w=[tm])
                pb.put(b, 1, t)
            barrier()
            u, lg, bb, eb, enb, ekd, qd, ki, kd = (carve(6400 + 512 * q, 512) for q in range(9))
            qde, qdo, kdt = (carve(6400 + 512 * (9 + q), 2, 256) for q in range(3))
            state = carve(12544, 2, 4, 128)
            sm = carve(13568, 8, 128)
            V("memset", qde, 0.0)
            V("memset", qdo, 0.0)
            V("memset", sm, 0.0)
            b, bw = pb.get()
            for f in range(2):
                tm = mm(ps[:, b, f * 256:f * 256 + 256], [(PR(f"gk2{l}", 16)[:, f * 128:(f + 1) * 128], lrT)], w=[t_lr, *bw])
            for f in range(2):
                t = V("ts", u[:, f * 256:f * 256 + 256], ps[:, b, f * 256:f * 256 + 256], PR(f"bgk{l}")[:, f:f + 1], None,
                      ALU.add, w=[tm])
            pb.put(b, 1, t)
            t = A(bb, u, ACT.Abs, w=[t])
            t = A(eb, bb, ACT.Exp, scale=-1.0, w=[t])
            t = A(enb, eb, ACT.Ln, bias=1.0)
            t = V("stt", lg, u, 0.0, enb, ALU.min, ALU.subtract, w=[t])
            for f in range(2):
                t = V("scan", bb[:, f * 256:f * 256 + 256], C("reset"), lg[:, f * 256:f * 256 + 256], 0.0, ALU.mult, ALU.add)
            A(eb, bb, ACT.Exp, scale=1 / 16, w=[t])
            t1 = A(enb, bb, ACT.Exp, scale=-1 / 16)
            b4 = bb.rearrange("p (c s) -> p c s", s=64)
            t = V("tt", u.rearrange("p (c s) -> p c s", s=64), b4[:, :, 63:64].to_broadcast([128, 8, 64]), b4, ALU.subtract)
            t2 = A(ekd, u, ACT.Exp, scale=1 / 16, w=[t])
            gq = gqT.rearrange("p a b -> p (a b)")
            gk = gkT.rearrange("p a b -> p (a b)")
            V("stt", qd, gq, 0.125, eb, ALU.mult, ALU.mult, w=[t1])
            V("tt", ki, gk, enb, ALU.mult)
            t = V("tt", kd, gk, ekd, ALU.mult, w=[t2])
            qd4 = qd.rearrange("p (f c e s) -> p f c e s", f=2, c=2, e=2)
            for e, dst in ((0, qde), (1, qdo)):
                tqd = V("copy", dst.rearrange("p f (c e s) -> p f c e s", c=2, e=2)[:, :, :, e, :], qd4[:, :, :, e, :])
            b, bw = pb.get()
            for i in range(2):
                for f in range(2):
                    tm = tr(ps[:, b, i * 256 + f * 128:i * 256 + f * 128 + 128],
                            kd[:, f * 256 + i * 128:f * 256 + i * 128 + 128], w=[t, *bw])
            tk = acopy(kdt, ps[:, b, :].rearrange("p (a b) -> p a b", b=256), w=[tm])
            pb.put(b, 1, tk)
            b, bw = pb.get(3)
            for c in range(3):
                pr = slice((c % 2) * 64, (c % 2) * 64 + 64)
                for f in range(2):
                    tm = mm(ps[:, b + c, f * 256:f * 256 + 256],
                            [(kdt[pr, c // 2, f * 128:(f + 1) * 128], proj[pr, c // 2, 1536 + f * 256:1536 + f * 256 + 256])],
                            w=[tk, *bw])
            for c in range(3):
                for f in range(2):
                    for hh in range(2):
                        pr = slice(hh * 64, hh * 64 + 64)
                        o = state[pr, f, c + 1, :]
                        kv = ps[pr, b + c, f * 256 + hh * 128:f * 256 + hh * 128 + 128]
                        if c == 0:
                            ts = V("copy", o, kv, w=[tm])
                        else:
                            ts = V("stt", o, state[pr, f, c, :], eb[pr, f * 256 + c * 64 + 63:f * 256 + c * 64 + 64], kv,
                                   ALU.mult, ALU.add, w=[tm])
            pb.put(b, 3, ts)
            b, bw = pb.get(2)
            for i in range(2):
                for h in range(4):
                    pr, f = slice((h % 2) * 64, (h % 2) * 64 + 64), h // 2
                    cs = slice(f * 256 + i * 128, f * 256 + i * 128 + 128)
                    tm = mm(ps[:, b + h % 2, i * 256 + f * 128:i * 256 + f * 128 + 128], [(ki[pr, cs], qd[pr, cs])], w=[tqd, *bw])
            gm = bc(C("glam"), 1, 4).bitcast(U32)
            for i in range(2):
                t = V("cpred", sm[:, 4 * i:4 * i + 4, :], gm, ps[:, b + i, :].rearrange("p (a b) -> p a b", b=128), w=[tm])
            pb.put(b, 2, t)
            b, bw = pb.get(4)
            for i in range(2):
                for h in range(4):
                    pr, f = slice((h % 2) * 64, (h % 2) * 64 + 64), h // 2
                    cs = slice(i * 128, i * 128 + 128)
                    pairs = [(sm[:, 4 * (h % 2) + 2 * i + f, :], proj[:, i, 1536 + h * 128:1536 + h * 128 + 128])]
                    if i:
                        pairs.append((qde[pr, f, cs], state[pr, f, 2, :]))
                    pairs.append((qdo[pr, f, cs], state[pr, f, 2 * i + 1, :]))
                    tm = mm(ps[:, b + 2 * i + h % 2, f * 128:f * 128 + 128], pairs, w=[t, ts, *bw])
            o = carve(14592, 2, 512)
            sg = carve(15616, 2, 512)
            s2 = carve(16640, 2, 512)
            for i in range(2):
                t = V("copy", o[:, i, :].rearrange("p (f e d) -> p e f d", f=2, e=2),
                      ps[:, b + 2 * i:b + 2 * i + 2, 0:256].rearrange("p e (f d) -> p e f d", d=128), w=[tm])
            pb.put(b, 4, t)
            V("tt", s2, o, o, ALU.mult)
            t = V("red", st[:, 0:8], s2.rearrange("p i (h d) -> p (i h) d", d=128), AX.X, ALU.add)
            t1 = rstd(st[:, 8:16], st[:, 0:8], 128, w=[t])
            t = A(sg, proj[:, :, 2048:2560], ACT.Exp, scale=-1.0)
            V("ts", sg, sg, 1.0, None, ALU.add, w=[t])
            V("recip", sg, sg)
            V("tt", sg, sg, proj[:, :, 2048:2560], ALU.mult)
            V("tt", o.rearrange("p i (h d) -> p (i h) d", d=128), o.rearrange("p i (h d) -> p (i h) d", d=128),
              bc(st[:, 8:16], 2, 128), ALU.mult, w=[t1])
            t = V("tt", mix[:, :, 512:1024], o, sg, ALU.mult)
            barrier()
            out_proj(mix, carve(6400, 8, 256), PR(f"mg{l}"), [t], 0)
            barrier()

        over_at = []

        def moe_plan(l):
            wg, wu, wd = (a[k][l].rearrange("g e a b -> (g e) a b") for k in ("w_gate", "w_up", "w_down"))
            for e in range(33):
                if e < 32:
                    W.add(wg[e].rearrange("(p k) f -> p k f", k=8), 8, 256)
                    W.add(wu[e].rearrange("(p k) f -> p k f", k=8), 8, 256)
                if e:
                    W.add(wd[e - 1].rearrange("(p k) d -> p k d", k=2), 2, 1024)
            over_at.append(len(SP.items))
            SP.items.append(None)


        def overflow(l, totals, w):
            v = carve(U_N + 3568, 16)
            V("ts", v[:, 0:4], totals, 128.5, None, ALU.is_gt, w=w)
            V("tt", v[:, 4:8], v[:, 0:4], C("iota8")[:, 0:4], ALU.mult)
            V("red", v[:, 8:10], v[:, 0:8].rearrange("p (a b) -> p a b", b=4), AX.X, ALU.add)
            return V("copy", flags[:, l, :], v[:, 8:10])

        def rest(l, flag_tok, pos, ew):
            barrier()
            waits = [e.now() for e in ENG]
            order = (PE, DV, AC, PO, SP)
            for e, n in zip(order, ("pe", "dve", "act", "pool", "sp")):
                e.begin(sem(f"r{l}_{n}"))
            s_w = [sem(f"r{l}_w{q}") for q in range(3)]
            x5, p5, p5T = carve(0, 2, 1024), carve(2048, 2, 128), carve(2304, 256)
            xg, combs = carve(2624, 8, 128), carve(2560, 8)
            wb = [carve(3712 + 2048 * q, 2048) for q in range(3)]
            sl, hs, aT, ys = carve(9920, 256), carve(10176, 256), carve(10432, 2, 128), carve(0, 1024)
            pos5 = carve(2576, 2, 4)
            t = V("ts", pos5, pos, -128.0, None, ALU.add)
            for i in range(2):
                V("ts", x5[:, i, :], x[:, i, :], st[:, 2 + i:3 + i], None, ALU.mult)
                V("ts", p5[:, i, :], C("slot"), pos5[:, i, 0:1], None, ALU.is_equal)
                for g in range(1, 4):
                    t = V("stt", p5[:, i, :], C("slot"), pos5[:, i, g:g + 1], p5[:, i, :], ALU.is_equal, ALU.add)
            for k in range(8):
                tm = mm(ps[:, k // 4, 128 * (k % 4):128 * (k % 4) + 128],
                        [(x5[:, i, k::8], p5[:, i, :]) for i in range(2)], w=[t])
            tm = mm(ps[:, 2, 0:8], [(p5[:, i, :], ew[:, i, :]) for i in range(2)], w=[t])
            for i in range(2):
                tm = tr(ps[:, 3, 128 * i:128 * i + 128], p5[:, i, :], w=[t])
            for k in range(8):
                A(xg[:, k, :], ps[:, k // 4, 128 * (k % 4):128 * (k % 4) + 128], ACT.Identity,
                  scale=aff[:, 2, k:k + 1], bias=aff[:, 3, k:k + 1], w=[tm])
            acopy(combs, ps[:, 2, 0:8])
            tx = acopy(p5T, ps[:, 3, 0:256])
            wv = [a["w_gate"][l], a["w_up"][l], a["w_down"][l]]
            down, group = None, []
            for e in range(8):
                def source(eng, q, e):
                    if not group:
                        group.append(eng.value_load(flags[0:1, l, 1:2], min_val=0, max_val=3))
                    v = wv[q][bass.ds(group[0], 1), e, :, :].rearrange("o a b -> (o a) b")
                    return v.rearrange("(p k) f -> p (k f)", p=128)

                toks = []
                for q in range(3):
                    toks.append(SP.dma(lambda eng, q=q, e=e: eng.dma_start(wb[q], source(eng, q, e)), s_w[q], 16 * (e + 1),
                                       *(waits if e == 0 else [down])))
                for q in range(2):
                    wt = wb[q].rearrange("p (k f) -> p k f", k=8)
                    tm = mm(ps[:, 4, 256 * q:256 * q + 256], [(xg[:, k, :], wt[:, k, :]) for k in range(8)], w=[toks[q], tx])
                t = A(sl, ps[:, 4, 0:256], ACT.Silu, w=[tm])
                t = V("stt", hs, ps[:, 4, 256:512], combs[:, e:e + 1], sl, ALU.mult, ALU.mult, w=[t])
                for f in range(2):
                    tm = tr(ps[:, 5, 128 * f:128 * f + 128], hs[:, f::2], w=[t])
                t = acopy(aT, ps[:, 5, 0:256].rearrange("p (f n) -> p f n", f=2), w=[tm])
                wt = wb[2].rearrange("p (k f) -> p k f", k=2)
                for c in range(2):
                    for f in range(2):
                        down = mm1(ps[:, 6 + c, :], aT[:, f, :], wt[:, f, 512 * c:512 * c + 512], e == 0 and f == 0,
                                   e == 7 and f == 1, w=[toks[2], t], inc=(f == 1))
                tx = down
            t = acopy(ys, ps[:, 6:8, :].rearrange("p c n -> p (c n)"), w=[down])
            for i in range(2):
                for c in range(2):
                    tm = mm(ps[:, 2 * i + c, :], [(p5T[:, 128 * i:128 * i + 128], ys[:, 512 * c:512 * c + 512])], w=[t])
            for i in range(2):
                for c in range(2):
                    o = xn[:, i, 512 * c:512 * c + 512]
                    t = V("tt", o, o, ps[:, 2 * i + c, :], ALU.add, w=[tm])
            DV.items.append(([t], None, None, 0))
            for e in order:
                e.end(flags[0:1, l, 0:1], flag_tok, over_at.pop(0) if e is SP else None)
            pb.freed = [[] for _ in range(8)]

        def moe(l):
            barrier()
            S = U_N
            stage = carve(S, 8, 256)
            P = carve(S + 2048, 2, 512)
            lgt = carve(S + 3072, 2, 36)
            lT = carve(S + 3200, 256)[0:36, :]
            g8, m8, sel, ew, oh1, oh2 = (carve(S + 3456 + 16 * q, 2, 8) for q in range(6))
            tmp = carve(S + 3584, 2, 32)
            ohg, pos, et, sc = (carve(S + 3648 + 8 * q, 2, 4) for q in range(4))
            w12 = carve(S + 3680, 8, 2)
            combs = carve(S + 3712, 4, 8)
            gst = [carve(S + 3776 + 512 * q, 512) for q in range(2)]
            sl = [carve(S + 4800 + 256 * q, 256) for q in range(2)]
            hs = [carve(S + 5312 + 256 * q, 256) for q in range(2)]
            xg = [ur[:, 4096 * q:4096 * q + 4096].rearrange("p (k n) -> p k n", k=8) for q in range(2)]
            pr_ = ur[:, 8192:9216].rearrange("p (i n) -> p i n", i=2)
            xs = [hh[:, q, :].rearrange("p (i n) -> p i n", i=2) for q in range(2)]
            t = norm()
            th = to_T(xn, stage, aff[:, 2, :], aff[:, 3, :], [t], split=False)
            txs = split2(hh[:, 0, :], hh[:, 1, :], xn[:, :, :].rearrange("p i n -> p (i n)"), [t])
            rw = PR(f"rw{l}").rearrange("p (k n) -> p k n", k=8)
            b, bw = pb.get()
            tm = mm(ps[0:36, b, 0:256], [(rw[:, k, :], stage[:, k, :]) for k in range(8)], w=[*th, *bw])
            t = acopy(lT, ps[0:36, b, 0:256], w=[tm])
            pb.put(b, 1, t)
            b, bw = pb.get()
            for i in range(2):
                tm = tr(ps[:, b, i * 36:i * 36 + 36], lT[:, i * 128:(i + 1) * 128], w=[t, *bw])
            V("memset", g8, -3e38)
            t = V("tt", lgt, ps[:, b, 0:72].rearrange("p (i n) -> p i n", i=2), bc(PR(f"rb{l}"), 1, 2), ALU.add, w=[tm])
            pb.put(b, 1, t)

            def top(v):
                for i in range(2):
                    V("max", m8[:, i, :], v[:, i, :])
                    V("maxidx", ixt[:, i, :], m8[:, i, :], v[:, i, :])
                return V("copy", et8, ixt[:, :, :])

            et8 = carve(S + 3552, 2, 8)
            V("copy", g8[:, :, 0:4], lgt[:, :, 0:4])
            top(g8)
            tohg = V("tt", ohg, bc(C("iota8")[:, 0:4], 1, 2), et8[:, :, 0:1].to_broadcast([128, 2, 4]), ALU.is_equal)
            t = V("tt", et, lgt[:, :, 0:4], m8[:, :, 0:1].to_broadcast([128, 2, 4]), ALU.subtract)
            t = A(et, et, ACT.Exp, w=[t])
            b, bw = pb.get()
            o = ps[:, b, 0:12].rearrange("p (i n) -> p i n", n=4)
            mm(o[:, 0, :], [(C("stri"), ohg[:, 0, :])], w=[tohg, *bw])
            mm(o[:, 1, :], [(C("stri"), ohg[:, 1, :]), (C("ones"), ohg[:, 0, :])])
            tm = mm(o[:, 2, :], [(C("ones"), ohg[:, 0, :]), (C("ones"), ohg[:, 1, :])])
            V("stt", pos.rearrange("p i g -> p (i g)"), ohg.rearrange("p i g -> p (i g)"), -1e6, ps[:, b, 0:8],
              ALU.mult, ALU.add, w=[tm])
            p4 = P.rearrange("p i (g s) -> p (i g) s", s=128)
            tP = V("tt", p4, bc(C("slot"), 1, 8), bc(pos.rearrange("p i g -> p (i g)"), 2, 128), ALU.is_equal)
            flag_tok = overflow(l, o[:, 2, :], [tm])
            pb.put(b, 1, DV.now())
            tpr = acopy(pr_.rearrange("p i n -> p (i n)"), P.rearrange("p i n -> p (i n)"), w=[tP])
            tx = None
            for k in range(8):
                b, bw = pb.get()
                for q, (i, z) in enumerate(((0, 0), (0, 1), (1, 0), (1, 1))):
                    tm = mm1(ps[:, b, :], xs[z][:, i, k::8], pr_[:, i, :], q == 0, q == 3, w=[tpr, txs, *bw], inc=(q == 3))
                g = gst[k % 2]
                t = A(g, ps[:, b, :], ACT.Identity, scale=aff[:, 2, k:k + 1], bias=aff[:, 3, k:k + 1], w=[tm, tx])
                pb.put(b, 1, t)
                V("copy", xg[0][:, k, :], g, w=[t])
                tx = V("tt", xg[1][:, k, :], g, xg[0][:, k, :], ALU.subtract)
            tg_all = tm
            V("red", sc[:, :, 0:1].rearrange("p i o -> p (i o)"), et, AX.X, ALU.add)
            V("recip", sc[:, :, 1], sc[:, :, 0])
            t4 = tmp.rearrange("p i (g e) -> p i g e", e=8)
            V("tt", t4, lgt[:, :, 4:36].rearrange("p i (g e) -> p i g e", e=8), bc(ohg, 3, 8), ALU.mult)
            V("red", sel, tmp.rearrange("p i (g e) -> p i e g", e=8), AX.X, ALU.add)
            top(sel)
            V("tt", oh1, bc(C("iota8"), 1, 2), et8[:, :, 0:1].to_broadcast([128, 2, 8]), ALU.is_equal)
            V("tt", oh2, bc(C("iota8"), 1, 2), et8[:, :, 1:2].to_broadcast([128, 2, 8]), ALU.is_equal)
            t = V("tt", w12[:, 0, :], m8[:, :, 1], m8[:, :, 0], ALU.subtract)
            t = A(w12[:, 1, :], w12[:, 0, :], ACT.Exp, w=[t])
            V("ts", w12[:, 2, :], w12[:, 1, :], 1.0, None, ALU.add, w=[t])
            V("recip", w12[:, 3, :], w12[:, 2, :])
            V("tt", w12[:, 4, :], w12[:, 3, :], sc[:, :, 1], ALU.mult)
            V("tt", w12[:, 5, :], w12[:, 4, :], w12[:, 1, :], ALU.mult)
            V("tt", oh1, oh1, bc(w12[:, 4, :], 2, 8), ALU.mult)
            V("tt", oh2, oh2, bc(w12[:, 5, :], 2, 8), ALU.mult)
            tew = V("tt", ew, oh1, oh2, ALU.add)
            b, bw = pb.get()
            for g in range(4):
                tm = mm(ps[:, b, 8 * g:8 * g + 8], [(P[:, i, 128 * g:128 * g + 128], ew[:, i, :]) for i in range(2)],
                        w=[tew, tP, *bw])
            tcs = V("copy", combs.rearrange("p g e -> p (g e)"), ps[:, b, 0:32], w=[tm])
            pb.put(b, 1, tcs)
            pT = hh[:, 0, 0:1024].rearrange("p (g n) -> p g n", g=4)
            ys = [hh[:, 1, 1024 * z:1024 * z + 1024] for z in range(2)]
            aT = [[hh[:, 0, 1024 + 512 * q + 256 * z:1280 + 512 * q + 256 * z].rearrange("p (f n) -> p f n", f=2)
                   for z in range(2)] for q in range(2)]
            tpT = []
            for g2 in range(2):
                b, bw = pb.get()
                for gg in range(2):
                    for i in range(2):
                        g = 2 * g2 + gg
                        tm = tr(ps[:, b, 256 * gg + 128 * i:256 * gg + 128 * i + 128], P[:, i, 128 * g:128 * g + 128],
                                w=[tP, *bw])
                t = acopy(pT[:, 2 * g2:2 * g2 + 2, :], ps[:, b, :].rearrange("p (g n) -> p g n", g=2), w=[tm, tg_all])
                pb.put(b, 1, t)
                tpT.append(t)
            barrier()
            gu_free, h_done, tr_done, aT_done = [None] * 2, [None] * 2, [None] * 2, [None] * 2
            aT_free, y_free, ys_free, sc_free = [None] * 2, None, None, [None] * 2

            def turn(e):
                q = e % 2
                for f in range(2):
                    t = tr(ps[:, 4 + q, 128 * f:128 * f + 128], hs[q][:, f::2], w=[h_done[q], aT_done[q]])
                tr_done[q] = t
                src = ps[:, 4 + q, 0:256].rearrange("p (f n) -> p f n", f=2)
                t = AC.op(lambda eng: eng.activation(aT[q][0], src, ACT.Copy), t, aT_free[q], chain=False)
                aT_done[q] = DV.op(lambda eng: eng.tensor_tensor(aT[q][1], src, aT[q][0], ALU.subtract), t, chain=False)

            for e in range(33):
                q, g = e % 2, e // 8
                if e < 32:
                    for z in range(2):
                        tile, tok, n = W.next()
                        for k in range(8):
                            pr = parts3([v[:, k, 128 * g:128 * g + 128] for v in xg], [v[:, k, :] for v in tile])
                            for j, (l_, r_) in enumerate(pr):
                                tm = mm1(ps[:, 2 + q, 256 * z:256 * z + 256], l_, r_, k == 0 and j == 0 and z == 0,
                                         k == 7 and j == 2, w=[tok, gu_free[q]], inc=(k == 7 and j == 2))
                        W.free(n, tm)
                        if z == 0 and e:
                            turn(e - 1)
                    t = AC.op(lambda eng, q=q: eng.activation(sl[q], ps[:, 2 + q, 0:256], ACT.Silu), tm, h_done[q], chain=False)
                    h_done[q] = gu_free[q] = DV.op(
                        lambda eng, q=q, g=g, e=e: eng.scalar_tensor_tensor(
                            out=hs[q], in0=ps[:, 2 + q, 256:512], scalar=combs[:, g, e % 8:e % 8 + 1], in1=sl[q],
                            op0=ALU.mult, op1=ALU.mult), t, tr_done[q], chain=False)
                else:
                    turn(e - 1)
                if not e:
                    continue
                d, q = e - 1, (e - 1) % 2
                tile, tok, n = W.next()
                for c in range(2):
                    for f in range(2):
                        pr = parts3([v[:, f, :] for v in aT[q]], [v[:, f, 512 * c:512 * c + 512] for v in tile])
                        for j, (l_, r_) in enumerate(pr):
                            tm = mm1(ps[:, c, :], l_, r_, d % 8 == 0 and f == 0 and j == 0,
                                     d % 8 == 7 and f == 1 and j == 2, w=[tok, aT_done[q], y_free],
                                     inc=(f == 1 and j == 2))
                W.free(n, tm)
                aT_free[q] = tm
                if d % 8 < 7:
                    continue
                g = d // 8
                yv = ps[:, 0:2, :].rearrange("p c n -> p (c n)")
                t = acopy(ys[0], yv, w=[tm, ys_free])
                t = y_free = V("tt", ys[1], yv, ys[0], ALU.subtract, w=[t])
                for i in range(2):
                    for c in range(2):
                        for z in range(2):
                            tm = mm1(ps[:, 6 + c, :], pT[:, g, 128 * i:128 * i + 128], ys[z][:, 512 * c:512 * c + 512],
                                     z == 0, z == 1, w=[t, *tpT, sc_free[c]], inc=(z == 1))
                        o = xn[:, i, 512 * c:512 * c + 512]
                        if g == 0:
                            sc_free[c] = V("copy", o, ps[:, 6 + c, :], w=[tm])
                        else:
                            sc_free[c] = V("tt", o, o, ps[:, 6 + c, :], ALU.add, w=[tm])
                ys_free = tm
            rest(l, flag_tok, pos, ew)
            gv = gate[:, 1, :]
            for i in range(2):
                V("tt", xn[:, i, :], xn[:, i, :], gv, ALU.mult)
                V("tt", x[:, i, :], x[:, i, :], xn[:, i, :], ALU.add)
            barrier()

        s_na = sem("s_na")
        n_na = [0]

        def mix2_plan(l):
            for c in range(5):
                cols_plan(a["w_in_2"][l], c * 480, 480)
            W.add(a["mla_w_uq_2"][l][0:128, :], 384, split=False)
            W.add(a["mla_w_uq_2"][l][128:192, :], 384, parts=64, split=False)
            W.add(a["mla_w_uk_2"][l], 256, split=False)
            W.add(a["mla_w_uv_2"][l], 256, split=False)
            for c in range(2):
                cols_plan(a["w_out_2"][l], c * 512, 512)

        def mix2(l):
            barrier()
            proj = carve(0, 2, 2400)
            q3 = carve(4800, 2, 1152)
            naT = carve(7104, 4, 6, 64)
            mix = carve(8640, 2, 1024)
            qT = carve(10688, 4, 256)
            kT = carve(11712, 4, 256)
            sc_ = carve(12736, 4, 256)
            pt = carve(13760, 4, 256)
            ptT = carve(14784, 4, 2, 128)
            cT = carve(15808, 2, 256)
            ckT = carve(16320, 256)
            rt = carve(16576, 2, 512)
            rt2 = xn[:, :, 512:1024]
            stage = carve(12736, 8, 256)
            sm = st
            rp = a["na_rpb"][l]
            toks = None
            for s in range(2):
                for h in range(4):
                    src = bass.AP(rp.tensor, rp.offset + 76 + 31 * s + 465 * h, [[1, 64], [31, 6], [1, 64]])
                    n_na[0] += 16
                    toks = AC.dma(lambda e, s=s, h=h, src=src: e.dma_start(naT[64 * s:64 * s + 64, h, :, :], src),
                                  s_na, n_na[0])
            th = norm_T(stage, PR(f"n1{l}"))
            P = []
            for c in range(5):
                def sink(i, p, t, c=c):
                    o = proj[:, i, c * 480:(c + 1) * 480]
                    return acopy(o, p, w=[t]) if i else V("copy", o, p, w=[t])
                P += cols(480, th, sink)
            for h in range(4):
                V("tt", naT[:, h, :, :], naT[:, h, :, :], bc(C("nam")[:, ::-1], 1, 6), ALU.add, w=[toks])

            def na_bias(i, hh):
                v = naT[:, 2 - 2 * hh:4 - 2 * hh, :, :].rearrange("p h r c -> p h (r c)")
                return v[:, ::-1, 128 * i:128 * i + 256][:, :, ::-1]

            def rope(dst, src, heads, dim, w=()):
                hf = dim // 2
                t = None
                for i in range(2):
                    cs = bc(C(f"cos{dim}")[:, i * hf:(i + 1) * hf], 1, heads)
                    sn = bc(C(f"sin{dim}")[:, i * hf:(i + 1) * hf], 1, heads)
                    x1, x2 = src[:, i, :, 0:hf], src[:, i, :, hf:dim]
                    r1 = rt[:, 0, 0:heads * hf].rearrange("p (h d) -> p h d", d=hf)
                    r2 = rt2[:, 0, 0:heads * hf].rearrange("p (h d) -> p h d", d=hf)
                    r3 = rt[:, 1, 0:heads * hf].rearrange("p (h d) -> p h d", d=hf)
                    r4 = rt2[:, 1, 0:heads * hf].rearrange("p (h d) -> p h d", d=hf)
                    V("tt", r1, x1, cs, ALU.mult, w=w)
                    V("tt", r2, x2, sn, ALU.mult)
                    V("tt", r3, x2, cs, ALU.mult)
                    V("tt", r4, x1, sn, ALU.mult)
                    V("tt", dst[:, i, :, 0:hf], r1, r2, ALU.subtract)
                    t = V("tt", dst[:, i, :, hf:dim], r3, r4, ALU.add)
                return t

            def hd(ap, d):
                return ap.rearrange("p i (h d) -> p i h d", d=d)

            def transp(dst, srcs, w):
                t = None
                for m0 in range(0, len(srcs), 2):
                    b, bw = pb.get()
                    n = srcs[m0](0).shape[-1]
                    grp = srcs[m0:m0 + 2]
                    for m, s in enumerate(grp):
                        for i in range(2):
                            tm = tr(ps[0:n, b, m * 256 + i * 128:m * 256 + i * 128 + 128], s(i), w=[*w, *bw])
                    t = acopy(dst[0:n, m0:m0 + len(grp), :],
                              ps[0:n, b, 0:256 * len(grp)].rearrange("p (a b) -> p a b", b=256), w=[tm])
                    pb.put(b, 1, t)
                return t

            def attend(i, q, k, v, scale, w, bias_=None, sink_=None, apart=False):
                nb = 4 if apart else 2
                b, bw = pb.get(nb)
                for h in range(4):
                    o = ps[:, b + h, 0:256] if apart else ps[:, b + h // 2, (h % 2) * 256:(h % 2) * 256 + 256]
                    tm = mm(o, [(q(h), k(h))], w=[*w, *bw])
                s = ps[:, b:b + 4, 0:256] if apart else ps[:, b:b + 2, :].rearrange("p a (h n) -> p (a h) n", n=256)
                if bias_ is not None:
                    for hh in range(2):
                        V("stt", sc_[:, 2 * hh:2 * hh + 2, :], s[:, 2 * hh:2 * hh + 2, :], scale, bias_(hh), ALU.mult, ALU.add,
                          w=[tm])
                    s, f = sc_, 1.0
                else:
                    f = scale
                V("red", sm[:, 0:4], s, AX.X, ALU.max, w=[tm])
                if sink_ is not None:
                    V("tt", sm[:, 0:4], sm[:, 0:4], sink_, ALU.max)
                t = V("ts", sm[:, 0:4], sm[:, 0:4], -f, None, ALU.mult)
                for h in range(4):
                    t = A(pt[:, h, :], s[:, h, :], ACT.Exp, bias=sm[:, h:h + 1], scale=f, accum_out=sm[:, 4 + h:5 + h], w=[t])
                pb.put(b, nb, t)
                if sink_ is not None:
                    t = V("tt", sm[:, 8:12], sink_, sm[:, 0:4], ALU.add, w=[t])
                    t = A(sm[:, 12:16], sm[:, 8:12], ACT.Exp, w=[t])
                    t = V("tt", sm[:, 4:8], sm[:, 4:8], sm[:, 12:16], ALU.add, w=[t])
                t = V("recip", sm[:, 16:20], sm[:, 4:8], w=[t])
                return t

            def weigh(p4, n, v, w):
                t = None
                for h0 in range(0, n, 2):
                    b, bw = pb.get()
                    for h in range(h0, h0 + 2):
                        for kt in range(2):
                            tm = tr(ps[:, b, (h - h0) * 256 + kt * 128:(h - h0) * 256 + kt * 128 + 128],
                                    p4(h)[:, kt * 128:(kt + 1) * 128], w=[*w, *bw])
                    t = acopy(ptT[:, h0:h0 + 2, :, :].rearrange("p a b c -> p (a b c)"), ps[:, b, :], w=[tm])
                    pb.put(b, 1, t)
                b, bw = pb.get()
                for h in range(n):
                    tm = mm(ps[:, b, h * 64:h * 64 + 64], [(ptT[:, h, kt, :], v(kt, h)) for kt in range(2)], w=[t, *bw])
                return b, tm

            def heads_out(i, c0, b, tm):
                t = V("tt", mix[:, i, c0:c0 + 256].rearrange("p (h d) -> p h d", d=64),
                      ps[:, b, 0:256].rearrange("p (h d) -> p h d", d=64), bc(sm[:, 16:20], 2, 64), ALU.mult, w=[tm])
                pb.put(b, 1, t)
                return t

            def group_norm(c0, w):
                V("tt", rt[:, :, 0:256], mix[:, :, c0:c0 + 256], mix[:, :, c0:c0 + 256], ALU.mult, w=w)
                t = V("red", sm[:, 20:22], rt[:, :, 0:256], AX.X, ALU.add)
                t = rstd(sm[:, 22:24], sm[:, 20:22], 256, w=[t])
                return V("tt", mix[:, :, c0:c0 + 256], mix[:, :, c0:c0 + 256], bc(sm[:, 22:24], 2, 256), ALU.mult, w=[t])

            V("tt", rt[:, :, 0:320], proj[:, :, 0:320], proj[:, :, 0:320], ALU.mult, w=P)
            V("red", sm[:, 24:26], rt[:, :, 0:192], AX.X, ALU.add)
            t = V("red", sm[:, 26:28], rt[:, :, 192:320], AX.X, ALU.add)
            rstd(sm[:, 28:30], sm[:, 24:26], 192, w=[t])
            t = rstd(sm[:, 30:32], sm[:, 26:28], 128)
            V("tt", xn[:, :, 0:192], proj[:, :, 0:192], bc(sm[:, 28:30], 2, 192), ALU.mult, w=[t])
            t = V("tt", xn[:, :, 192:320], proj[:, :, 192:320], bc(sm[:, 30:32], 2, 128), ALU.mult)
            b, bw = pb.get(2)
            for i in range(2):
                for m, (o, wd_) in enumerate(((0, 128), (128, 64), (192, 128))):
                    tm = tr(ps[0:wd_, b + m // 2, (m % 2) * 256 + i * 128:(m % 2) * 256 + i * 128 + 128],
                            xn[:, i, o:o + wd_], w=[t, *bw])
            V("ts", cT[:, 0, :], ps[:, b, 0:256], PR(f"mq{l}")[:, 0:1], None, ALU.mult, w=[tm])
            V("ts", cT[0:64, 1, :], ps[0:64, b, 256:512], PR(f"mq{l}", 64)[:, 1:2], None, ALU.mult)
            t = V("ts", ckT, ps[:, b + 1, 0:256], PR(f"mkv{l}"), None, ALU.mult)
            pb.put(b, 2, t)
            w0, k0, n0 = W.next()
            w1, k1, n1 = W.next()
            w2, k2, n2 = W.next()
            w3, k3, n3 = W.next()
            for i in range(2):
                ts_ = slice(i * 128, i * 128 + 128)
                b, bw = pb.get(2)
                mm(ps[:, b, 0:384], [(cT[:, 0, ts_], w0), (cT[0:64, 1, ts_], w1)], w=[t, k0, k1, *bw])
                mm(ps[:, b + 1, 0:256], [(ckT[:, ts_], w2)], w=[k2])
                tm = mm(ps[:, b + 1, 256:512], [(ckT[:, ts_], w3)], w=[k3])
                V("copy", q3[:, i, 0:384], ps[:, b, 0:384], w=[tm])
                tv = acopy(q3[:, i, 384:640], ps[:, b + 1, 256:512], w=[tm])
                t1 = V("copy", q3[:, i, 640:1024].rearrange("p (h d) -> p h d", d=96)[:, :, 0:64],
                       ps[:, b + 1, 0:256].rearrange("p (h d) -> p h d", d=64), w=[tv])
                pb.put(b, 2, tv, t1)
            for n in (n0, n1, n2, n3):
                W.free(n, tm)
            qv = q3[:, :, 0:384].rearrange("p i (h d) -> p i h d", d=96)
            kv = q3[:, :, 640:1024].rearrange("p i (h d) -> p i h d", d=96)
            rope(qv[:, :, :, 64:96], qv[:, :, :, 64:96], 4, 32)
            rope(hd(xn[:, :, 320:352], 32), hd(proj[:, :, 320:352], 32), 1, 32)
            for h in range(4):
                t = V("copy", kv[:, :, h, 64:96], xn[:, :, 320:352])
            t1 = transp(qT, [lambda i, h=h: q3[:, i, h * 96:h * 96 + 96] for h in range(4)], [t])
            t2 = transp(kT, [lambda i, h=h: q3[:, i, 640 + h * 96:736 + h * 96] for h in range(4)], [t])
            for i in range(2):
                ts_ = slice(i * 128, i * 128 + 128)
                t = attend(i, lambda h: qT[0:96, h, ts_], lambda h: kT[0:96, h, :], None, 96 ** -0.5, [t1, t2])
                b, tm = weigh(lambda h: pt[:, h, :], 4, lambda kt, h: q3[:, kt, 384 + h * 64:448 + h * 64], [t, tv])
                t = heads_out(i, 0, b, tm)
            group_norm(0, [t])
            lv = PR(f"lam{l}")
            V("tt", rt[:, 0, 0:32], lv[:, 0:32], lv[:, 32:64], ALU.mult)
            V("tt", rt[:, 0, 32:64], lv[:, 64:96], lv[:, 96:128], ALU.mult)
            t = V("red", sm[:, 32:34], rt[:, 0, 0:64].rearrange("p (a b) -> p a b", b=32), AX.X, ALU.add)
            t = A(sm[:, 34:36], sm[:, 32:34], ACT.Exp, w=[t])
            li = 0.8 - 0.6 * math.exp(-0.3 * l)
            V("tt", sm[:, 36:37], sm[:, 35:36], sm[:, 34:35], ALU.subtract, w=[t])
            V("ts", sm[:, 37:38], sm[:, 36:37], -li, None, ALU.add)
            t = rope(hd(xn[:, :, 0:512], 32), hd(proj[:, :, 352:864], 32), 16, 32)
            t1 = transp(qT, [lambda i, m=m: xn[:, i, m * 128:(m + 1) * 128] for m in range(2)], [t])
            t2 = transp(kT, [lambda i, m=m: xn[:, i, 256 + m * 128:256 + (m + 1) * 128] for m in range(2)], [t])
            for i in range(2):
                ts_ = slice(i * 128, i * 128 + 128)
                for m in range(2):
                    def qs(h):
                        return slice(32 * h, 32 * h + 32)
                    t = attend(i, lambda h: qT[qs(h), m, ts_], lambda h: kT[qs(h), m, :], None, 32 ** -0.5, [t1, t2], apart=True)
                    s4 = sm[:, 16:20].rearrange("p (h c) -> p h c", c=2)
                    t = V("ts", s4[:, :, 1], s4[:, :, 1], sm[:, 37:38], None, ALU.mult)
                    for h in range(2):
                        V("ts", sc_[:, h, :], pt[:, 2 * h + 1, :], sm[:, 17 + 2 * h:18 + 2 * h], None, ALU.mult)
                        t = V("stt", sc_[:, 2 + h, :], pt[:, 2 * h, :], sm[:, 16 + 2 * h:17 + 2 * h], sc_[:, h, :],
                              ALU.mult, ALU.add)
                    b, tm = weigh(lambda h: sc_[:, 2 + h, :], 2,
                                  lambda kt, h: proj[:, kt, 864 + (2 * m + h) * 64:928 + (2 * m + h) * 64], [t])
                    t = V("copy", mix[:, i, 256 + m * 128:384 + m * 128], ps[:, b, 0:128], w=[tm])
                    pb.put(b, 1, t)
            V("tt", rt[:, :, 0:256], mix[:, :, 256:512], mix[:, :, 256:512], ALU.mult)
            t = V("red", sm[:, 40:48], rt[:, :, 0:256].rearrange("p i (h d) -> p i h d", d=64), AX.X, ALU.add)
            t = rstd(sm[:, 48:56], sm[:, 40:48], 64, w=[t])
            V("ts", sm[:, 48:56], sm[:, 48:56], 1.0 - li, None, ALU.mult, w=[t])
            for i in range(2):
                mv = mix[:, i, 256:512].rearrange("p (h d) -> p h d", d=64)
                t = V("tt", mv, mv, bc(sm[:, 48 + 4 * i:52 + 4 * i], 2, 64), ALU.mult)
            t = rope(hd(xn[:, :, 0:384], 64), hd(proj[:, :, 1120:1504], 64), 6, 64)
            t1 = transp(qT, [lambda i, m=m: xn[:, i, m * 64:(m + 1) * 64] for m in range(4)], [t])
            t2 = transp(kT, [lambda i, m=m: xn[:, i, 256 + m * 64:256 + (m + 1) * 64] for m in range(2)], [t])
            swm = C("swa").rearrange("p (i n) -> p i n", i=2)
            for i in range(2):
                ts_ = slice(i * 128, i * 128 + 128)
                t = attend(i, lambda h: qT[0:64, h, ts_], lambda h: kT[0:64, h // 2, :], None, 0.125, [t1, t2],
                           bias_=lambda hh: bc(swm[:, i, :], 1, 2), sink_=PR(f"sink{l}"))
                b, tm = weigh(lambda h: pt[:, h, :], 4, lambda kt, h: proj[:, kt, 1504 + (h // 2) * 64:1568 + (h // 2) * 64], [t])
                t = heads_out(i, 512, b, tm)
            group_norm(512, [t])
            t1 = transp(qT, [lambda i, m=m: proj[:, i, 1632 + m * 64:1696 + m * 64] for m in range(4)], P)
            t2 = transp(kT, [lambda i, m=m: proj[:, i, 1888 + m * 64:1952 + m * 64] for m in range(4)], P)
            for i in range(2):
                ts_ = slice(i * 128, i * 128 + 128)
                t = attend(i, lambda h: qT[0:64, h, ts_], lambda h: kT[0:64, h, :], None, 0.125, [t1, t2],
                           bias_=lambda hh: na_bias(i, hh))
                b, tm = weigh(lambda h: pt[:, h, :], 4, lambda kt, h: proj[:, kt, 2144 + h * 64:2208 + h * 64], [t])
                t = heads_out(i, 768, b, tm)
            t = group_norm(768, [t])
            barrier()
            out_proj(mix, stage, PR(f"m2g{l}"), [t])
            barrier()

        def mlp_plan(l):
            wd = a["w_down_2"][l].rearrange("(f p) d -> p f d", p=128)
            for c in range(9):
                if c < 8:
                    cols_plan(a["w_up_2"][l], c * 512, 512)
                if c:
                    for f2 in (2 * c - 2, 2 * c - 1):
                        W.add(wd[:, 2 * f2:2 * f2 + 2, :], 2, 1024)

        def mlp(l):
            barrier()
            th = norm_T(carve(U_N, 8, 256), PR(f"n2{l}"))
            uT = [[ur[:, 2048 * q + 1024 * z:2048 * q + 1024 * z + 1024] for z in range(2)] for q in range(3)]
            stg = [carve(U_N + 2048 + 1024 * q, 1024) for q in range(2)]
            barrier()
            up_free, u_free, u_done, st_free = [None] * 2, [None] * 3, [None] * 3, [None] * 2
            for c in range(9):
                if c < 8:
                    _, tm = colsT(512, th, bank=(4 + 2 * (c % 2), [up_free[c % 2]]))
                    v = stg[c % 2]
                    for m in range(2):
                        t = A(v[:, 512 * m:512 * m + 512], ps[:, 4 + 2 * (c % 2) + m, :], ACT.Relu, w=[tm, st_free[c % 2]])
                    up_free[c % 2] = t
                    t = V("tt", v, v, v, ALU.mult, w=[t])
                    t = acopy(uT[c % 3][0], v, w=[t, u_free[c % 3]])
                    t = V("tt", uT[c % 3][1], v, uT[c % 3][0], ALU.subtract, w=[t])
                    u_done[c % 3] = st_free[c % 2] = t
                if c:
                    d = c - 1
                    uv = [v.rearrange("p (f n) -> p f n", f=4) for v in uT[d % 3]]
                    for f2 in range(2):
                        tile, tok, n = W.next()
                        for i in range(2):
                            for cc in range(2):
                                for f in range(2):
                                    pr = parts3([v[:, 2 * f2 + f, i * 128:(i + 1) * 128] for v in uv],
                                                [v[:, f, cc * 512:(cc + 1) * 512] for v in tile])
                                    for q, (l_, r_) in enumerate(pr):
                                        first = d == 0 and f2 == 0 and f == 0 and q == 0
                                        last = d == 7 and f2 == 1 and f == 1 and q == 2
                                        tm = mm1(ps[:, 2 * i + cc, :], l_, r_, first, last, w=[tok, u_done[d % 3]],
                                                 inc=(f == 1 and q == 2))
                        W.free(n, tm)
                    u_free[d % 3] = tm
            for i in range(2):
                for c in range(2):
                    residual(c, i, ps[:, 2 * i + c, :], tm)
            barrier()

        s_out = sem("s_out")

        def final(normed):
            barrier()
            t = DV.now()
            if normed:
                fin = carve(0, 1024)
                load(fin, a["final_norm_g_2"].partition_broadcast(128), t, PE.now())
                for i in range(2):
                    t = A(xn[:, i, :], x[:, i, :], ACT.Square, accum_out=st[:, i:i + 1], w=[t])
                t = rstd(st[:, 2:4], st[:, 0:2], 1024, w=[t])
                for i in range(2):
                    t = V("stt", xn[:, i, :], x[:, i, :], st[:, 2 + i:3 + i], fin, ALU.mult, ALU.mult, w=[t, (s_ld, n_ld)])
            src = xn if normed else x
            tok = SP.dma(lambda e: e.dma_start(out.rearrange("b (i p) d -> p (b i) d", p=128), src[:, :, :]), s_out, 16, t)
            SP.items.append(([tok], None, None, 0))

        for what, l in plan:
            if what == "mix1":
                ada_plan(l)
                mix1_plan(l)
            elif what == "moe":
                moe_plan(l)
            elif what == "mix2":
                mix2_plan(l)
            elif what == "mlp":
                mlp_plan(l)
        for what, l in plan:
            if what == "mix1":
                ada(l)
                mix1(l)
            elif what == "moe":
                moe(l)
            elif what == "mix2":
                mix2(l)
            elif what == "mlp":
                mlp(l)
        final(plan[-1][0] == "final")

        block = ctx.enter_context(nc.Block())

        @block.sync
        def _(eng):
            SP.replay(eng)

        @block.tensor
        def _(eng):
            PE.replay(eng)

        @block.vector
        def _(eng):
            DV.replay(eng)

        @block.scalar
        def _(eng):
            AC.replay(eng)

        @block.gpsimd
        def _(eng):
            PO.replay(eng)


def constants():
    c = {}
    p = np.arange(128)
    f = np.arange(128)
    c["ident"] = np.eye(128)
    c["tri"] = -(p[:, None] >= f[None, :]).astype(np.float32)
    c["neg1"] = -np.ones((128, 128))
    c["mneg"] = np.where(p[:, None] >= f[None, :], NEG, 0.0)
    c["keep"] = (p[:, None] < f[None, :])
    c["glam"] = (p[:, None] <= f[None, :]) & (p[:, None] // 64 == f[None, :] // 64)
    t = np.arange(256)
    c["swa"] = np.concatenate([np.where(np.abs(t[None, :] - (i * 128 + p[:, None])) <= 128, 0.0, NEG) for i in range(2)], 1)
    qc, kc = (p % 64)[:, None], np.arange(64)[None, :]
    lo = np.clip(qc - 8, 0, 48)
    c["nam"] = np.where((kc >= lo) & (kc < lo + 16), 0.0, NEG)
    for dim in (32, 64):
        inv = (1.0 / (np.float32(10000.0) ** (np.arange(0, dim, 2, dtype=np.float32) / np.float32(dim)))).astype(np.float32)
        ang = (t.astype(np.float32)[:, None] * inv[None, :]).astype(np.float32)
        for n, fn in (("cos", np.cos), ("sin", np.sin)):
            v = fn(ang).astype(np.float32)
            c[f"{n}{dim}"] = np.concatenate([v[0:128], v[128:256]], 1)
    c["reset"] = np.broadcast_to((t % 64 != 0), (128, 256))
    c["iota8"] = np.broadcast_to(np.arange(8), (128, 8))
    c["stri"] = (p[:, None] < f[None, :])
    c["slot"] = np.broadcast_to(np.arange(128) - 1e6, (128, 128))
    c["ones"] = np.ones((128, 128))
    return np.concatenate([np.asarray(c[n], np.float32) for n, _ in CONSTS], 1)


def params(a):
    z = {}

    def pk(v):
        return v.reshape(128, 8)

    def row(v, n=128):
        return np.broadcast_to(v.reshape(1, -1), (n, v.size))

    z["c"] = pk(a["c"][0])
    one = np.ones(512, np.float32)
    pad = np.zeros(64, np.float32)
    for l in range(2):
        z[f"nm{l}"], z[f"nf{l}"] = pk(a["norm_mix"][l]), pk(a["norm_ffn"][l])
        z[f"bgk{l}"] = a["b_gk"][l].reshape(2, 128).T
        z[f"qg{l}"] = np.tile(a["q_gain"][l], 2).reshape(128, 1)
        z[f"kg{l}"] = np.tile(a["k_gain"][l], 2).reshape(128, 1)
        z[f"mg{l}"] = pk(np.concatenate([one, np.tile(a["gla_gain"][l], 4)]))
        z[f"rb{l}"] = row(np.concatenate([a["b_router_grp"][l], a["b_router_exp"][l]]))
        z[f"rw{l}"] = np.concatenate([a["w_router_grp"][l], a["w_router_exp"][l]], 1).reshape(128, 288)
        z[f"gk2{l}"] = np.concatenate([a["w_gk2"][l], np.zeros((112, 256), np.float32)], 0)
        z[f"n1{l}"], z[f"n2{l}"] = pk(a["norm1_g_2"][l]), pk(a["norm2_g_2"][l])
        z[f"mq{l}"] = np.concatenate([a["mla_q_norm_g_2"][l], pad]).reshape(2, 128).T
        z[f"mkv{l}"] = a["mla_kv_norm_g_2"][l].reshape(128, 1)
        z[f"m2g{l}"] = pk(np.concatenate([a["out_g_mla_2"][l], np.tile(a["diff_subln_g_2"][l], 4), a["out_g_swa_2"][l],
                                          a["out_g_na_2"][l]]))
        z[f"sink{l}"] = row(a["swa_sinks_2"][l])
        z[f"lam{l}"] = row(np.concatenate([a[f"diff_lambda_{n}_2"][l] for n in ("q1", "k1", "q2", "k2")]))
    return np.ascontiguousarray(np.concatenate([z[n] for n, _ in PARAMS], 1))


PLAN = [("mix1", 0), ("moe", 0), ("mix1", 1), ("moe", 1), ("mix2", 0), ("mlp", 0), ("mix2", 1), ("mlp", 1), ("final", 0)]
_INS = ["x", "b_ada", "w_ada", "w_in", "w_out", "w_gate", "w_up", "w_down", "w_in_2", "mla_w_uq_2", "mla_w_uk_2",
        "mla_w_uv_2", "na_rpb_2", "w_out_2", "w_up_2", "w_down_2", "final_norm_g_2"]


def kernel(**inputs):
    import numpy as _np
    import concourse.bacc as _bacc
    from concourse import mybir as _mybir
    from concourse.bass_utils import run_bass_kernel_spmd as _run

    nc = _bacc.Bacc("TRN2", target_bir_lowering=False, num_devices=1)
    host = {n: _np.ascontiguousarray(inputs[n]) for n in _INS}
    host["na_rpb_2"] = _np.ascontiguousarray(host["na_rpb_2"][:, ::-1, ::-1, ::-1])
    host["cst"] = constants()
    host["prm"] = params({n: _np.asarray(v) for n, v in inputs.items()})
    arrays, aps = {}, {}
    for name, v in host.items():
        arrays[f"in_{name}"] = v
        aps[name] = nc.dram_tensor(f"in_{name}", v.shape, _mybir.dt.from_np(v.dtype), kind="ExternalInput").ap()
    aps["na_rpb"] = aps["na_rpb_2"]
    out = nc.dram_tensor("out_0", (1, 256, 1024), F32, kind="ExternalOutput").ap()
    program(nc, aps, out, PLAN)
    r = _run(nc, [arrays], core_ids=[0])
    return r.results[0]["out_0"]
```

```python
import math
from contextlib import ExitStack

import numpy as np
import concourse.bass as bass
from concourse import mybir

F32 = mybir.dt.float32
F32R = mybir.dt.float32r
U32 = mybir.dt.uint32
ALU = mybir.AluOpType
ACT = mybir.ActivationFunctionType
AX = mybir.AxisListType
EPS = 1e-6
NEG = -1e30
RING = 4
SPLIT = 3
CH = 2048
ORDER = {"mix1": "02221300112110412434132423441232243141134323124314241331324132412424412313",
         "mix1b": "012022304424340432422442342424333422433444334332322222334",
         "mix2": "010002030221330012030"}


def layout(parts):
    at, n = {}, 0
    for name, w in parts:
        at[name] = (n, w)
        n += w
    return at, n


CONSTS = [("ident", 128), ("tri", 128), ("neg1", 128), ("mneg", 128), ("keep", 128), ("glam", 128),
          ("swa", 512), ("nam", 64), ("cos32", 32), ("sin32", 32), ("cos64", 64), ("sin64", 64),
          ("reset", 256), ("iota8", 8), ("ones", 128), ("stri", 128), ("slot", 128)]
PARAMS = [("c", 8)]
for _l in range(2):
    PARAMS += [(f"nm{_l}", 8), (f"nf{_l}", 8), (f"bgk{_l}", 2), (f"qg{_l}", 1), (f"kg{_l}", 1), (f"mg{_l}", 8),
               (f"rb{_l}", 36), (f"rw{_l}", 288), (f"gk2{_l}", 256), (f"bm{_l}", 48)]
for _l in range(2):
    PARAMS += [(f"n1{_l}", 8), (f"n2{_l}", 8), (f"mq{_l}", 2), (f"mkv{_l}", 1), (f"m2g{_l}", 8), (f"sink{_l}", 4),
               (f"lam{_l}", 128)]
C_AT, C_N = layout(CONSTS)
P_AT, P_N = layout(PARAMS)


class Eng:

    def __init__(self, sem):
        self.sem, self.n, self.items = sem, 0, []

    def op(self, fn, *waits, inc=True, chain=True):
        w = [t for t in waits if t is not None]
        if chain and self.n:
            w.append((self.sem, self.n))
        if inc:
            self.n += 1
        self.items.append((w, fn, self.sem if inc else None, 1))
        return (self.sem, self.n)

    def dma(self, fn, sem, value, *waits):
        self.items.append(([t for t in waits if t is not None], fn, sem, 16))
        return (sem, value)

    def begin(self, sem):
        self.outer = (self.items, self.n, self.sem)
        self.items, self.n, self.sem = [], 0, sem

    def end(self, flag, wait, at=None):
        body = self.items
        self.items, self.n, self.sem = self.outer
        item = ("if", flag, wait, body)
        if at is None:
            self.items.append(item)
        else:
            self.items[at] = item

    def now(self):
        return (self.sem, self.n) if self.n else None

    def replay(self, eng, items=None):
        seen = {}
        for waits, fn, sem, by in self.items if items is None else items:
            if waits == "if":
                flag, wait, body = fn, sem, by
                eng.wait_ge(*wait)
                seen[wait[0]] = max(seen.get(wait[0], 0), wait[1])
                with eng.If(eng.value_load(flag, min_val=0, max_val=1) > 0):
                    self.replay(eng, body)
                continue
            for t in waits:
                s, v = t() if callable(t) else t
                if seen.get(s, 0) < v:
                    eng.wait_ge(s, v)
                    seen[s] = v
            if fn is None:
                continue
            ins = fn(eng)
            if sem is not None:
                ins.then_inc(sem, by)


def program(nc, a, out, plan):
    ctx = ExitStack()
    with ctx:
        base = (nc.sbuf_base + 63) // 64 * 64
        top = [base]
        ctx.enter_context(nc.sbuf_tensor("fence", [128, (nc.sbuf_usable_end - base) // 4 - 32], F32))

        def sb(name, shape, dt=F32, at=None):
            if at is None:
                at = top[0]
                top[0] += (int(np.prod(shape[1:])) * 4 + 31) // 32 * 32
                assert top[0] <= nc.sbuf_usable_end
            return nc.alloc_sbuf_tensor_at(name, shape, dt, offset=at)

        def sem(name):
            return ctx.enter_context(nc.semaphore(name))

        ring = sb("ring", [128, RING, CH])
        x = sb("x", [128, 2, 1024])
        xn = sb("xn", [128, 2, 1024])
        hh = sb("hh", [128, 2, 2048], F32R)
        hw = sb("hw", [128, 4096], at=top[0] - 4096 * 4)
        spl = sb("spl", [128, SPLIT, 2, CH], F32R)
        sw = sb("sw", [128, SPLIT * 2 * CH], at=top[0] - SPLIT * 2 * CH * 4)
        cst = sb("cst", [128, C_N])
        prm = sb("prm", [128, P_N])
        gate = sb("gate", [128, 2, 1024])
        modc = sb("modc", [128, 6, 8])
        aff = sb("aff", [128, 4, 8])
        st = sb("st", [128, 416])
        cact = sb("cact", [128, 24])
        ccol = sb("ccol", [128, 8, 32])
        dg = sb("dg", [128, 2, 128])
        ixt = sb("ixt", [128, 2, 8], U32)
        flags = sb("flags", [128, 2, 2], mybir.dt.int32)
        U_N = 9216
        A_N = (nc.sbuf_usable_end - top[0]) // 128 * 32
        ur = sb("ur", [128, U_N], F32R, at=top[0])
        ar = sb("ar", [128, A_N], F32, at=top[0])
        hT = tuple(hh[:, q, :].rearrange("p (k n) -> p k n", k=8) for q in range(2))
        ps = ctx.enter_context(nc.psum_tensor("ps", [128, 8, 512], F32))

        PE, DV, AC, PO, SP = (Eng(sem(f"e_{n}")) for n in ("pe", "dve", "act", "pool", "sp"))
        ENG = (PE, DV, AC, PO)

        def C(name):
            o, w = C_AT[name]
            return cst[:, o:o + w]

        def PR(name, rows=128):
            o, w = P_AT[name]
            return prm[0:rows, o:o + w]

        ident = C("ident")

        def carve(off, *dims, of=ar):
            n = int(np.prod(dims))
            assert off + n <= of.shape[1], (off, n, of.shape)
            v = of[:, off:off + n]
            if len(dims) == 2:
                return v.rearrange("p (a b) -> p a b", b=dims[1])
            if len(dims) == 3:
                return v.rearrange("p (a b c) -> p a b c", b=dims[1], c=dims[2])
            if len(dims) == 4:
                return v.rearrange("p (a b c d) -> p a b c d", b=dims[1], c=dims[2], d=dims[3])
            return v

        def bc(ap, axis, n):
            v = ap.unsqueeze(axis)
            shape = list(v.shape)
            shape[axis] = n
            return v.to_broadcast(shape)

        def V(name, *args, w=(), **kw):
            return DV.op(lambda e: getter(e, name)(*args, **kw), *w)

        table = {}

        def getter(e, name):
            return table[name](e)

        table.update({
            "copy": lambda e: e.tensor_copy, "tt": lambda e: e.tensor_tensor, "ts": lambda e: e.tensor_scalar,
            "stt": lambda e: e.scalar_tensor_tensor, "red": lambda e: e.tensor_reduce,
            "scan": lambda e: e.tensor_tensor_scan, "recip": lambda e: e.reciprocal, "memset": lambda e: e.memset,
            "cpred": lambda e: e.copy_predicated, "max": lambda e: e.max, "maxidx": lambda e: e.max_index,
        })

        def G(name, *args, w=(), **kw):
            return PO.op(lambda e: getter(e, name)(*args, **kw), *w)

        def A(out_, in_, func, w=(), **kw):
            return AC.op(lambda e: e.activation(out_, in_, func, **kw), *w)

        def acopy(out_, in_, w=()):
            return AC.op(lambda e: e.activation(out_, in_, ACT.Copy), *w)

        def mm(out_, pairs, w=()):
            t, n = None, len(pairs)
            for i, (l, r) in enumerate(pairs):
                t = PE.op(lambda e, l=l, r=r, i=i: e.matmul(out_, l, r, start=(i == 0), stop=(i == n - 1)),
                          *(w if i == 0 else ()), inc=(i == n - 1), chain=False)
            return t

        def mm1(out_, l, r, start, stop, w=(), inc=False):
            return PE.op(lambda e: e.matmul(out_, l, r, start=start, stop=stop, skip_group_check=True), *w,
                         inc=inc, chain=False)

        def parts3(l, r):
            return [(l[0], r[0]), (l[0], r[1]), (l[1], r[0])]

        def tr(out_, in_, w=(), inc=True):
            k = in_.shape[0]
            return PE.op(lambda e: e.transpose(out_, in_, ident[0:k, 0:k]), *w, inc=inc, chain=False)

        class Banks:
            def __init__(self, lo=0, hi=8):
                self.lo, self.hi, self.at, self.freed = lo, hi, lo, [[] for _ in range(8)]

            def get(self, n=1):
                if self.at + n > self.hi:
                    self.at = self.lo
                b = self.at
                self.at += n
                w = [t for i in range(b, b + n) for t in self.freed[i]]
                for i in range(b, b + n):
                    self.freed[i] = None
                return b, w

            def put(self, b, n, *tokens):
                for i in range(b, b + n):
                    self.freed[i] = [t for t in tokens if t is not None]

        pb = Banks()

        class Stream:
            def __init__(self):
                self.sems = [sem(f"w{i}") for i in range(RING)]
                self.plan, self.raw_free, self.toks, self.tiles = [], [], [], []
                self.at = self.ready = 0
                self.hold, self.end, self.came = True, 1 << 30, [0] * RING
                self.spl_free, self.n_spl, self.spl_of = [()] * SPLIT, 0, {}

            def add(self, src, *dims, parts=128, split=True):
                n, slot = len(self.plan), len(self.plan) % RING
                size = int(np.prod(dims))
                tile = ring[0:parts, slot, 0:size]
                self.plan.append((tile, dims, split, parts, size))
                self.raw_free.append(None)
                v = tile.rearrange("p (a b) -> p a b", b=dims[1]) if len(dims) == 2 else tile
                waits = [lambda: self.raw_free[n - RING]] if n >= RING else []
                self.came[slot] += 16
                self.toks.append(SP.dma(lambda e: e.dma_start(v, src), self.sems[slot], self.came[slot], *waits))

            def add_many(self, *srcs):
                n, slot, c = len(self.plan), len(self.plan) % RING, 0
                waits = [lambda: self.raw_free[n - RING]] if n >= RING else []
                views = []
                for src in srcs:
                    p, w = src.shape
                    v = ring[0:p, slot, c:c + w]
                    c += w
                    self.came[slot] += 16
                    tok = SP.dma(lambda e, v=v, src=src: e.dma_start(v, src), self.sems[slot], self.came[slot], *waits)
                    views.append(v)
                self.plan.append((views, (), False, 0, 0))
                self.raw_free.append(None)
                self.toks.append(tok)

            def prepare(self):
                while self.ready < len(self.plan) and self.ready < self.at + SPLIT:
                    n = self.ready
                    tile, dims, split, parts, size = self.plan[n]

                    def shaped(v):
                        return v.rearrange("p (a b) -> p a b", b=dims[1]) if len(dims) == 2 else v

                    if split:
                        if self.hold or n >= self.end:
                            return
                        s = self.n_spl % SPLIT
                        if self.spl_free[s] is None:
                            return
                        self.n_spl += 1
                        self.spl_of[n] = s
                        hi, lo = spl[0:parts, s, 0, 0:size], spl[0:parts, s, 1, 0:size]
                        t = AC.op(lambda e, hi=hi, tile=tile: e.activation(hi, tile, ACT.Copy), self.toks[n], *self.spl_free[s], chain=False)
                        t = DV.op(lambda e, hi=hi, lo=lo, tile=tile: e.tensor_tensor(lo, tile, hi, ALU.subtract), t, chain=False)
                        self.spl_free[s] = None
                        self.raw_free[n] = t
                        self.tiles.append(((shaped(hi), shaped(lo)), t))
                    else:
                        self.tiles.append((shaped(tile), self.toks[n]))
                    self.ready += 1

            def ahead(self, k):
                self.hold, self.end = False, self.at + k
                self.prepare()

            def release(self):
                self.hold, self.end = False, 1 << 30
                self.prepare()

            def next(self):
                n = self.at
                self.at += 1
                self.prepare()
                return (*self.tiles[n], n)

            def free(self, n, tok):
                if n in self.spl_of:
                    self.spl_free[self.spl_of[n]] = (tok,)
                else:
                    self.raw_free[n] = tok
                self.prepare()

        W = Stream()

        def barrier():
            toks = [e.now() for e in ENG]
            for e in ENG:
                e.items.append(([t for t in toks if t is not None], None, None, 0))
            pb.freed = [[] for _ in range(8)]
            pb.at = 0

        def merge(gens, order=""):
            live = dict(enumerate(gens))

            def step(q):
                try:
                    next(live[q])
                except StopIteration:
                    del live[q]

            for q in order:
                if int(q) in live:
                    step(int(q))
            while live:
                for q in list(live):
                    step(q)

        def lanes(order, *gens):
            toks = [PE.now(), AC.now(), DV.now(), PO.now()]
            for e in ENG:
                e.items.append((toks, None, None, 0))
            W.hold = True
            merge(gens, order)
            barrier()

        s_ld = sem("s_ld")
        n_ld = 0

        def load(dst, src, *waits):
            nonlocal n_ld
            n_ld += 16
            SP.dma(lambda e: e.dma_start(dst, src), s_ld, n_ld, *waits)

        load(cst[:, :], a["cst"])
        load(prm[:, :], a["prm"])
        load(x[:, :, :], a["x"].rearrange("b (i p) d -> p (b i) d", p=128))
        LD = (s_ld, n_ld)
        for e in ENG:
            e.items.append(([LD], None, None, 0))
        mh = st[:, 128:160]
        G("memset", mh, -0.5)

        def rstd(dst, ss, dim, w=()):
            n = dst.shape[-1]
            G("ts", dst, ss, 1.0 / dim, EPS, ALU.mult, ALU.add, w=w)
            return G("tt", dst, dst, mh[:, 0:n], ALU.pow)

        sq_tok = {}

        def square(i, c, t):
            h = slice(c * 512, c * 512 + 512)
            sq_tok[i, c] = A(xn[:, i, h], x[:, i, h], ACT.Square, accum_out=st[:, 4 + 2 * i + c:5 + 2 * i + c], w=[t])

        def row_rstd(i):
            G("tt", st[:, i:i + 1], st[:, 4 + 2 * i:5 + 2 * i], st[:, 5 + 2 * i:6 + 2 * i], ALU.add, w=[sq_tok[i, 0], sq_tok[i, 1]])
            return rstd(st[:, 2 + i:3 + i], st[:, i:i + 1], 1024)

        def norm():
            t = [row_rstd(i) for i in range(2)]
            for i in range(2):
                tn = V("ts", xn[:, i, :], x[:, i, :], st[:, 2 + i:3 + i], None, ALU.mult, w=[t[i]])
            return tn

        def norm_T(stage, gain, shift=None, w=()):
            t = [row_rstd(i) for i in range(2)]
            t = [V("ts", dg[:, i, :], ident, st[:, 2 + i:3 + i], None, ALU.mult, w=[t[i]]) for i in range(2)]
            W.ahead(1)
            return to_T(x, stage, gain, shift, w, diag=t)

        def split2(hi, lo, src, w):
            t = acopy(hi, src, w=w)
            return V("tt", lo, src, hi, ALU.subtract, w=[t])

        def to_T(src, stage, gain, shift, w, split=True, diag=None):
            toks, each = [], []
            for k2 in range(4):
                b, bw = pb.get()
                for kk in range(2):
                    for i in range(2):
                        o, v = ps[:, b, kk * 256 + i * 128:kk * 256 + i * 128 + 128], src[:, i, 2 * k2 + kk::8]
                        t = mm(o, [(v, dg[:, i, :])], w=[diag[i], *w, *bw]) if diag else tr(o, v, w=[*w, *bw])
                for kk in range(2):
                    k = 2 * k2 + kk
                    o = ps[:, b, kk * 256:kk * 256 + 256]
                    if not split and kk:
                        u = V("ts", stage[:, k, :], o, gain[:, k:k + 1], shift[:, k:k + 1], ALU.mult, ALU.add, w=[t, u])
                        each += [[u]] * 2
                        continue
                    u = A(stage[:, k, :], o, ACT.Identity, scale=gain[:, k:k + 1],
                          **({} if shift is None else {"bias": shift[:, k:k + 1]}), w=[t])
                pb.put(b, 1, u)
                if split:
                    ks = slice(2 * k2, 2 * k2 + 2)
                    u = V("copy", hT[0][:, ks, :], stage[:, ks, :], w=[u])
                    u = V("tt", hT[1][:, ks, :], stage[:, ks, :], hT[0][:, ks, :], ALU.subtract)
                toks.append(u)
                if split and k2 == 0:
                    W.ahead(1)
            if split:
                W.release()
            return toks if split else each

        def rows(wap, c0, cn, k0, kn):
            return wap[:, c0:c0 + cn].rearrange("(p k) n -> p k n", k=8)[:, k0:k0 + kn, :]

        def cols(cn, w, sink, last=False):
            b, bw = pb.get(2)
            done = [None] * 2
            if last:
                W.end = min(W.end, W.at + 2)
            for half in range(2):
                tile, tok, n = W.next()
                for i in range(2):
                    for k in range(4):
                        kk = 4 * half + k
                        pr = parts3([v[:, kk, i * 128:(i + 1) * 128] for v in hT], [v[:, k, :] for v in tile])
                        for q, (l, r) in enumerate(pr):
                            t = mm1(ps[:, b + i, 0:cn], l, r, kk == 0 and q == 0, kk == 7 and q == 2,
                                    w=[tok, w[kk // 2], *bw], inc=(k == 3 and q == 2))
                    done[i] = t
                if half:
                    used = [sink(i, ps[:, b + i, 0:cn], done[i]) for i in range(2)]
                W.hold = W.hold or (last and half == 1)
                W.free(n, t)
            pb.put(b, 2, *used)
            return used

        def colsT(cn, w, bank=None):
            nb = cn // 256
            b, bw = pb.get(nb) if bank is None else bank
            t = None
            for half in range(2):
                tile, tok, n = W.next()
                for m in range(cn // 128):
                    for k in range(4):
                        kk = 4 * half + k
                        pr = parts3([v[:, k, m * 128:(m + 1) * 128] for v in tile], [v[:, kk, :] for v in hT])
                        for q, (l, r) in enumerate(pr):
                            t = mm1(ps[:, b + m // 2, (m % 2) * 256:(m % 2) * 256 + 256], l, r,
                                    kk == 0 and q == 0 and m % 2 == 0, kk == 7 and q == 2,
                                    w=[tok, w[kk // 2], *bw], inc=(k == 3 and q == 2))
                W.free(n, t)
            return b, t

        cc = PR("c")
        t = A(cact[:, 0:8], cc, ACT.Exp, scale=-1.0)
        V("ts", cact[:, 8:16], cact[:, 0:8], 1.0, None, ALU.add, w=[t])
        V("recip", cact[:, 8:16], cact[:, 8:16])
        CACT = V("tt", cact[:, 16:24], cact[:, 8:16], cc, ALU.mult)
        V("memset", ccol[:, :, :], 0.0)
        CACT = V("copy", ccol[:, :, 0:1], cact[:, 16:24].unsqueeze(2))
        s_gb = sem("s_gb")

        def ada_plan(l, blocks):
            for c in blocks:
                for half in range(2):
                    W.add(rows(a["w_ada"][l], c * 512, 512, 4 * half, 4), 4, 512, split=False)

        def gate_bias(l):
            w = DV.now()
            for g, s in ((0, 2), (1, 5)):
                t = AC.dma(lambda e, g=g, s=s: e.dma_start(
                    gate[:, g, :], a["b_ada"][l, s * 1024:(s + 1) * 1024].partition_broadcast(128)),
                    s_gb, 32 * l + 16 * g + 16, w)
            return (s_gb, 32 * l + 32)

        ada_free = {}

        def ada(l, blocks, bank, tb=None):
            ev = carve(A_N - 1024, 2, 512)
            for c in blocks:
                q, (s, h) = c % 2, divmod(c, 2)
                for half in range(2):
                    tile, tok, n = W.next()
                    for k in range(4):
                        t = mm1(ps[32 * k:32 * k + 32, bank, :], ccol[:, 4 * half + k, :], tile[:, k, :], half == 0, half == 1,
                                w=[tok, CACT, ada_free.get(bank)], inc=(k == 3))
                    W.free(n, t)
                yield
                t = acopy(ev[:, q, :], ps[:, bank, :], w=[t])
                yield
                if s in (2, 5):
                    t = mm(ps[:, bank, :], [(C("ones"), ev[:, q, :])], w=[t])
                    yield
                    gs = gate[:, s // 3, h * 512:h * 512 + 512]
                    ada_free[bank] = V("tt", gs, gs, ps[:, bank, :], ALU.add, w=[t, tb])
                    continue
                hp = slice(64 * h, 64 * h + 64)
                for k in range(8):
                    tm = mm(ps[hp, bank, k:k + 1], [(ev[:, q, k::8], C("ones")[:, 0:1])], w=[t])
                yield
                bm = PR(f"bm{l}")[hp, 8 * s:8 * s + 8]
                d = {0: 1, 1: 0, 3: 3, 4: 2}[s]
                o = aff[hp, d, :] if d % 2 else modc[hp, s, :]
                ada_free[bank] = V("tt", o, ps[hp, bank, 0:8], bm, ALU.add, w=[tm])
                if d % 2 == 0:
                    V("stt", aff[hp, d, :], o, 1.0, PR(f"nf{l}" if d else f"nm{l}")[hp, :], ALU.add, ALU.mult)

        def residual(c, i, p, t, g=None):
            xs = x[:, i, c * 512:(c + 1) * 512]
            if g is None:
                t1 = V("tt", xs, xs, p, ALU.add, w=[t])
                square(i, c, t1)
                return t1
            tmp = xn[:, i, c * 512:(c + 1) * 512]
            t1 = V("tt", tmp, p, gate[:, g, c * 512:(c + 1) * 512], ALU.mult, w=[t])
            square(i, c, V("tt", xs, xs, tmp, ALU.add))
            return t1

        def cols_plan(wap, c0, cn):
            for half in range(2):
                W.add(rows(wap, c0, cn, 4 * half, 4), 4, cn)

        def out_proj(mix, stage, gain, w, g=None):
            tt = to_T(mix, stage, gain, None, w)
            for c in range(2):
                cols(512, tt, lambda i, p, t, c=c: residual(c, i, p, t, g), c == 1)

        def mix1_plan(l):
            win = a["w_in"][l]
            if l == 0:
                ada_plan(0, range(4))
            W.add(rows(win, 3072, 16, 0, 8), 8, 16, split=False)
            for c in (0, 512, 1536, 1024, 2048, 2560):
                cols_plan(win, c, 512)
            ada_plan(l, range(4, 12))
            if l == 0:
                ada_plan(1, range(4))
            for c in range(2):
                cols_plan(a["w_out"][l], c * 512, 512)

        def mix1(l):
            barrier()
            proj = carve(0, 2, 2560)
            gqT = carve(5120, 2, 256)
            gkT = carve(5632, 2, 256)
            mix = xn
            qkT = carve(6400, 8, 256)
            stage = carve(8448, 8, 256)
            tb = gate_bias(l)
            if l == 0:
                merge([ada(0, (q, q + 2), q) for q in range(2)])
            th = norm_T(stage, aff[:, 0, :], aff[:, 1, :], [DV.now()])

            def sink(c):
                return lambda i, p, t: (acopy if i else lambda o, s, w: V("copy", o, s, w=w))(
                    proj[:, i, c * 512:(c + 1) * 512], p, w=[t])

            tile, tok, n = W.next()
            b, bw = pb.get()
            tm = mm(ps[0:16, b, 0:256], [(tile[:, k, :], stage[:, k, :]) for k in range(8)], w=[tok, *th, *bw])
            W.free(n, tm)
            lrT = carve(6144, 256)[0:16, :]
            t = acopy(lrT, ps[0:16, b, 0:256], w=[tm])
            pb.put(b, 1, t)
            u, lg, bb, eb, enb, ekd = (carve(12544 + 512 * q, 512) for q in range(6))
            qd, ki, kd = lg, u, ekd
            b, bw = pb.get()
            for f in range(2):
                tm = mm(ps[:, b, f * 256:f * 256 + 256], [(PR(f"gk2{l}", 16)[:, f * 128:(f + 1) * 128], lrT)], w=[t, *bw])
            for f in range(2):
                t = V("ts", u[:, f * 256:f * 256 + 256], ps[:, b, f * 256:f * 256 + 256], PR(f"bgk{l}")[:, f:f + 1], None,
                      ALU.add, w=[tm])
            pb.put(b, 1, t)
            t = A(bb, u, ACT.Abs, w=[t])
            t = A(eb, bb, ACT.Exp, scale=-1.0)
            t = A(enb, eb, ACT.Ln, bias=1.0)
            cols(512, th, sink(0))
            t = V("stt", lg, u, 0.0, enb, ALU.min, ALU.subtract, w=[t])
            for f in range(2):
                t = V("scan", bb[:, f * 256:f * 256 + 256], C("reset"), lg[:, f * 256:f * 256 + 256], 0.0, ALU.mult, ALU.add)
            A(eb, bb, ACT.Exp, scale=1 / 16, w=[t])
            t_e = A(enb, bb, ACT.Exp, scale=-1 / 16)
            b4 = bb.rearrange("p (c s) -> p c s", s=64)
            t = V("tt", u.rearrange("p (c s) -> p c s", s=64), b4[:, :, 63:64].to_broadcast([128, 8, 64]), b4, ALU.subtract)
            t_k = A(ekd, u, ACT.Exp, scale=1 / 16, w=[t])
            t = cols(512, th, sink(1))
            sq = carve(8448, 2, 1024)
            t = A(sq, proj[:, :, 0:1024], ACT.Square, w=[*t, *th])
            b, tm = colsT(512, th)
            t1 = acopy(gqT, ps[:, b, :].rearrange("p (a b) -> p a b", b=256), w=[tm])
            t2 = V("copy", gkT, ps[:, b + 1, :].rearrange("p (a b) -> p a b", b=256), w=[tm])
            pb.put(b, 2, t1, t2)
            t = V("red", st[:, 0:32], sq.rearrange("p i (h d) -> p (i h) d", d=64), AX.X, ALU.add, w=[t])
            t_n = rstd(st[:, 32:64], st[:, 0:32], 64, w=[t])
            gq = gqT.rearrange("p a b -> p (a b)")
            gk = gkT.rearrange("p a b -> p (a b)")
            V("stt", qd, gq, 0.125, eb, ALU.mult, ALU.mult, w=[t1, t_e])
            V("tt", ki, gk, enb, ALU.mult, w=[t_k])
            V("tt", kd, gk, ekd, ALU.mult)
            cols(512, th, sink(2))
            for i in range(2):
                V("tt", xn[:, i, :].rearrange("p (h d) -> p h d", d=64),
                  proj[:, i, 0:1024].rearrange("p (h d) -> p h d", d=64),
                  bc(st[:, 32 + 16 * i:48 + 16 * i], 2, 64), ALU.mult, w=[t_n])
            for c in range(3, 5):
                cols(512, th, sink(c))

            def stick():
                bk = Banks(0, 4)
                for c in (0, 2, 1, 3):
                    b, bw = bk.get()
                    for m in range(2):
                        for i in range(2):
                            tm = tr(ps[:, b, m * 256 + i * 128:m * 256 + i * 128 + 128],
                                    xn[:, i, (2 * c + m) * 128:(2 * c + m + 1) * 128], w=bw)
                    o = qkT[:, 2 * c:2 * c + 2, :]
                    s = ps[:, b, :].rearrange("p (a b) -> p a b", b=256)
                    if c < 2:
                        tv = V("ts", o, s, PR(f"qg{l}"), 0.125, ALU.mult, ALU.mult, w=[tm])
                    else:
                        tv = V("ts", o, s, PR(f"kg{l}"), None, ALU.mult, w=[tm])
                    bk.put(b, 1, tv)
                    tq.append(tv)
                    yield
                xn_read.append(tm)

            def heads(lane):
                while not xn_read:
                    yield
                b = 2 * lane
                ab, sp = (carve(8448 + 1536 * lane + 768 * q, 2, 384) for q in range(2))
                free = None
                for g in (lane, lane + 2):
                    def scores(j):
                        pr, ct = slice(64 * j, 64 * j + 64), g
                        kk, qq = qkT[pr, 4 + ct, :], qkT[pr, ct, :]
                        return ((ps[:, b + j, 0:256], kk[:, 0:128], qq), (ps[:, b + j, 256:384], kk[:, 128:256], qq[:, 128:256]))

                    for j in range(2):
                        for o, ll, rr in scores(j):
                            tm = mm(o, [(ll, rr)], w=[*tq, free])
                    yield
                    z = ps[:, b:b + 2, 0:384]
                    t = A(ab, z, ACT.Abs, w=[tm])
                    t = A(ab, ab, ACT.Exp, scale=-1.0)
                    yield
                    t = A(ab, ab, ACT.Ln, bias=1.0)
                    yield
                    t = V("stt", sp, z, 0.0, ab, ALU.max, ALU.add, w=[t])
                    s3 = sp.rearrange("p j (c n) -> p j c n", n=128)[:, :, 0::2, :]
                    t = V("tt", s3, s3, bc(bc(C("keep"), 1, 2), 1, 2), ALU.mult)
                    yield
                    for j in range(2):
                        (o0, l0, r0), (o1, l1, r1) = scores(j)
                        mm1(o0, l0, r0, True, False, w=[t])
                        mm1(o0, C("tri"), sp[:, j, 0:256], False, False)
                        mm1(o0[:, 128:256], C("neg1"), sp[:, j, 256:384], False, False)
                        mm1(o0[:, 0:128], ident, C("mneg"), False, True)
                        mm1(o1, l1, r1, True, False)
                        mm1(o1, C("tri"), sp[:, j, 256:384], False, False)
                        tm = mm1(o1, ident, C("mneg"), False, True, inc=True)
                    yield
                    t = A(ab, z, ACT.Exp, w=[tm])
                    yield
                    for j in range(2):
                        vc = slice(1024 + (2 * g + j) * 64, 1024 + (2 * g + j) * 64 + 64)
                        mm(ps[:, b, j * 64:j * 64 + 64], [(ab[:, j, 0:128], proj[:, 0, vc])], w=[t])
                        tm = mm(ps[:, b, 128 + j * 64:128 + j * 64 + 64],
                                [(ab[:, j, 128:256], proj[:, 0, vc]), (ab[:, j, 256:384], proj[:, 1, vc])])
                    yield
                    free = V("copy", mix[:, :, g * 128:(g + 1) * 128],
                             ps[:, b, 0:256].rearrange("p (a b) -> p a b", b=128), w=[tm])
                    yield

            def gla():
                bk = Banks(4, 7)
                qde, qdo, kdt = (carve(512 * (9 + q), 2, 256, of=sw) for q in range(3))
                state = carve(6144, 2, 4, 128, of=sw)
                sm = carve(7168, 8, 128, of=sw)
                o, sg, s2 = (carve(8192 + 1024 * q, 2, 512, of=sw) for q in range(3))
                G("memset", qde, 0.0)
                G("memset", qdo, 0.0)
                tz = G("memset", sm, 0.0)
                tg = A(sg, proj[:, :, 2048:2560], ACT.Silu)
                qd4 = qd.rearrange("p (f c e s) -> p f c e s", f=2, c=2, e=2)
                for e, dst in ((0, qde), (1, qdo)):
                    tqd = V("copy", dst.rearrange("p f (c e s) -> p f c e s", c=2, e=2)[:, :, :, e, :], qd4[:, :, :, e, :], w=[tz])
                yield
                b, bw = bk.get()
                for i in range(2):
                    for f in range(2):
                        tm = tr(ps[:, b, i * 256 + f * 128:i * 256 + f * 128 + 128],
                                kd[:, f * 256 + i * 128:f * 256 + i * 128 + 128], w=bw)
                yield
                tk = acopy(kdt, ps[:, b, :].rearrange("p (a b) -> p a b", b=256), w=[tm])
                bk.put(b, 1, tk)
                yield
                for c in range(3):
                    pr = slice((c % 2) * 64, (c % 2) * 64 + 64)
                    b, bw = bk.get()
                    for f in range(2):
                        tm = mm(ps[:, b, f * 256:f * 256 + 256],
                                [(kdt[pr, c // 2, f * 128:(f + 1) * 128], proj[pr, c // 2, 1536 + f * 256:1536 + f * 256 + 256])],
                                w=[tk, *bw])
                    yield
                    for f in range(2):
                        for hh in range(2):
                            pr = slice(hh * 64, hh * 64 + 64)
                            so = state[pr, f, c + 1, :]
                            kv = ps[pr, b, f * 256 + hh * 128:f * 256 + hh * 128 + 128]
                            if c == 0:
                                ts = V("copy", so, kv, w=[tm])
                            else:
                                ts = V("stt", so, state[pr, f, c, :], eb[pr, f * 256 + c * 64 + 63:f * 256 + c * 64 + 64], kv,
                                       ALU.mult, ALU.add, w=[tm])
                    bk.put(b, 1, ts)
                yield
                b, bw = bk.get(2)
                for i in range(2):
                    for h in range(4):
                        pr, f = slice((h % 2) * 64, (h % 2) * 64 + 64), h // 2
                        cs = slice(f * 256 + i * 128, f * 256 + i * 128 + 128)
                        tm = mm(ps[:, b + h % 2, i * 256 + f * 128:i * 256 + f * 128 + 128], [(ki[pr, cs], qd[pr, cs])],
                                w=[tqd, *bw])
                yield
                gm = bc(C("glam"), 1, 4).bitcast(U32)
                for i in range(2):
                    t = V("cpred", sm[:, 4 * i:4 * i + 4, :], gm, ps[:, b + i, :].rearrange("p (a b) -> p a b", b=128), w=[tm])
                bk.put(b, 2, t)
                yield
                for i in range(2):
                    b, bw = bk.get(2)
                    for h in range(4):
                        pr, f = slice((h % 2) * 64, (h % 2) * 64 + 64), h // 2
                        cs = slice(i * 128, i * 128 + 128)
                        pairs = [(sm[:, 4 * (h % 2) + 2 * i + f, :], proj[:, i, 1536 + h * 128:1536 + h * 128 + 128])]
                        if i:
                            pairs.append((qde[pr, f, cs], state[pr, f, 2, :]))
                        pairs.append((qdo[pr, f, cs], state[pr, f, 2 * i + 1, :]))
                        tm = mm(ps[:, b + h % 2, f * 128:f * 128 + 128], pairs, w=[t, ts, *bw])
                    yield
                    t = V("copy", o[:, i, :].rearrange("p (f e d) -> p e f d", f=2, e=2),
                          ps[:, b:b + 2, 0:256].rearrange("p e (f d) -> p e f d", d=128), w=[tm])
                    bk.put(b, 2, t)
                    yield
                V("tt", s2, o, o, ALU.mult)
                t = V("red", st[:, 64:72], s2.rearrange("p i (h d) -> p (i h) d", d=128), AX.X, ALU.add)
                t1 = rstd(st[:, 72:80], st[:, 64:72], 128, w=[t])
                yield
                V("tt", o.rearrange("p i (h d) -> p (i h) d", d=128), o.rearrange("p i (h d) -> p (i h) d", d=128),
                  bc(st[:, 72:80], 2, 128), ALU.mult, w=[t1])
                V("tt", mix[:, :, 512:1024], o, sg, ALU.mult, w=[tg, *xn_read])

            xn_read, tq = [], []
            more = [ada(l, range(4, 12), 7, tb)]
            if l == 0:
                more.append(ada(1, range(4), 7))

            def chained(gens):
                for g in gens:
                    yield from g

            ad = chained(more)
            lanes(ORDER["mix1b" if l else "mix1"], stick(), ad, gla(), heads(0), heads(1))
            out_proj(mix, carve(6400, 8, 256), PR(f"mg{l}"), [], 0)
            barrier()

        over_at = []

        def moe_plan(l):
            wg, wu, wd = (a[k][l].rearrange("g e a b -> (g e) a b") for k in ("w_gate", "w_up", "w_down"))
            for e in range(33):
                if e < 32:
                    W.add(wg[e].rearrange("(p k) f -> p k f", k=8), 8, 256)
                    W.add(wu[e].rearrange("(p k) f -> p k f", k=8), 8, 256)
                if e:
                    W.add(wd[e - 1].rearrange("(p k) d -> p k d", k=2), 2, 1024)
            over_at.append(len(SP.items))
            SP.items.append(None)


        def overflow(l, totals, w):
            v = carve(U_N + 3568, 16)
            V("ts", v[:, 0:4], totals, 128.5, None, ALU.is_gt, w=w)
            V("tt", v[:, 4:8], v[:, 0:4], C("iota8")[:, 0:4], ALU.mult)
            V("red", v[:, 8:10], v[:, 0:8].rearrange("p (a b) -> p a b", b=4), AX.X, ALU.add)
            return V("copy", flags[:, l, :], v[:, 8:10])

        def rest(l, flag_tok, pos, ew):
            barrier()
            waits = [e.now() for e in ENG]
            order = (PE, DV, AC, PO, SP)
            for e, n in zip(order, ("pe", "dve", "act", "pool", "sp")):
                e.begin(sem(f"r{l}_{n}"))
            s_w = [sem(f"r{l}_w{q}") for q in range(3)]
            x5, p5, p5T = carve(0, 2, 1024), carve(2048, 2, 128), carve(2304, 256)
            xg, combs = carve(2624, 8, 128), carve(2560, 8)
            wb = [carve(3712 + 2048 * q, 2048) for q in range(3)]
            sl, hs, aT, ys = carve(9920, 256), carve(10176, 256), carve(10432, 2, 128), carve(0, 1024)
            pos5 = carve(2576, 2, 4)
            t = V("ts", pos5, pos, -128.0, None, ALU.add)
            for i in range(2):
                V("ts", x5[:, i, :], x[:, i, :], st[:, 2 + i:3 + i], None, ALU.mult)
                V("ts", p5[:, i, :], C("slot"), pos5[:, i, 0:1], None, ALU.is_equal)
                for g in range(1, 4):
                    t = V("stt", p5[:, i, :], C("slot"), pos5[:, i, g:g + 1], p5[:, i, :], ALU.is_equal, ALU.add)
            for k in range(8):
                tm = mm(ps[:, k // 4, 128 * (k % 4):128 * (k % 4) + 128],
                        [(x5[:, i, k::8], p5[:, i, :]) for i in range(2)], w=[t])
            tm = mm(ps[:, 2, 0:8], [(p5[:, i, :], ew[:, i, :]) for i in range(2)], w=[t])
            for i in range(2):
                tm = tr(ps[:, 3, 128 * i:128 * i + 128], p5[:, i, :], w=[t])
            for k in range(8):
                A(xg[:, k, :], ps[:, k // 4, 128 * (k % 4):128 * (k % 4) + 128], ACT.Identity,
                  scale=aff[:, 2, k:k + 1], bias=aff[:, 3, k:k + 1], w=[tm])
            acopy(combs, ps[:, 2, 0:8])
            tx = acopy(p5T, ps[:, 3, 0:256])
            wv = [a["w_gate"][l], a["w_up"][l], a["w_down"][l]]
            down, group = None, []
            for e in range(8):
                def source(eng, q, e):
                    if not group:
                        group.append(eng.value_load(flags[0:1, l, 1:2], min_val=0, max_val=3))
                    v = wv[q][bass.ds(group[0], 1), e, :, :].rearrange("o a b -> (o a) b")
                    return v.rearrange("(p k) f -> p (k f)", p=128)

                toks = []
                for q in range(3):
                    toks.append(SP.dma(lambda eng, q=q, e=e: eng.dma_start(wb[q], source(eng, q, e)), s_w[q], 16 * (e + 1),
                                       *(waits if e == 0 else [down])))
                for q in range(2):
                    wt = wb[q].rearrange("p (k f) -> p k f", k=8)
                    tm = mm(ps[:, 4, 256 * q:256 * q + 256], [(xg[:, k, :], wt[:, k, :]) for k in range(8)], w=[toks[q], tx])
                t = A(sl, ps[:, 4, 0:256], ACT.Silu, w=[tm])
                t = V("stt", hs, ps[:, 4, 256:512], combs[:, e:e + 1], sl, ALU.mult, ALU.mult, w=[t])
                for f in range(2):
                    tm = tr(ps[:, 5, 128 * f:128 * f + 128], hs[:, f::2], w=[t])
                t = acopy(aT, ps[:, 5, 0:256].rearrange("p (f n) -> p f n", f=2), w=[tm])
                wt = wb[2].rearrange("p (k f) -> p k f", k=2)
                for c in range(2):
                    for f in range(2):
                        down = mm1(ps[:, 6 + c, :], aT[:, f, :], wt[:, f, 512 * c:512 * c + 512], e == 0 and f == 0,
                                   e == 7 and f == 1, w=[toks[2], t], inc=(f == 1))
                tx = down
            t = acopy(ys, ps[:, 6:8, :].rearrange("p c n -> p (c n)"), w=[down])
            for i in range(2):
                for c in range(2):
                    tm = mm(ps[:, 2 * i + c, :], [(p5T[:, 128 * i:128 * i + 128], ys[:, 512 * c:512 * c + 512])], w=[t])
            for i in range(2):
                for c in range(2):
                    o = xn[:, i, 512 * c:512 * c + 512]
                    t = V("tt", o, o, ps[:, 2 * i + c, :], ALU.add, w=[tm])
            DV.items.append(([t], None, None, 0))
            for e in order:
                e.end(flags[0:1, l, 0:1], flag_tok, over_at.pop(0) if e is SP else None)
            pb.freed = [[] for _ in range(8)]

        def moe(l):
            barrier()
            S = U_N
            stage = carve(S, 8, 256)
            P = carve(S + 2048, 2, 512)
            lgt = carve(S + 3072, 2, 36)
            lT = carve(S + 3200, 256)[0:36, :]
            g8, m8, sel, ew, oh1, oh2 = (carve(S + 3456 + 16 * q, 2, 8) for q in range(6))
            tmp = carve(S + 3584, 2, 32)
            ohg, pos, et, sc = (carve(S + 3648 + 8 * q, 2, 4) for q in range(4))
            w12 = carve(S + 3680, 8, 2)
            combs = carve(S + 3712, 4, 8)
            gst = [carve(S + 3776 + 512 * q, 512) for q in range(2)]
            sl = [carve(S + 4800 + 256 * q, 256) for q in range(2)]
            hs = [carve(S + 5312 + 256 * q, 256) for q in range(2)]
            xg = [ur[:, 4096 * q:4096 * q + 4096].rearrange("p (k n) -> p k n", k=8) for q in range(2)]
            pr_ = ur[:, 8192:9216].rearrange("p (i n) -> p i n", i=2)
            xs = [hh[:, q, :].rearrange("p (i n) -> p i n", i=2) for q in range(2)]
            t = norm()
            W.ahead(1)
            th = to_T(xn, stage, aff[:, 2, :], aff[:, 3, :], [t], split=False)
            V("copy", hh[:, 0, :], xn[:, :, :].rearrange("p i n -> p (i n)"), w=[t])
            rw = PR(f"rw{l}").rearrange("p (k n) -> p k n", k=8)
            V("memset", g8, -3e38)
            b, bw = pb.get()
            for k in range(8):
                tm = mm1(ps[0:36, b, 0:256], rw[:, k, :], stage[:, k, :], k == 0, k == 7, w=[*th[k], *bw], inc=(k == 7))
            t = acopy(lT, ps[0:36, b, 0:256], w=[tm])
            pb.put(b, 1, t)
            b, bw = pb.get()
            for i in range(2):
                tm = tr(ps[:, b, i * 36:i * 36 + 36], lT[:, i * 128:(i + 1) * 128], w=[t, *bw])
            t = V("tt", lgt, ps[:, b, 0:72].rearrange("p (i n) -> p i n", i=2), bc(PR(f"rb{l}"), 1, 2), ALU.add, w=[tm])
            pb.put(b, 1, t)

            def top(v):
                for i in range(2):
                    V("max", m8[:, i, :], v[:, i, :])
                    V("maxidx", ixt[:, i, :], m8[:, i, :], v[:, i, :])
                return V("copy", et8, ixt[:, :, :])

            et8 = carve(S + 3552, 2, 8)
            V("copy", g8[:, :, 0:4], lgt[:, :, 0:4])
            top(g8)
            tohg = V("tt", ohg, bc(C("iota8")[:, 0:4], 1, 2), et8[:, :, 0:1].to_broadcast([128, 2, 4]), ALU.is_equal)
            b, bw = pb.get()
            o = ps[:, b, 0:12].rearrange("p (i n) -> p i n", n=4)
            mm(o[:, 0, :], [(C("stri"), ohg[:, 0, :])], w=[tohg, *bw])
            mm(o[:, 1, :], [(C("stri"), ohg[:, 1, :]), (C("ones"), ohg[:, 0, :])])
            tm = mm(o[:, 2, :], [(C("ones"), ohg[:, 0, :]), (C("ones"), ohg[:, 1, :])])
            t = V("tt", et, lgt[:, :, 0:4], m8[:, :, 0:1].to_broadcast([128, 2, 4]), ALU.subtract)
            tet = A(et, et, ACT.Exp, w=[t])
            txs = V("tt", hh[:, 1, :], xn[:, :, :].rearrange("p i n -> p (i n)"), hh[:, 0, :], ALU.subtract)
            V("stt", pos.rearrange("p i g -> p (i g)"), ohg.rearrange("p i g -> p (i g)"), -1e6, ps[:, b, 0:8],
              ALU.mult, ALU.add, w=[tm])

            def places(v):
                return V("tt", v.rearrange("p i (g s) -> p (i g) s", s=128), bc(C("slot"), 1, 8),
                         bc(pos.rearrange("p i g -> p (i g)"), 2, 128), ALU.is_equal)

            tpr = places(pr_)
            tot = carve(S + 3696, 4)
            t = V("copy", tot, o[:, 2, :])
            pb.put(b, 1, t)
            pT = hh[:, 0, 0:1024].rearrange("p (g n) -> p g n", g=4)
            ys = [hh[:, 1, 1024 * z:1024 * z + 1024] for z in range(2)]
            aT = [[hh[:, 0, 1024 + 512 * q + 256 * z:1280 + 512 * q + 256 * z].rearrange("p (f n) -> p f n", f=2)
                   for z in range(2)] for q in range(2)]
            tpT = []
            flag = []

            def gather():
                bk = Banks(4, 8)
                tx = [None] * 2
                for k in range(8):
                    b, bw = bk.get()
                    for q, (i, z) in enumerate(((0, 0), (0, 1), (1, 0), (1, 1))):
                        tm = mm1(ps[:, b, :], xs[z][:, i, k::8], pr_[:, i, :], q == 0, q == 3, w=[tpr, txs, *bw], inc=(q == 3))
                    yield
                    g = gst[k % 2]
                    t = A(g, ps[:, b, :], ACT.Identity, scale=aff[:, 2, k:k + 1], bias=aff[:, 3, k:k + 1], w=[tm, tx[k % 2]])
                    bk.put(b, 1, t)
                    t = acopy(xg[0][:, k, :], g)
                    tx[k % 2] = V("tt", xg[1][:, k, :], g, xg[0][:, k, :], ALU.subtract, w=[t])
                    done.append(tx[k % 2])
                x_read.append(tm)

            done, x_read, tP = [], [], []

            def weights():
                tP.append(places(P))
                yield
                V("red", sc[:, :, 0:1].rearrange("p i o -> p (i o)"), et, AX.X, ALU.add, w=[tet])
                V("recip", sc[:, :, 1], sc[:, :, 0])
                t4 = tmp.rearrange("p i (g e) -> p i g e", e=8)
                yield
                V("tt", t4, lgt[:, :, 4:36].rearrange("p i (g e) -> p i g e", e=8), bc(ohg, 3, 8), ALU.mult)
                V("red", sel, tmp.rearrange("p i (g e) -> p i e g", e=8), AX.X, ALU.add)
                yield
                top(sel)
                yield
                V("tt", oh1, bc(C("iota8"), 1, 2), et8[:, :, 0:1].to_broadcast([128, 2, 8]), ALU.is_equal)
                V("tt", oh2, bc(C("iota8"), 1, 2), et8[:, :, 1:2].to_broadcast([128, 2, 8]), ALU.is_equal)
                t = V("tt", w12[:, 0, :], m8[:, :, 1], m8[:, :, 0], ALU.subtract)
                t = A(w12[:, 1, :], w12[:, 0, :], ACT.Exp, w=[t])
                yield
                V("ts", w12[:, 2, :], w12[:, 1, :], 1.0, None, ALU.add, w=[t])
                V("recip", w12[:, 3, :], w12[:, 2, :])
                V("tt", w12[:, 4, :], w12[:, 3, :], sc[:, :, 1], ALU.mult)
                V("tt", w12[:, 5, :], w12[:, 4, :], w12[:, 1, :], ALU.mult)
                yield
                V("tt", oh1, oh1, bc(w12[:, 4, :], 2, 8), ALU.mult)
                V("tt", oh2, oh2, bc(w12[:, 5, :], 2, 8), ALU.mult)
                tP.append(V("tt", ew, oh1, oh2, ALU.add))
                yield
                flag.append(overflow(l, tot, []))

            PE.items.append(([AC.now(), DV.now()], None, None, 0))
            pb.freed = [[] for _ in range(8)]
            pb.at = 0
            merge([gather(), weights()])
            W.release()
            for g2 in range(2):
                for gg in range(2):
                    for i in range(2):
                        g = 2 * g2 + gg
                        t = tr(ps[:, 1 + 2 * g2, 256 * gg + 128 * i:256 * gg + 128 * i + 128], P[:, i, 128 * g:128 * g + 128],
                               w=tP[0:1])
                t = acopy(pT[:, 2 * g2:2 * g2 + 2, :], ps[:, 1 + 2 * g2, :].rearrange("p (g n) -> p g n", g=2), w=[t, *x_read])
                tpT.append(t)
            for g in range(4):
                tm = mm(ps[:, 0, 8 * g:8 * g + 8], [(P[:, i, 128 * g:128 * g + 128], ew[:, i, :]) for i in range(2)], w=tP)
            cs = V("copy", combs.rearrange("p g e -> p (g e)"), ps[:, 0, 0:32], w=[tm])
            gu_free, h_done, tr_done, aT_done = [None, tpT[1]], [None] * 2, [None] * 2, [None] * 2
            aT_free, y_free, ys_free, sc_free = [None] * 2, None, None, [None] * 2

            def turn(e):
                q = e % 2
                for f in range(2):
                    t = tr(ps[:, 4 + q, 128 * f:128 * f + 128], hs[q][:, f::2], w=[h_done[q], aT_done[q]])
                tr_done[q] = t
                src = ps[:, 4 + q, 0:256].rearrange("p (f n) -> p f n", f=2)
                t = AC.op(lambda eng: eng.activation(aT[q][0], src, ACT.Copy), t, aT_free[q], chain=False)
                aT_done[q] = DV.op(lambda eng: eng.tensor_tensor(aT[q][1], src, aT[q][0], ALU.subtract), t, chain=False)

            def back(g, t, i):
                for c in range(2):
                    for z in range(2):
                        tm = mm1(ps[:, 6 + c, :], pT[:, g, 128 * i:128 * i + 128], ys[z][:, 512 * c:512 * c + 512],
                                 z == 0, z == 1, w=[t, *tpT, sc_free[c]], inc=(z == 1))
                    o = xn[:, i, 512 * c:512 * c + 512]
                    if g == 0:
                        sc_free[c] = V("copy", o, ps[:, 6 + c, :], w=[tm])
                    else:
                        sc_free[c] = V("tt", o, o, ps[:, 6 + c, :], ALU.add, w=[tm])
                return tm

            pending = []
            for e in range(33):
                q, g = e % 2, e // 8
                if e < 32:
                    for z in range(2):
                        tile, tok, n = W.next()
                        for k in range(8):
                            pr = parts3([v[:, k, 128 * g:128 * g + 128] for v in xg], [v[:, k, :] for v in tile])
                            for j, (l_, r_) in enumerate(pr):
                                tm = mm1(ps[:, 2 + q, 256 * z:256 * z + 256], l_, r_, k == 0 and j == 0 and z == 0,
                                         k == 7 and j == 2, w=[tok, gu_free[q], *done], inc=(k == 7 and j == 2))
                        if z:
                            t = AC.op(lambda eng, q=q: eng.activation(sl[q], ps[:, 2 + q, 0:256], ACT.Silu), tm, h_done[q],
                                      chain=False)
                            h_done[q] = gu_free[q] = DV.op(
                                lambda eng, q=q, g=g, e=e: eng.scalar_tensor_tensor(
                                    out=hs[q], in0=ps[:, 2 + q, 256:512], scalar=combs[:, g, e % 8:e % 8 + 1], in1=sl[q],
                                    op0=ALU.mult, op1=ALU.mult), t, tr_done[q], cs, chain=False)
                        W.free(n, tm)
                if pending:
                    ys_free = back(*pending.pop(0))
                n = None
                if e:
                    d, p = e - 1, (e - 1) % 2
                    tile, tok, n = W.next()
                    for c in range(2):
                        for f in range(2):
                            pr = parts3([v[:, f, :] for v in aT[p]], [v[:, f, 512 * c:512 * c + 512] for v in tile])
                            for j, (l_, r_) in enumerate(pr):
                                td = mm1(ps[:, c, :], l_, r_, d % 8 == 0 and f == 0 and j == 0,
                                         d % 8 == 7 and f == 1 and j == 2, w=[tok, aT_done[p], y_free],
                                         inc=(f == 1 and j == 2))
                    aT_free[p] = td
                if e < 32:
                    turn(e)
                if e and d % 8 == 7:
                    yv = ps[:, 0:2, :].rearrange("p c n -> p (c n)")
                    t = acopy(ys[0], yv, w=[td, ys_free])
                    t = y_free = V("tt", ys[1], yv, ys[0], ALU.subtract, w=[t])
                    pending = [(d // 8, t, i) for i in range(2)]
                W.hold = e == 32
                if n is not None:
                    W.free(n, td)
            for p in pending:
                back(*p)
            rest(l, flag[0], pos, ew)
            gv = gate[:, 1, :]
            for i in range(2):
                for c in range(2):
                    h = slice(512 * c, 512 * c + 512)
                    V("tt", xn[:, i, h], xn[:, i, h], gv[:, h], ALU.mult)
                    square(i, c, V("tt", x[:, i, h], x[:, i, h], xn[:, i, h], ALU.add))
            barrier()

        s_na = sem("s_na")
        n_na = [0]

        def mix2_plan(l):
            for c in range(5):
                cols_plan(a["w_in_2"][l], c * 480, 480)
                if c == 3:
                    uq = a["mla_w_uq_2"][l]
                    W.add_many(uq[0:128, :], uq[128:192, :], a["mla_w_uk_2"][l], a["mla_w_uv_2"][l])
            for c in range(2):
                cols_plan(a["w_out_2"][l], c * 512, 512)

        def mix2(l):
            barrier()
            proj = carve(0, 2, 2400)
            q3 = carve(4800, 2, 1152)
            naT = carve(7104, 4, 6, 64)
            mix = carve(8640, 2, 1024)
            stage = carve(10688, 8, 256)
            rp = a["na_rpb"][l]
            toks = None
            for s in range(2):
                for h in range(4):
                    src = bass.AP(rp.tensor, rp.offset + 76 + 31 * s + 465 * h, [[1, 64], [31, 6], [1, 64]])
                    n_na[0] += 16
                    toks = AC.dma(lambda e, s=s, h=h, src=src: e.dma_start(naT[64 * s:64 * s + 64, h, :, :], src),
                                  s_na, n_na[0])
            th = norm_T(stage, PR(f"n1{l}"))
            class Lane:

                def __init__(self, n, qk, pt, ptT, tmp):
                    self.bk, self.sm = Banks(2 * n, 2 * n + 2), st[:, 160 + 56 * n:216 + 56 * n]
                    (self.qT, self.kT), self.pt, self.ptT, self.tmp = qk, pt, ptT, tmp

            def hd(ap, d):
                return ap.rearrange("p i (h d) -> p i h d", d=d)

            def na_bias(i, hh):
                v = naT[:, 2 - 2 * hh:4 - 2 * hh, :, :].rearrange("p h r c -> p h (r c)")
                return v[:, ::-1, 128 * i:128 * i + 256][:, :, ::-1]

            def rope(L, dst, src, heads, dim, E=V, w=()):
                hf = dim // 2
                cs, sn = (bc(C(f"{n}{dim}").rearrange("p (i d) -> p i d", i=2), 2, heads) for n in ("cos", "sin"))
                x1, x2 = src[:, :, :, 0:hf], src[:, :, :, hf:dim]
                r1, r2, r3, r4 = (L.tmp(q, heads * hf).rearrange("p i (h d) -> p i h d", d=hf) for q in range(4))
                E("tt", r1, x1, cs, ALU.mult, w=w)
                E("tt", r2, x2, sn, ALU.mult)
                E("tt", r3, x2, cs, ALU.mult)
                E("tt", r4, x1, sn, ALU.mult)
                yield
                E("tt", dst[:, :, :, 0:hf], r1, r2, ALU.subtract)
                L.t = E("tt", dst[:, :, :, hf:dim], r3, r4, ALU.add)
                yield

            LL = Lane(0, (carve(0, 4, 256, of=sw), carve(1024, 4, 256, of=sw)), carve(2048, 4, 256, of=sw),
                      carve(3072, 4, 2, 128, of=sw), lambda q, n: carve(15296 + 128 * q, 2, n))
            LD_ = Lane(1, (carve(0, 2, 256, of=hw), carve(512, 2, 256, of=hw)), carve(1024, 4, 256, of=hw),
                       carve(2048, 2, 2, 128, of=hw), lambda q, n: carve(15296 + 512 * q, 2, n))
            LW = Lane(2, (carve(11456, 4, 256), carve(12480, 2, 256)), carve(12992, 4, 256), carve(14016, 4, 2, 128),
                      lambda q, n: carve(12992 + 384 * q, 2, n))
            xc, rq = xn[:, :, 512:864], carve(10688, 2, 384)
            kv = q3[:, :, 640:1024].rearrange("p i (h d) -> p i h d", d=96)
            lam_i = 0.8 - 0.6 * math.exp(-0.3 * l)
            for h in range(4):
                G("tt", naT[:, h, :, :], naT[:, h, :, :], bc(C("nam")[:, ::-1], 1, 6), ALU.add, w=[toks])
            for c in range(5):
                def sink(i, p, t, c=c):
                    o = proj[:, i, c * 480:(c + 1) * 480]
                    return acopy(o, p, w=[t]) if i else V("copy", o, p, w=[t])
                u = cols(480, th, sink)
                if c == 0:
                    sq, sm = carve(4800, 2, 320), LL.sm
                    V("tt", sq, proj[:, :, 0:320], proj[:, :, 0:320], ALU.mult, w=u)
                    V("red", sm[:, 24:26], sq[:, :, 0:192], AX.X, ALU.add)
                    t = V("red", sm[:, 26:28], sq[:, :, 192:320], AX.X, ALU.add)
                    rstd(sm[:, 28:30], sm[:, 24:26], 192, w=[t])
                    t_n = rstd(sm[:, 30:32], sm[:, 26:28], 128)
                    for _ in rope(LW, hd(xc[:, :, 320:352], 32), hd(proj[:, :, 320:352], 32), 1, 32, E=G, w=[*u, th[-1]]):
                        pass
                    t_pe = LW.t
                    sm, lv, tl = LD_.sm, PR(f"lam{l}"), carve(15168, 64)
                    V("tt", tl[:, 0:32], lv[:, 0:32], lv[:, 32:64], ALU.mult)
                    V("tt", tl[:, 32:64], lv[:, 64:96], lv[:, 96:128], ALU.mult)
                    t = V("red", sm[:, 32:34], tl.rearrange("p (a b) -> p a b", b=32), AX.X, ALU.add)
                    t_l = A(sm[:, 34:36], sm[:, 32:34], ACT.Exp, w=[t])
                elif c == 1:
                    for _ in rope(LD_, hd(xn[:, :, 0:512], 32), hd(proj[:, :, 352:864], 32), 16, 32, E=G, w=u):
                        pass
                    sm = LL.sm
                    V("tt", xc[:, :, 0:192], proj[:, :, 0:192], bc(sm[:, 28:30], 2, 192), ALU.mult, w=[t_n])
                    t_c = V("tt", xc[:, :, 192:320], proj[:, :, 192:320], bc(sm[:, 30:32], 2, 128), ALU.mult)
                    for i in range(2):
                        V("copy", kv[:, i, :, 64:96], bc(xc[:, i, 320:352], 1, 4), w=[t_pe])
                    sm = LD_.sm
                    V("tt", sm[:, 36:37], sm[:, 35:36], sm[:, 34:35], ALU.subtract, w=[t_l])
                    V("ts", sm[:, 37:38], sm[:, 36:37], -lam_i, None, ALU.add)
                elif c == 2:
                    cT, ckT = carve(8640, 2, 256), carve(9152, 256)
                    b, bw = pb.get(2)
                    for i in range(2):
                        for m, (o, wd_) in enumerate(((0, 128), (128, 64), (192, 128))):
                            tm = tr(ps[0:wd_, b + m // 2, (m % 2) * 256 + i * 128:(m % 2) * 256 + i * 128 + 128],
                                    xc[:, i, o:o + wd_], w=[t_c, *bw])
                    V("ts", cT[:, 0, :], ps[:, b, 0:256], PR(f"mq{l}")[:, 0:1], None, ALU.mult, w=[tm])
                    V("ts", cT[0:64, 1, :], ps[0:64, b, 256:512], PR(f"mq{l}", 64)[:, 1:2], None, ALU.mult)
                    t_c = V("ts", ckT, ps[:, b + 1, 0:256], PR(f"mkv{l}"), None, ALU.mult)
                    pb.put(b, 2, t_c)
                elif c == 3:
                    for _ in rope(LW, hd(rq, 64), hd(proj[:, :, 1120:1504], 64), 6, 64, E=G, w=u):
                        pass
                    W.end = W.at + 3
                    (w0, w1, w2, w3), tok, n = W.next()
                    for i in range(2):
                        ts_ = slice(i * 128, i * 128 + 128)
                        b, bw = pb.get(2)
                        mm(ps[:, b, 0:384], [(cT[:, 0, ts_], w0), (cT[0:64, 1, ts_], w1)], w=[t_c, tok, *bw])
                        mm(ps[:, b + 1, 0:256], [(ckT[:, ts_], w2)])
                        tm = mm(ps[:, b + 1, 256:512], [(ckT[:, ts_], w3)])
                        V("copy", q3[:, i, 0:384], ps[:, b, 0:384], w=[tm])
                        t = acopy(q3[:, i, 384:640], ps[:, b + 1, 256:512], w=[tm])
                        t = V("copy", q3[:, i, 640:1024].rearrange("p (h d) -> p h d", d=96)[:, :, 0:64],
                              ps[:, b + 1, 0:256].rearrange("p (h d) -> p h d", d=64), w=[t])
                        pb.put(b, 2, t)
                    W.free(n, tm)
                    qv = q3[:, :, 0:384].rearrange("p i (h d) -> p i h d", d=96)
                    for _ in rope(LL, qv[:, :, :, 64:96], qv[:, :, :, 64:96], 4, 32, w=[LD_.t]):
                        pass

            def transp(L, dst, srcs, w):
                for m0 in range(0, len(srcs), 2):
                    b, bw = L.bk.get()
                    n = srcs[m0](0).shape[-1]
                    grp = srcs[m0:m0 + 2]
                    for m, s in enumerate(grp):
                        for i in range(2):
                            tm = tr(ps[0:n, b, m * 256 + i * 128:m * 256 + i * 128 + 128], s(i), w=[*w, *bw])
                    yield
                    L.t = acopy(dst[0:n, m0:m0 + len(grp), :],
                                ps[0:n, b, 0:256 * len(grp)].rearrange("p (a b) -> p a b", b=256), w=[tm])
                    L.bk.put(b, 1, L.t)

            def attend(L, q, k, scale, w, bias_=None, sink_=None, apart=False):
                sm, pt = L.sm, L.pt
                b, bw = L.bk.get(2)
                done = []
                for h in range(4):
                    o = b + (h % 2 if apart else h // 2), 256 * (h // 2 if apart else h % 2)
                    done.append(mm(ps[:, o[0], o[1]:o[1] + 256], [(q(h), k(h))],
                                   w=[*w, *bw, *([done[h - 2]] if apart and h > 1 else [])]))
                s = ps[:, b:b + 2, :].rearrange("p a (e n) -> p e a n" if apart else "p a (e n) -> p a e n", n=256)
                tm = done[-1]
                yield
                if bias_ is not None:
                    for hh in range(2):
                        V("stt", pt[:, 2 * hh:2 * hh + 2, :], s[:, hh, :, :], scale, bias_(hh), ALU.mult, ALU.add, w=[tm])
                    s, f = pt.rearrange("p (a e) n -> p a e n", e=2), 1.0
                else:
                    f = scale
                V("red", sm[:, 0:4].rearrange("p (a e) -> p a e", e=2), s, AX.X, ALU.max, w=[tm])
                if sink_ is not None:
                    V("tt", sm[:, 0:4], sm[:, 0:4], sink_, ALU.max)
                t = V("ts", sm[:, 0:4], sm[:, 0:4], -f, None, ALU.mult)
                yield
                if sink_ is not None:
                    t = V("tt", sm[:, 8:12], sink_, sm[:, 0:4], ALU.add)
                    A(sm[:, 12:16], sm[:, 8:12], ACT.Exp, w=[t])
                for h in range(4):
                    t = A(pt[:, h, :], s[:, h // 2, h % 2, :], ACT.Exp, bias=sm[:, h:h + 1], scale=f,
                          accum_out=sm[:, 4 + h:5 + h], w=[t])
                L.bk.put(b, 2, t)
                yield
                if sink_ is not None:
                    t = V("tt", sm[:, 4:8], sm[:, 4:8], sm[:, 12:16], ALU.add, w=[t])
                L.t = V("recip", sm[:, 16:20], sm[:, 4:8], w=[t])

            def weigh(L, p4, n, v, w):
                toks = []
                for h0 in range(0, n, 2):
                    b, bw = L.bk.get()
                    for h in range(h0, h0 + 2):
                        for kt in range(2):
                            tm = tr(ps[:, b, (h - h0) * 256 + kt * 128:(h - h0) * 256 + kt * 128 + 128],
                                    p4(h)[:, kt * 128:(kt + 1) * 128], w=[*w, *bw])
                    o = L.ptT[:, h0:h0 + 2, :, :].rearrange("p a b c -> p (a b c)")
                    yield
                    t = V("copy", o, ps[:, b, :], w=[tm]) if h0 else acopy(o, ps[:, b, :], w=[tm])
                    L.bk.put(b, 1, t)
                    toks.append(t)
                yield
                b, bw = L.bk.get()
                for h in range(n):
                    tm = mm(ps[:, b, h * 64:h * 64 + 64], [(L.ptT[:, h, kt, :], v(kt, h)) for kt in range(2)], w=[*toks, *bw])
                yield
                L.o = b, tm

            def heads_out(L, i, c0):
                b, tm = L.o
                L.t = V("tt", mix[:, i, c0:c0 + 256].rearrange("p (h d) -> p h d", d=64),
                        ps[:, b, 0:256].rearrange("p (h d) -> p h d", d=64), bc(L.sm[:, 16:20], 2, 64), ALU.mult, w=[tm])
                L.bk.put(b, 1, L.t)

            def group_norm(L, c0):
                sm, m = L.sm, mix[:, :, c0:c0 + 256]
                sq = L.pt.rearrange("p a b -> p (a b)")[:, 0:512].rearrange("p (i n) -> p i n", i=2)
                V("tt", sq, m, m, ALU.mult)
                t = V("red", sm[:, 20:22], sq, AX.X, ALU.add)
                yield
                t = rstd(sm[:, 22:24], sm[:, 20:22], 256, w=[t])
                yield
                V("tt", m, m, bc(sm[:, 22:24], 2, 256), ALU.mult, w=[t])

            def tile_of(i):
                return slice(i * 128, i * 128 + 128)

            def latent():
                L = LL
                yield from transp(L, L.qT, [lambda i, h=h: q3[:, i, h * 96:h * 96 + 96] for h in range(4)], [])
                yield from transp(L, L.kT, [lambda i, h=h: q3[:, i, 640 + h * 96:736 + h * 96] for h in range(4)], [])
                yield
                for i in range(2):
                    ts_ = tile_of(i)
                    yield from attend(L, lambda h: L.qT[0:96, h, ts_], lambda h: L.kT[0:96, h, :], 96 ** -0.5, [L.t])
                    yield from weigh(L, lambda h: L.pt[:, h, :], 4, lambda kt, h: q3[:, kt, 384 + h * 64:448 + h * 64], [L.t])
                    heads_out(L, i, 0)
                    yield
                yield from group_norm(L, 0)

            def differential():
                L = LD_
                yield from transp(L, L.qT, [lambda i, m=m: xn[:, i, m * 128:(m + 1) * 128] for m in range(2)], [])
                yield from transp(L, L.kT, [lambda i, m=m: xn[:, i, 256 + m * 128:256 + (m + 1) * 128] for m in range(2)], [])
                yield
                D.update(qT=L.qT, kT=L.kT, lam=L.sm[:, 37:38], t=L.t)
                yield from maps(L, 0, carve(2560, 4, 256, of=hw))

            D = {}

            def maps(L, m, wd_):
                sm = L.sm
                while not D:
                    yield
                L.t = D["t"]
                for i in range(2):
                    ts_ = tile_of(i)

                    def qs(h):
                        return slice(32 * h, 32 * h + 32)
                    yield from attend(L, lambda h: D["qT"][qs(h), m, ts_], lambda h: D["kT"][qs(h), m, :], 32 ** -0.5, [L.t],
                                      apart=True)
                    s4 = sm[:, 16:20].rearrange("p (h c) -> p h c", c=2)
                    V("ts", s4[:, :, 1], s4[:, :, 1], D["lam"], None, ALU.mult)
                    for h in range(2):
                        V("ts", wd_[:, h, :], L.pt[:, 2 * h + 1, :], sm[:, 17 + 2 * h:18 + 2 * h], None, ALU.mult)
                        t = V("stt", wd_[:, 2 + h, :], L.pt[:, 2 * h, :], sm[:, 16 + 2 * h:17 + 2 * h], wd_[:, h, :],
                              ALU.mult, ALU.add)
                    yield
                    yield from weigh(L, lambda h: wd_[:, 2 + h, :], 2,
                                     lambda kt, h: proj[:, kt, 864 + (2 * m + h) * 64:928 + (2 * m + h) * 64], [t])
                    b, tm = L.o
                    mv = mix[:, i, 256 + m * 128:384 + m * 128]
                    L.t = V("copy", mv, ps[:, b, 0:128], w=[tm])
                    L.bk.put(b, 1, L.t)
                    yield
                li = 0.8 - 0.6 * math.exp(-0.3 * l)
                mv = mix[:, :, 256 + m * 128:384 + m * 128]
                sq = wd_[:, 0, :].rearrange("p (i n) -> p i n", i=2)
                V("tt", sq, mv, mv, ALU.mult)
                t = V("red", sm[:, 40:44], sq.rearrange("p i (h d) -> p i h d", d=64), AX.X, ALU.add)
                yield
                t = rstd(sm[:, 48:52], sm[:, 40:44], 64, w=[t])
                yield
                V("ts", sm[:, 48:52], sm[:, 48:52], 1.0 - li, None, ALU.mult, w=[t])
                for i in range(2):
                    mh_ = mv[:, i, :].rearrange("p (h d) -> p h d", d=64)
                    V("tt", mh_, mh_, bc(sm[:, 48 + 2 * i:50 + 2 * i], 2, 64), ALU.mult)

            def window():
                L = LW
                yield from transp(L, L.qT, [lambda i, m=m: rq[:, i, m * 64:(m + 1) * 64] for m in range(4)], [])
                yield from transp(L, L.kT, [lambda i, m=m: rq[:, i, 256 + m * 64:256 + (m + 1) * 64] for m in range(2)], [])
                yield
                swm = C("swa").rearrange("p (i n) -> p i n", i=2)
                for i in range(2):
                    ts_ = tile_of(i)
                    yield from attend(L, lambda h: L.qT[0:64, h, ts_], lambda h: L.kT[0:64, h // 2, :], 0.125, [L.t],
                                      bias_=lambda hh: bc(swm[:, i, :], 1, 2), sink_=PR(f"sink{l}"))
                    yield from weigh(L, lambda h: L.pt[:, h, :], 4,
                                     lambda kt, h: proj[:, kt, 1504 + (h // 2) * 64:1568 + (h // 2) * 64], [L.t])
                    heads_out(L, i, 512)
                    yield
                yield from group_norm(L, 512)

            def neighbourhood():
                L = Lane(3, (carve(6656, 4, 256, of=sw), carve(7680, 4, 256, of=sw)), carve(8704, 4, 256, of=sw),
                         carve(9728, 4, 2, 128, of=sw), None)
                yield from transp(L, L.qT, [lambda i, m=m: proj[:, i, 1632 + m * 64:1696 + m * 64] for m in range(4)], [])
                yield from transp(L, L.kT, [lambda i, m=m: proj[:, i, 1888 + m * 64:1952 + m * 64] for m in range(4)], [])
                yield
                for i in range(2):
                    ts_ = tile_of(i)
                    yield from attend(L, lambda h: L.qT[0:64, h, ts_], lambda h: L.kT[0:64, h, :], 0.125, [L.t],
                                      bias_=lambda hh: na_bias(i, hh))
                    yield from weigh(L, lambda h: L.pt[:, h, :], 4, lambda kt, h: proj[:, kt, 2144 + h * 64:2208 + h * 64], [L.t])
                    heads_out(L, i, 768)
                    yield
                yield from group_norm(L, 768)
                yield
                yield from maps(L, 1, carve(6656, 4, 256, of=sw))

            lanes(ORDER["mix2"], neighbourhood(), latent(), differential(), window())
            out_proj(mix, stage, PR(f"m2g{l}"), [])
            barrier()

        def mlp_plan(l):
            wd = a["w_down_2"][l].rearrange("(f p) d -> p f d", p=128)
            for c in range(9):
                if c < 8:
                    cols_plan(a["w_up_2"][l], c * 512, 512)
                if c:
                    for f2 in (2 * c - 2, 2 * c - 1):
                        W.add(wd[:, 2 * f2:2 * f2 + 2, :], 2, 1024)

        def mlp(l):
            barrier()
            th = norm_T(carve(U_N, 8, 256), PR(f"n2{l}"))
            uT = [[ur[:, 2048 * q + 1024 * z:2048 * q + 1024 * z + 1024] for z in range(2)] for q in range(3)]
            stg = [carve(U_N + 2048 + 1024 * q, 1024) for q in range(2)]
            up_free, u_free, u_done, st_free = [None] * 2, [None] * 3, [None] * 3, [None] * 2
            down = [None] * 4
            for c in range(9):
                if c < 8:
                    _, tm = colsT(512, th, bank=(4 + 2 * (c % 2), [up_free[c % 2]]))
                    v = stg[c % 2]
                    for m in range(2):
                        t = A(v[:, 512 * m:512 * m + 512], ps[:, 4 + 2 * (c % 2) + m, :], ACT.Relu, w=[tm, st_free[c % 2]])
                    up_free[c % 2] = t
                    t = V("tt", v, v, v, ALU.mult, w=[t])
                    t = acopy(uT[c % 3][0], v, w=[t, u_free[c % 3]])
                    t = V("tt", uT[c % 3][1], v, uT[c % 3][0], ALU.subtract, w=[t])
                    u_done[c % 3] = st_free[c % 2] = t
                if c:
                    d = c - 1
                    uv = [v.rearrange("p (f n) -> p f n", f=4) for v in uT[d % 3]]
                    for f2 in range(2):
                        tile, tok, n = W.next()
                        for i in range(2):
                            for cc in range(2):
                                for f in range(2):
                                    pr = parts3([v[:, 2 * f2 + f, i * 128:(i + 1) * 128] for v in uv],
                                                [v[:, f, cc * 512:(cc + 1) * 512] for v in tile])
                                    for q, (l_, r_) in enumerate(pr):
                                        first = d == 0 and f2 == 0 and f == 0 and q == 0
                                        last = d == 7 and f2 == 1 and f == 1 and q == 2
                                        tm = mm1(ps[:, 2 * i + cc, :], l_, r_, first, last, w=[tok, u_done[d % 3]],
                                                 inc=(f == 1 and q == 2))
                                down[2 * i + cc] = tm
                        if d == 7 and f2:
                            for i in range(2):
                                for cc in range(2):
                                    residual(cc, i, ps[:, 2 * i + cc, :], down[2 * i + cc])
                            W.hold = True
                        W.free(n, tm)
                    u_free[d % 3] = tm
            barrier()

        s_out = sem("s_out")

        def final(normed):
            barrier()
            t = DV.now()
            if normed:
                fin = carve(0, 1024)
                load(fin, a["final_norm_g_2"].partition_broadcast(128), t, PE.now())
                for i in range(2):
                    t = row_rstd(i)
                    t = V("stt", xn[:, i, :], x[:, i, :], st[:, 2 + i:3 + i], fin, ALU.mult, ALU.mult, w=[t, (s_ld, n_ld)])
            src = xn if normed else x
            tok = SP.dma(lambda e: e.dma_start(out.rearrange("b (i p) d -> p (b i) d", p=128), src[:, :, :]), s_out, 16, t)
            SP.items.append(([tok], None, None, 0))

        for what, l in plan:
            if what == "mix1":
                mix1_plan(l)
            elif what == "moe":
                moe_plan(l)
            elif what == "mix2":
                mix2_plan(l)
            elif what == "mlp":
                mlp_plan(l)
        for i in range(2):
            for c in range(2):
                square(i, c, None)
        for what, l in plan:
            if what == "mix1":
                mix1(l)
            elif what == "moe":
                moe(l)
            elif what == "mix2":
                mix2(l)
            elif what == "mlp":
                mlp(l)
        final(plan[-1][0] == "final")

        block = ctx.enter_context(nc.Block())

        @block.sync
        def _(eng):
            SP.replay(eng)

        @block.tensor
        def _(eng):
            PE.replay(eng)

        @block.vector
        def _(eng):
            DV.replay(eng)

        @block.scalar
        def _(eng):
            AC.replay(eng)

        @block.gpsimd
        def _(eng):
            PO.replay(eng)


def constants():
    c = {}
    p = np.arange(128)
    f = np.arange(128)
    c["ident"] = np.eye(128)
    c["tri"] = -(p[:, None] >= f[None, :]).astype(np.float32)
    c["neg1"] = -np.ones((128, 128))
    c["mneg"] = np.where(p[:, None] >= f[None, :], NEG, 0.0)
    c["keep"] = (p[:, None] < f[None, :])
    c["glam"] = (p[:, None] <= f[None, :]) & (p[:, None] // 64 == f[None, :] // 64)
    t = np.arange(256)
    c["swa"] = np.concatenate([np.where(np.abs(t[None, :] - (i * 128 + p[:, None])) <= 128, 0.0, NEG) for i in range(2)], 1)
    qc, kc = (p % 64)[:, None], np.arange(64)[None, :]
    lo = np.clip(qc - 8, 0, 48)
    c["nam"] = np.where((kc >= lo) & (kc < lo + 16), 0.0, NEG)
    for dim in (32, 64):
        inv = (1.0 / (np.float32(10000.0) ** (np.arange(0, dim, 2, dtype=np.float32) / np.float32(dim)))).astype(np.float32)
        ang = (t.astype(np.float32)[:, None] * inv[None, :]).astype(np.float32)
        for n, fn in (("cos", np.cos), ("sin", np.sin)):
            v = fn(ang).astype(np.float32)
            c[f"{n}{dim}"] = np.concatenate([v[0:128], v[128:256]], 1)
    c["reset"] = np.broadcast_to((t % 64 != 0), (128, 256))
    c["iota8"] = np.broadcast_to(np.arange(8), (128, 8))
    c["stri"] = (p[:, None] < f[None, :])
    c["slot"] = np.broadcast_to(np.arange(128) - 1e6, (128, 128))
    c["ones"] = np.ones((128, 128))
    return np.concatenate([np.asarray(c[n], np.float32) for n, _ in CONSTS], 1)


def params(a):
    z = {}

    def pk(v):
        return v.reshape(128, 8)

    def row(v, n=128):
        return np.broadcast_to(v.reshape(1, -1), (n, v.size))

    z["c"] = pk(a["c"][0])
    one = np.ones(512, np.float32)
    pad = np.zeros(64, np.float32)
    for l in range(2):
        z[f"nm{l}"], z[f"nf{l}"] = pk(a["norm_mix"][l]), pk(a["norm_ffn"][l])
        z[f"bgk{l}"] = a["b_gk"][l].reshape(2, 128).T
        z[f"qg{l}"] = np.tile(a["q_gain"][l], 2).reshape(128, 1)
        z[f"kg{l}"] = np.tile(a["k_gain"][l], 2).reshape(128, 1)
        z[f"mg{l}"] = pk(np.concatenate([one, np.tile(a["gla_gain"][l], 4)]))
        z[f"rb{l}"] = row(np.concatenate([a["b_router_grp"][l], a["b_router_exp"][l]]))
        z[f"rw{l}"] = np.concatenate([a["w_router_grp"][l], a["w_router_exp"][l]], 1).reshape(128, 288)
        z[f"bm{l}"] = a["b_ada"][l].reshape(6, 128, 8).transpose(1, 0, 2).reshape(128, 48)
        z[f"gk2{l}"] = np.concatenate([a["w_gk2"][l], np.zeros((112, 256), np.float32)], 0)
        z[f"n1{l}"], z[f"n2{l}"] = pk(a["norm1_g_2"][l]), pk(a["norm2_g_2"][l])
        z[f"mq{l}"] = np.concatenate([a["mla_q_norm_g_2"][l], pad]).reshape(2, 128).T
        z[f"mkv{l}"] = a["mla_kv_norm_g_2"][l].reshape(128, 1)
        z[f"m2g{l}"] = pk(np.concatenate([a["out_g_mla_2"][l], np.tile(a["diff_subln_g_2"][l], 4), a["out_g_swa_2"][l],
                                          a["out_g_na_2"][l]]))
        z[f"sink{l}"] = row(a["swa_sinks_2"][l])
        z[f"lam{l}"] = row(np.concatenate([a[f"diff_lambda_{n}_2"][l] for n in ("q1", "k1", "q2", "k2")]))
    return np.ascontiguousarray(np.concatenate([z[n] for n, _ in PARAMS], 1))


PLAN = [("mix1", 0), ("moe", 0), ("mix1", 1), ("moe", 1), ("mix2", 0), ("mlp", 0), ("mix2", 1), ("mlp", 1), ("final", 0)]
_INS = ["x", "b_ada", "w_ada", "w_in", "w_out", "w_gate", "w_up", "w_down", "w_in_2", "mla_w_uq_2", "mla_w_uk_2",
        "mla_w_uv_2", "na_rpb_2", "w_out_2", "w_up_2", "w_down_2", "final_norm_g_2"]


def kernel(**inputs):
    import numpy as _np
    import concourse.bacc as _bacc
    from concourse import mybir as _mybir
    from concourse.bass_utils import run_bass_kernel_spmd as _run

    nc = _bacc.Bacc("TRN2", target_bir_lowering=False, num_devices=1)
    host = {n: _np.ascontiguousarray(inputs[n]) for n in _INS}
    host["na_rpb_2"] = _np.ascontiguousarray(host["na_rpb_2"][:, ::-1, ::-1, ::-1])
    host["cst"] = constants()
    host["prm"] = params({n: _np.asarray(v) for n, v in inputs.items()})
    arrays, aps = {}, {}
    for name, v in host.items():
        arrays[f"in_{name}"] = v
        aps[name] = nc.dram_tensor(f"in_{name}", v.shape, _mybir.dt.from_np(v.dtype), kind="ExternalInput").ap()
    aps["na_rpb"] = aps["na_rpb_2"]
    out = nc.dram_tensor("out_0", (1, 256, 1024), F32, kind="ExternalOutput").ap()
    program(nc, aps, out, PLAN)
    r = _run(nc, [arrays], core_ids=[0])
    return r.results[0]["out_0"]
```
